# Optimizing a Trainium2 kernel written in Bass

```python
import jax, jax.numpy as jnp
from jax import lax
import numpy as np
import math

D_MODEL = 2048
BATCH = 1
SEQ = 512
DEPTH = 1

MIX_W = D_MODEL
ATT_W = MIX_W // 2
HEAD_DIM = 128
N_ATT_HEADS = ATT_W // HEAD_DIM
CONV_W = MIX_W // 4
CONV_TAPS = 3
POOL_W = MIX_W - ATT_W - CONV_W
POOL_WINDOWS = (2, 4, 8, 16)
POOL_GROUP = POOL_W // len(POOL_WINDOWS)
Q_BLOCK = 128
LN_EPS = 1e-5
DEEPNORM_ALPHA = (2 * DEPTH) ** 0.25
DEEPNORM_BETA = (8 * DEPTH) ** -0.25

IN_WIDTHS = (ATT_W, ATT_W, ATT_W, ATT_W, N_ATT_HEADS,
             CONV_W, CONV_W, CONV_W, CONV_W, POOL_W, POOL_W)
IN_W = sum(IN_WIDTHS)
IN_SPLITS = tuple(sum(IN_WIDTHS[:i + 1]) for i in range(len(IN_WIDTHS) - 1))


def layer_norm(x, g, b):
    x32 = x.astype(jnp.float32)
    mu = jnp.mean(x32, axis=-1, keepdims=True)
    var = jnp.mean(jnp.square(x32 - mu), axis=-1, keepdims=True)
    return ((x32 - mu) * lax.rsqrt(var + LN_EPS) * g + b).astype(x.dtype)

def forgetting_attention(q, k, v, fg_logit, b_f):
    b, s, h, dh = q.shape
    nb = s // Q_BLOCK
    log_f = jax.nn.log_sigmoid(fg_logit.astype(jnp.float32) + b_f.astype(jnp.float32))
    cum = jnp.cumsum(log_f, axis=1)
    cum_k = jnp.transpose(cum, (0, 2, 1))
    q_blocks = q.reshape(b, nb, Q_BLOCK, h, dh).transpose(1, 0, 2, 3, 4)
    c_blocks = cum.reshape(b, nb, Q_BLOCK, h).transpose(1, 0, 3, 2)
    k_pos = jnp.arange(s)
    scale = HEAD_DIM ** -0.5

    def block(args):
        qb, cb, i = args
        logits = jnp.einsum('bqhd,bkhd->bhqk', qb, k).astype(jnp.float32) * scale
        logits = logits + cb[..., None] - cum_k[:, :, None, :]
        q_pos = i * Q_BLOCK + jnp.arange(Q_BLOCK)
        causal = k_pos[None, :] <= q_pos[:, None]
        logits = jnp.where(causal, logits, -jnp.inf)
        p = jax.nn.softmax(logits, axis=-1).astype(v.dtype)
        return jnp.einsum('bhqk,bkhd->bqhd', p, v)

    out = lax.map(block, (q_blocks, c_blocks, jnp.arange(nb)))
    return out.transpose(1, 0, 2, 3, 4).reshape(b, s, h * dh)

def short_conv_mixer(gate_b, gate_c, h, conv_w):
    s = h.shape[1]
    u = gate_c * h
    up = jnp.pad(u, ((0, 0), (CONV_TAPS - 1, 0), (0, 0)))
    y = conv_w[0] * up[:, 0:s]
    for j in range(1, CONV_TAPS):
        y = y + conv_w[j] * up[:, j:j + s]
    return gate_b * y

def multiscale_pool_mixer(u, pool_w, pool_scale):
    s = u.shape[1]
    u32 = u.astype(jnp.float32)
    cs = jnp.pad(jnp.cumsum(u32, axis=1), ((0, 0), (1, 0), (0, 0)))
    t1 = jnp.arange(1, s + 1, dtype=jnp.float32)
    outs = []
    for g, w in enumerate(POOL_WINDOWS):
        sl = slice(g * POOL_GROUP, (g + 1) * POOL_GROUP)
        csg = cs[:, :, sl]
        lagged = jnp.pad(csg[:, :s - w + 1], ((0, 0), (w - 1, 0), (0, 0)))
        count = jnp.minimum(t1, float(w))
        mean = (csg[:, 1:] - lagged) / count[None, :, None]
        z = (mean - u32[:, :, sl]).astype(u.dtype)
        outs.append(jnp.einsum('bsc,cd->bsd', z, pool_w[g]))
    return jnp.concatenate(outs, axis=-1) * pool_scale

def first_inputs(seed: int = 0) -> dict:
    key = jax.random.key(seed)
    ks = jax.random.split(key, 10)
    x = jax.random.normal(ks[0], (BATCH, SEQ, D_MODEL), jnp.float32)
    w_in = jax.random.normal(ks[1], (DEPTH, D_MODEL, IN_W), jnp.float32) * D_MODEL ** -0.5
    b_f = jax.random.uniform(ks[2], (DEPTH, N_ATT_HEADS), jnp.float32, 1.0, 4.0)
    conv_w = jax.random.normal(ks[3], (DEPTH, CONV_TAPS, CONV_W), jnp.float32) * CONV_TAPS ** -0.5
    pool_w = jax.random.normal(ks[4], (DEPTH, len(POOL_WINDOWS), POOL_GROUP, POOL_GROUP),
                               jnp.float32) * POOL_GROUP ** -0.5
    pool_scale = 1.0 + 0.1 * jax.random.normal(ks[5], (DEPTH, POOL_W), jnp.float32)
    w_out = jax.random.normal(ks[6], (DEPTH, MIX_W, D_MODEL), jnp.float32) * (
        MIX_W ** -0.5 * DEEPNORM_BETA)
    ln_g = 1.0 + 0.1 * jax.random.normal(ks[7], (DEPTH, D_MODEL), jnp.float32)
    ln_b = 0.02 * jax.random.normal(ks[8], (DEPTH, D_MODEL), jnp.float32)
    return {"x": x, "w_in": w_in, "b_f": b_f, "conv_w": conv_w, "pool_w": pool_w,
            "pool_scale": pool_scale, "w_out": w_out, "ln_g": ln_g, "ln_b": ln_b}

def first_block(x, w_in, b_f, conv_w, pool_w, pool_scale, w_out, ln_g, ln_b):
    b, s, _ = x.shape
    for l in range(DEPTH):
        proj = jnp.einsum('bsd,de->bse', x, w_in[l])
        (q, k, v, g_att, fg, c_b, c_c, c_h, g_conv, p_u, g_pool) = jnp.split(
            proj, IN_SPLITS, axis=-1)
        heads = (b, s, N_ATT_HEADS, HEAD_DIM)
        y_att = forgetting_attention(q.reshape(heads), k.reshape(heads), v.reshape(heads),
                                     fg, b_f[l]) * jax.nn.silu(g_att)
        y_conv = short_conv_mixer(c_b, c_c, c_h, conv_w[l]) * jax.nn.silu(g_conv)
        y_pool = multiscale_pool_mixer(p_u, pool_w[l], pool_scale[l]) * jax.nn.silu(g_pool)
        y = jnp.concatenate([y_att, y_conv, y_pool], axis=-1)
        y = jnp.einsum('bse,ed->bsd', y, w_out[l])
        x = layer_norm(DEEPNORM_ALPHA * x + y, ln_g[l], ln_b[l])
    return x


CHUNK = 64
D_MIX = D_MODEL
ATTN_WIDTH = D_MIX // 2
SSD_WIDTH = D_MIX - ATTN_WIDTH
ATTN_HEAD_DIM = 128
ATTN_Q_HEADS = ATTN_WIDTH // ATTN_HEAD_DIM
ATTN_KV_HEADS = 2
ROPE_THETA = 500000.0
ROPE_PARTIAL_DIV = 4
IDX_HEADS = 16
IDX_HEAD_DIM = 64
IDX_TOPK_MAX = 256
SSD_HEAD_DIM = 64
SSD_HEADS = SSD_WIDTH // SSD_HEAD_DIM
SSD_GROUPS = 4
SSD_HEADS_PER_GROUP = SSD_HEADS // SSD_GROUPS
SSD_STATE = 128
SSD_CONV = 4
SSD_CHUNK = CHUNK
SSD_XBC_WIDTH = SSD_WIDTH + 2 * SSD_GROUPS * SSD_STATE
DEEPNORM_ALPHA_2 = (2.0 * DEPTH) ** 0.25
DEEPNORM_BETA_2 = (8.0 * DEPTH) ** -0.25
RMS_EPS = 1e-5
IN_WIDTHS_2 = (
    ATTN_Q_HEADS * ATTN_HEAD_DIM,
    ATTN_KV_HEADS * ATTN_HEAD_DIM,
    ATTN_KV_HEADS * ATTN_HEAD_DIM,
    ATTN_WIDTH,
    IDX_HEADS * IDX_HEAD_DIM,
    IDX_HEAD_DIM,
    IDX_HEADS,
    SSD_WIDTH,
    SSD_XBC_WIDTH,
    SSD_HEADS,
)
IN_TOTAL = sum(IN_WIDTHS_2)
VALUE_COL = 2


def _split_cols(u, widths):
    out, start = [], 0
    for w in widths:
        out.append(u[..., start:start + w])
        start += w
    return out

def _layer_norm(x, g, b):
    x32 = x.astype(jnp.float32)
    mu = jnp.mean(x32, axis=-1, keepdims=True)
    var = jnp.mean(jnp.square(x32 - mu), axis=-1, keepdims=True)
    y = (x32 - mu) * lax.rsqrt(var + LN_EPS) * g.astype(jnp.float32) + b.astype(jnp.float32)
    return y.astype(x.dtype)

def _rope_partial(t, pos):
    d = t.shape[-1]
    rot = d // ROPE_PARTIAL_DIV
    half = rot // 2
    inv = ROPE_THETA ** (-jnp.arange(half, dtype=jnp.float32) * 2.0 / rot)
    ang = pos[:, None] * inv[None, :]
    cos = jnp.cos(ang)[:, None, :]
    sin = jnp.sin(ang)[:, None, :]
    t32 = t.astype(jnp.float32)
    x1 = t32[..., :half]
    x2 = t32[..., half:rot]
    out = jnp.concatenate([x1 * cos - x2 * sin, x2 * cos + x1 * sin, t32[..., rot:]], axis=-1)
    return out.astype(t.dtype)

def _dsa_attention(q, k, v, q_idx, k_idx, w_idx):
    bsz, seq = q.shape[0], q.shape[1]
    topk = min(IDX_TOPK_MAX, seq // 4)
    rep = ATTN_Q_HEADS // ATTN_KV_HEADS
    scale = ATTN_HEAD_DIM ** -0.5
    key_chunk = jnp.arange(seq) // CHUNK
    k_idx32 = k_idx.astype(jnp.float32)
    gather = jax.vmap(lambda a, ix: a[ix])

    def block(i):
        start = i * Q_BLOCK
        sl = lambda a: lax.dynamic_slice_in_dim(a, start, Q_BLOCK, axis=1)
        qb, qib, wb = sl(q), sl(q_idx), sl(w_idx)
        q_chunk = (start + jnp.arange(Q_BLOCK)) // CHUNK
        logits = jax.nn.relu(jnp.einsum('bqhd,bsd->bqhs', qib.astype(jnp.float32), k_idx32))
        score = jnp.einsum('bqhs,bqh->bqs', logits, wb.astype(jnp.float32))
        admissible = key_chunk[None, :] <= q_chunk[:, None]
        score = jnp.where(admissible[None], score, -jnp.inf)
        _, sel = lax.top_k(score, topk)
        valid = key_chunk[sel] <= q_chunk[None, :, None]
        kg = gather(k, sel)
        vg = gather(v, sel)
        qg = qb.reshape(bsz, Q_BLOCK, ATTN_KV_HEADS, rep, ATTN_HEAD_DIM)
        s = jnp.einsum('bqgrd,bqkgd->bqgrk', qg, kg).astype(jnp.float32) * scale
        s = jnp.where(valid[:, :, None, None, :], s, -jnp.inf)
        p = jax.nn.softmax(s, axis=-1).astype(vg.dtype)
        o = jnp.einsum('bqgrk,bqkgd->bqgrd', p, vg)
        return o.reshape(bsz, Q_BLOCK, ATTN_Q_HEADS * ATTN_HEAD_DIM)

    out = lax.map(block, jnp.arange(seq // Q_BLOCK))
    return out.transpose(1, 0, 2, 3).reshape(bsz, seq, ATTN_Q_HEADS * ATTN_HEAD_DIM)

def _causal_depthwise_conv(u, w, b):
    c = u.shape[-1]
    y = lax.conv_general_dilated(u, w[:, None, :], window_strides=(1,), padding=[(SSD_CONV - 1, 0)],
                                 dimension_numbers=('NWC', 'WIO', 'NWC'), feature_group_count=c)
    return y + b

def _ssd_mixer(xbc, z, dt_raw, conv_w, conv_b, dt_bias, a_log, d_skip, norm_w):
    bsz, seq, _ = xbc.shape
    G, R, P, N, l = SSD_GROUPS, SSD_HEADS_PER_GROUP, SSD_HEAD_DIM, SSD_STATE, SSD_CHUNK
    nc = seq // l
    xbc = jax.nn.silu(_causal_depthwise_conv(xbc, conv_w, conv_b))
    xs, bm, cm = _split_cols(xbc, (SSD_WIDTH, G * N, G * N))
    xs = xs.astype(jnp.float32).reshape(bsz, nc, l, G, R, P)
    bm = bm.astype(jnp.float32).reshape(bsz, nc, l, G, N)
    cm = cm.astype(jnp.float32).reshape(bsz, nc, l, G, N)
    dt = jax.nn.softplus(dt_raw.astype(jnp.float32) + dt_bias.astype(jnp.float32))
    dt = dt.reshape(bsz, nc, l, G, R)
    a = -jnp.exp(a_log.astype(jnp.float32)).reshape(G, R)
    xdt = xs * dt[..., None]
    a_cum = jnp.cumsum(dt * a, axis=2)
    seg = a_cum[:, :, :, None] - a_cum[:, :, None, :]
    tril = jnp.tril(jnp.ones((l, l), dtype=bool))[:, :, None, None]
    lmat = jnp.exp(jnp.where(tril, seg, -jnp.inf))
    cb = jnp.einsum('bclgn,bcsgn->bclsg', cm, bm)
    y_diag = jnp.einsum('bclsg,bclsgr,bcsgrp->bclgrp', cb, lmat, xdt)
    decay = jnp.exp(a_cum[:, :, -1:] - a_cum)
    states = jnp.einsum('bcsgn,bcsgr,bcsgrp->bcgrpn', bm, decay, xdt)
    chunk_decay = jnp.exp(a_cum[:, :, -1])

    def step(h, inp):
        st, dec = inp
        return h * dec[..., None, None] + st, h

    h0 = jnp.zeros((bsz, G, R, P, N), jnp.float32)
    _, prev = lax.scan(step, h0, (jnp.moveaxis(states, 1, 0), jnp.moveaxis(chunk_decay, 1, 0)))
    prev = jnp.moveaxis(prev, 0, 1)
    y_off = jnp.einsum('bclgn,bcgrpn,bclgr->bclgrp', cm, prev, jnp.exp(a_cum))
    y = y_diag + y_off + d_skip.astype(jnp.float32).reshape(G, R)[:, :, None] * xs
    y = y.reshape(bsz, seq, SSD_WIDTH)
    g = (y * jax.nn.silu(z.astype(jnp.float32))).reshape(bsz, seq, G, SSD_WIDTH // G)
    g = g * lax.rsqrt(jnp.mean(jnp.square(g), axis=-1, keepdims=True) + RMS_EPS)
    return (g.reshape(bsz, seq, SSD_WIDTH) * norm_w.astype(jnp.float32)).astype(z.dtype)

def second_inputs(seed: int = 0) -> dict:
    key = jax.random.key(seed)
    ks = jax.random.split(key, 12)
    x = jax.random.normal(ks[0], (BATCH, SEQ, D_MODEL), jnp.float32)
    blk_keys = jax.random.split(ks[1], len(IN_WIDTHS_2))
    blocks = []
    for j, w in enumerate(IN_WIDTHS_2):
        scale = D_MODEL ** -0.5 * (DEEPNORM_BETA_2 if j == VALUE_COL else 1.0)
        blocks.append(jax.random.normal(blk_keys[j], (DEPTH, D_MODEL, w), jnp.float32) * scale)
    w_in = jnp.concatenate(blocks, axis=-1)
    w_out = jax.random.normal(ks[2], (DEPTH, D_MIX, D_MODEL), jnp.float32) * (D_MIX ** -0.5 * DEEPNORM_BETA_2)
    conv_w = jax.random.normal(ks[3], (DEPTH, SSD_CONV, SSD_XBC_WIDTH), jnp.float32) * SSD_CONV ** -0.5
    conv_b = 0.01 * jax.random.normal(ks[4], (DEPTH, SSD_XBC_WIDTH), jnp.float32)
    u = jax.random.uniform(ks[5], (DEPTH, SSD_HEADS), jnp.float32)
    dt0 = jnp.exp(u * (math.log(0.1) - math.log(0.001)) + math.log(0.001))
    dt_bias = dt0 + jnp.log(-jnp.expm1(-dt0))
    a_log = jnp.log(jax.random.uniform(ks[6], (DEPTH, SSD_HEADS), jnp.float32, 1.0, 16.0))
    d_skip = 1.0 + 0.1 * jax.random.normal(ks[7], (DEPTH, SSD_HEADS), jnp.float32)
    ssd_norm_w = 1.0 + 0.1 * jax.random.normal(ks[8], (DEPTH, SSD_WIDTH), jnp.float32)
    ln_g = 1.0 + 0.1 * jax.random.normal(ks[9], (DEPTH, D_MODEL), jnp.float32)
    ln_b = 0.01 * jax.random.normal(ks[10], (DEPTH, D_MODEL), jnp.float32)
    return {"x": x, "w_in": w_in, "w_out": w_out, "conv_w": conv_w, "conv_b": conv_b,
            "dt_bias": dt_bias, "a_log": a_log, "d_skip": d_skip, "ssd_norm_w": ssd_norm_w,
            "ln_g": ln_g, "ln_b": ln_b}

def second_block(x, w_in, w_out, conv_w, conv_b, dt_bias, a_log, d_skip, ssd_norm_w, ln_g, ln_b):
    bsz, seq, _ = x.shape
    pos = jnp.arange(seq, dtype=jnp.float32)
    h = x
    for layer in range(DEPTH):
        u = jnp.einsum('bsd,de->bse', h, w_in[layer])
        q, k, v, z_attn, q_idx, k_idx, w_idx, z_ssd, xbc, dt_raw = _split_cols(u, IN_WIDTHS_2)
        q = _rope_partial(q.reshape(bsz, seq, ATTN_Q_HEADS, ATTN_HEAD_DIM), pos)
        k = _rope_partial(k.reshape(bsz, seq, ATTN_KV_HEADS, ATTN_HEAD_DIM), pos)
        v = v.reshape(bsz, seq, ATTN_KV_HEADS, ATTN_HEAD_DIM)
        q_idx = _rope_partial(q_idx.reshape(bsz, seq, IDX_HEADS, IDX_HEAD_DIM), pos)
        k_idx = _rope_partial(k_idx[:, :, None, :], pos)[:, :, 0, :]
        w_idx = w_idx * (IDX_HEADS ** -0.5 * IDX_HEAD_DIM ** -0.5)
        o_attn = _dsa_attention(q, k, v, q_idx, k_idx, w_idx) * jax.nn.silu(z_attn)
        o_ssd = _ssd_mixer(xbc, z_ssd, dt_raw, conv_w[layer], conv_b[layer], dt_bias[layer],
                           a_log[layer], d_skip[layer], ssd_norm_w[layer])
        mixed = jnp.concatenate([o_attn, o_ssd.astype(o_attn.dtype)], axis=-1)
        sub = jnp.einsum('bse,ed->bsd', mixed, w_out[layer])
        h = _layer_norm(DEEPNORM_ALPHA_2 * h + sub, ln_g[layer], ln_b[layer])
    return h


def setup_inputs(seed=0):
    out = dict(first_inputs(seed))
    for name, value in second_inputs(seed + 1).items():
        if name != "x":
            out[name + "_2"] = value
    return out


def reference(
    x, w_in, b_f, conv_w, pool_w, pool_scale, w_out, ln_g, ln_b, w_in_2, w_out_2, conv_w_2,
    conv_b_2, dt_bias_2, a_log_2, d_skip_2, ssd_norm_w_2, ln_g_2, ln_b_2,
):
    x = first_block(
        x, w_in, b_f, conv_w, pool_w, pool_scale, w_out, ln_g, ln_b,
    )
    return second_block(
        x, w_in_2, w_out_2, conv_w_2, conv_b_2, dt_bias_2, a_log_2, d_skip_2, ssd_norm_w_2,
        ln_g_2, ln_b_2,
    )


_drawn_inputs = setup_inputs


def setup_inputs(seed=0):
    import zlib

    import numpy as np

    out = dict(_drawn_inputs(seed))
    spreads = {}
    factors = {'pool_scale': 4.027, 'conv_b_2': 8.0, 'd_skip_2': 2.692, 'ln_b_2': 5.569}
    for name, (base, spread) in spreads.items():
        noise = np.random.default_rng([zlib.crc32(name.encode()), seed]).standard_normal(out[name].shape)
        drawn = base * np.exp(spread * noise) if base else spread * noise
        out[name] = __import__('jax').numpy.asarray(drawn.astype(out[name].dtype))
    for name, factor in factors.items():
        out[name] = (out[name] * factor).astype(out[name].dtype)
    return out
```

```python
from contextlib import ExitStack, contextmanager

import concourse.bass as bass
from concourse import mybir
import numpy as np

P = 128
S = 512
D = 2048
QB = S // P
KT = D // P
UNIT = 1024
UK = UNIT // P
HEADS = 8
IDX_HEADS = 16
SSD_HEADS = 16
GROUPS = 4
TOPK = min(256, S // 4)
SCALE = float(P) ** -0.5
W_IDX_SCALE = 16 ** -0.5 * 64 ** -0.5
ALPHA = 2.0 ** 0.25
EPS = 1e-5
BIG = 1e30
INADMISSIBLE = -1e38
TAKEN = -3e38

T_HEAD1 = 1
T_CONV = T_HEAD1 + 4 * HEADS
T_POOL = T_CONV + 4 * 4
T_BACK1 = T_POOL + 2 * 4
T_MISC = T_BACK1 + 16
T_IDX = T_MISC + 1
T_KV = T_IDX + 8
T_SSD = T_KV + 4
T_HEAD2 = T_SSD + 6 * GROUPS
T_BACK2 = T_HEAD2 + 2 * HEADS
T_END = T_BACK2 + 16
ROUNDS = T_END // 2
BACK_TILES = 16

PC = {}
NPAR = 0
for _name, _n in (("b_f", 1), ("conv_w", 12), ("pool_scale", 4), ("conv_w2", 64), ("conv_b2", 16),
                  ("dt_bias", 1), ("a_log", 1), ("d_skip", 8), ("norm_w", 8), ("inv_count", 16)):
    PC[_name] = NPAR
    NPAR += _n


class Steps:

    def __init__(self, eng, sem):
        self.eng, self.sem, self.n, self.off = eng, sem, 0, 0

    def __call__(self, ins):
        ins.then_inc(self.sem, 1)
        self.n += 1
        self.eng.wait_ge(self.sem, self.off + self.n)

    @contextmanager
    def loop(self, start, end, per):
        n0 = self.n
        with self.eng.Fori(start, end) as i:
            self.off = (i - start) * per
            yield i
            assert self.n - n0 == per, (self.n - n0, per)
        self.off = 0
        self.n = n0 + per * (end - start)


def at(i, n=1):
    return bass.ds(i, n)


def tile_at(first, n, i=0, per=0):
    return (first + n) // 2 + i * (per // 2), (first + n) % 2


def block_kernel(nc, x_t, x_rows, stream, params, pool_w, ln1, ln2, rope_idx, rope_qk, out):
    fp32, fp32r = mybir.dt.float32, mybir.dt.float32r
    ACT, ALU, AX = mybir.ActivationFunctionType, mybir.AluOpType, mybir.AxisListType.X
    MULT, ADD, SUB, MIN, MAX = ALU.mult, ALU.add, ALU.subtract, ALU.min, ALU.max
    h_rows = nc.dram_tensor("h_rows", [S, D], fp32, kind="Internal").ap()

    with ExitStack() as ctx:
        def sb(name, shape, dt=fp32):
            return ctx.enter_context(nc.sbuf_tensor(name, shape, dt))

        def sem(name):
            return ctx.enter_context(nc.semaphore(name))

        planes_hi = sb("planes_hi", [P, KT, S], fp32r)
        planes_lo = sb("planes_lo", [P, KT, S], fp32r)
        feats = sb("feats", [P, KT, S])
        raw = sb("raw", [P, 4, UNIT])
        w_hi = sb("w_hi", [P, 4, UNIT], fp32r)
        w_lo = sb("w_lo", [P, 4, UNIT], fp32r)
        kT = sb("kT", [P, 2, S])
        vN = sb("vN", [P, 2, QB, P])
        qT = sb("qT", [P, S])
        vT = sb("vT", [P, S])
        gT = sb("gT", [P, S])
        gate = sb("gate", [P, S])
        tmp = sb("tmp", [P, S])
        padded = sb("padded", [P, 16 + S])
        bias = sb("bias", [P, QB, S])
        probs = sb("probs", [P, QB, S])
        probsT = sb("probsT", [P, QB, S])
        wide = sb("wide", [P, D])
        rope_q = sb("rope_q", [P, 2, S])
        ident = sb("ident", [P, P])
        upper = sb("upper", [P, P])
        last_row = sb("last_row", [P, P])
        ones = sb("ones", [P, P])
        par = sb("par", [P, NPAR])
        cumT = sb("cumT", [SSD_HEADS, S])
        cumN = sb("cumN", [P, QB, 16])
        dtN = sb("dtN", [P, QB, 16])
        wN = sb("wN", [P, QB, 16])
        ecumN = sb("ecumN", [P, QB, 16])
        widxN = sb("widxN", [P, QB, 16])
        chunk_decay = sb("chunk_decay", [P, QB, 16])
        nmax = sb("nmax", [P, QB])
        rowsum = sb("rowsum", [P, QB])
        rinv = sb("rinv", [P, QB])
        stats = sb("stats", [P, QB, 4, 6])
        mv = sb("mv", [P, QB, 2])
        rstd = sb("rstd", [P, QB, 2])
        top8 = sb("top8", [P, 8])
        ea = sb("ea", [SSD_HEADS, 1])

        causal = rope_q[:, 1, :]
        cum_row = rope_q[0:SSD_HEADS, 0, :]
        poolw = probsT[:, 0, :].rearrange("p (g d) -> p g d", g=4)
        gamma = probsT[:, :, :].rearrange("p a b -> p (a b)")
        beta = wide[:, :]
        xdt = wide[:, 0:1024].rearrange("p (c f) -> p c f", c=QB)
        states = wide[:, 1024:2048].rearrange("p (c f) -> p c f", c=QB)
        resid = [bias, probs]
        rope_i = probsT[:, 0:2, :]

        banks = [ctx.enter_context(nc.psum_tensor(f"bank{i}", [P, S], fp32)) for i in range(8)]
        ACC, B, O, M = banks[0:2], banks[2:6], banks[6], banks[7]
        SETS = [B, [ACC[0], ACC[1], O, M]]

        raw_loaded = [sem(f"raw_loaded{s}") for s in range(4)]
        hi_ready, lo_ready, unit_used = sem("hi_ready"), sem("lo_ready"), sem("unit_used")
        acc_taken = sem("acc_taken")
        x_loaded = [sem(f"x_loaded{c}") for c in range(4)]
        par_loaded, poolw_loaded = sem("par_loaded"), sem("poolw_loaded")
        rope_i_loaded, rope_q_loaded = sem("rope_i_loaded"), sem("rope_q_loaded")
        consts, waits_passed = sem("consts"), sem("waits_passed")
        plane_hi, planes_ready = sem("plane_hi"), sem("planes_ready")
        act_steps, dve_steps, pool_steps = sem("act_steps"), sem("dve_steps"), sem("pool_steps")
        fg_turn = sem("fg_turn")
        cum_ready, cum_turned = sem("cum_ready"), sem("cum_turned")
        cum_row_ready, cum_spread = sem("cum_row_ready"), sem("cum_spread")
        scores_done, logits_ready = sem("scores_done"), sem("logits_ready")
        probs_ready, probs_scaled = sem("probs_ready"), sem("probs_scaled")
        probs_turned, probsT_ready, pv_done = sem("probs_turned"), sem("probsT_ready"), sem("pv_done")
        gate_exp, feat_done = sem("gate_exp"), sem("feat_done")
        v_turned, v_ready = sem("v_turned"), sem("v_ready")
        pool_in, pool_done = sem("pool_in"), sem("pool_done")
        resid_loaded = [sem("resid_loaded0"), sem("resid_loaded1")]
        ln_loaded, rows_taken = sem("ln_loaded"), sem("rows_taken")
        var_ready, rstd_ready, rows_normed = sem("var_ready"), sem("rstd_ready"), sem("rows_normed")
        rows_turned, rows_stored = sem("rows_turned"), sem("rows_stored")
        kidx_ready, prep_turn, prep_turned = sem("kidx_ready"), sem("prep_turn"), sem("prep_turned")
        prep_ready, decay_spread = sem("prep_ready"), sem("decay_spread")
        idx_roped, idx_scored, idx_summed = sem("idx_roped"), sem("idx_scored"), sem("idx_summed")
        k_roped, q_roped = sem("k_roped"), sem("q_roped")
        conv_done, silu_exp, silu_done = sem("conv_done"), sem("silu_exp"), sem("silu_done")
        ssd_mm, ssd_vec, ssd_exp = sem("ssd_mm"), sem("ssd_vec"), sem("ssd_exp")
        MM_STEPS, VEC_STEPS, EXP_STEPS = 14, 17, 10

        block = ctx.enter_context(nc.Block())

        @block.sync
        def _(sp):
            def load(m, s):
                sp.dma_start(raw[:, s, :], stream[at(4 * m + s), :, :].rearrange("u p n -> p (u n)"))\
                    .then_inc(raw_loaded[s], 16)

            for s in range(4):
                load(0, s)
                sp.dma_start(feats[:, 4 * s:4 * s + 4, :], x_t[:, 4 * s:4 * s + 4, :]).then_inc(x_loaded[s], 16)
            with sp.Fori(1, ROUNDS) as m:
                for s in range(4):
                    sp.wait_ge(lo_ready, 4 * m - 3 + s)
                    load(m, s)
            sp.wait_ge(rows_stored, 2 * 16 * QB)

        @block.gpsimd
        def _(pool):
            step = Steps(pool, pool_steps)

            def select(ap, op, fill, base, pattern, mult):
                step(nc.gpsimd.affine_select(out=ap, in_=ap, compare_op=op, fill=fill, base=base,
                                             pattern=pattern, channel_multiplier=mult))

            step(nc.gpsimd.memset(ident[:, :], 0.0))
            select(ident[:, :], ALU.not_equal, 1.0, 0, [[-1, P]], 1)
            step(nc.gpsimd.memset(causal, 0.0))
            select(causal[:, S - P:S], ALU.is_ge, BIG, 0, [[-1, P]], 1)
            step(nc.gpsimd.memset(upper[:, :], 0.0))
            select(upper[:, :], ALU.is_ge, -BIG, 0, [[1, P]], -1)
            step(nc.gpsimd.memset(last_row[:, :], 0.0))
            select(last_row[:, :], ALU.not_equal, 1.0, -(P - 1), [[0, P]], 1)
            step(nc.gpsimd.memset(padded[:, 0:16], 0.0))
            nc.gpsimd.memset(ones[:, :], 1.0).then_inc(consts, 1)
            with pool.Fori(0, ROUNDS) as m:
                for s in range(4):
                    pool.wait_ge(hi_ready, 4 * m + s + 1)
                    nc.gpsimd.tensor_sub(w_lo[:, s, :], raw[:, s, :], w_hi[:, s, :].bitcast(fp32))\
                        .then_inc(lo_ready, 1)

        @block.tensor
        def _(pe):
            def mm(o, a, b, start=True, stop=True):
                return nc.tensor.matmul(o, a, b, start=start, stop=stop)

            def turn(o, a):
                k = a.shape[0]
                return nc.tensor.transpose(o, a, ident[0:k, 0:k])

            def project(tile, acc_before):
                m, p = tile
                if acc_before is not None:
                    pe.wait_ge(acc_taken, acc_before)
                for u in range(2):
                    s = 2 * p + u
                    pe.wait_ge(lo_ready, 4 * m + s + 1)
                    for k in range(UK):
                        e = u * UK + k
                        if acc_before is None and p == 0:
                            pe.wait_ge(planes_ready, e + 1)
                        hi, lo = w_hi[:, s, P * k:P * k + P], w_lo[:, s, P * k:P * k + P]
                        mm(ACC[p][:, :], hi, planes_hi[:, e, :], e == 0, False)
                        mm(ACC[p][:, :], hi, planes_lo[:, e, :], False, False)
                        last = mm(ACC[p][:, :], lo, planes_hi[:, e, :], False, e == KT - 1)
                    last.then_inc(unit_used, 1)

            def head_scores(g):
                for i in range(QB):
                    n = P * (i + 1)
                    mm(B[i][:, 0:n], qT[:, P * i:n], kT[:, g, 0:n]).then_inc(scores_done, 1)

            def head_turn(a):
                for i in range(QB):
                    pe.wait_ge(probs_scaled, 4 * a + i + 1)
                    for j in range(i + 1):
                        last = turn(B[j][:, P * i:P * i + P], probs[:, i, P * j:P * j + P])
                last.then_inc(probs_turned, 1)

            def head_pv(a, g):
                pe.wait_ge(probsT_ready, a + 1)
                for j in range(QB):
                    last = mm(O[:, P * j:S], vN[:, g, j, :], probsT[:, j, P * j:S], j == 0, j == QB - 1)
                last.then_inc(pv_done, 1)

            def turn_v(g):
                for j in range(QB):
                    last = turn(M[:, P * j:P * j + P], (vT if g == 0 else qT)[:, P * j:P * j + P])
                last.then_inc(v_turned, 1)

            def attn_start1(a):
                pe.wait_ge(cum_row_ready, a + 1)
                pe.wait_ge(v_ready, a + 1)
                mm(M[:, :], ones[0:HEADS, :], cum_row[0:HEADS, :]).then_inc(cum_spread, 1)
                pe.wait_ge(acc_taken, T_HEAD1 + 4 * a + 2)
                head_scores(0)

            pe.wait_ge(consts, 1)
            project((0, 0), None)
            for j in range(4):
                project(tile_at(T_HEAD1, j), None if j == 0 else j)
            pe.wait_ge(cum_ready, 1)
            for i in range(QB):
                last = turn(M[:, 8 * i:8 * i + 8], cumT[0:HEADS, P * i:P * i + P])
            last.then_inc(cum_turned, 1)
            pe.wait_ge(acc_taken, T_HEAD1 + 3)
            pe.wait_ge(cum_row_ready, 1)
            turn_v(0)

            with pe.Fori(1, HEADS) as h:
                a = h - 1
                first = T_HEAD1 + 4 * h
                attn_start1(a)
                project(tile_at(T_HEAD1, 0, h, 4), first - 1)
                head_turn(a)
                project(tile_at(T_HEAD1, 1, h, 4), first)
                head_pv(a, 0)
                project(tile_at(T_HEAD1, 2, h, 4), first + 1)
                project(tile_at(T_HEAD1, 3, h, 4), first + 2)
                pe.wait_ge(acc_taken, first + 3)
                turn_v(0)
            a = HEADS - 1
            attn_start1(a)
            project(tile_at(T_CONV, 0), T_CONV - 1)
            head_turn(a)
            project(tile_at(T_CONV, 1), T_CONV)
            head_pv(a, 0)
            project(tile_at(T_CONV, 2), T_CONV + 1)
            project(tile_at(T_CONV, 3), T_CONV + 2)
            with pe.Fori(1, 4) as j:
                for t in range(4):
                    project(tile_at(T_CONV, t, j, 4), T_CONV + 4 * j + t - 1)
            pe.wait_ge(poolw_loaded, 16)
            for g in range(4):
                project(tile_at(T_POOL, 2 * g), T_POOL + 2 * g - 1)
                if g:
                    pe.wait_ge(pool_in, g)
                    mm(O[:, :], poolw[:, g - 1, :], tmp[:, :]).then_inc(pool_done, 1)
                project(tile_at(T_POOL, 2 * g + 1), T_POOL + 2 * g)
            pe.wait_ge(pool_in, 4)
            mm(O[:, :], poolw[:, 3, :], tmp[:, :]).then_inc(pool_done, 1)

            def project_back(blk, first):
                for db in range(4):
                    dst = SETS[db % 2]
                    if db >= 2:
                        pe.wait_ge(rows_taken, 16 * blk + 4 * (db - 1))
                    for q in range(4):
                        m, p = tile_at(first, 4 * db + q)
                        for u in range(2):
                            s = 2 * p + u
                            pe.wait_ge(lo_ready, 4 * m + s + 1)
                            for k in range(2):
                                e = 4 * q + 2 * u + k
                                if db == 0:
                                    pe.wait_ge(planes_ready, (16 if blk == 0 else 48) + e + 1)
                                hi, lo = w_hi[:, s, S * k:S * k + S], w_lo[:, s, S * k:S * k + S]
                                for r in range(QB):
                                    rows = slice(P * r, P * r + P)
                                    mm(dst[r][:, :], planes_hi[:, e, rows], hi, e == 0, False)
                                    mm(dst[r][:, :], planes_hi[:, e, rows], lo, False, False)
                                    last = mm(dst[r][:, :], planes_lo[:, e, rows], hi, False, e == KT - 1)
                            last.then_inc(unit_used, 1)

            project_back(0, T_BACK1)
            for r in range(QB):
                pe.wait_ge(rows_normed, r + 1)
                if r == 0:
                    pe.wait_ge(rows_taken, 16)
                if r >= 2:
                    pe.wait_ge(planes_ready, 32 + 4 * (r - 1))
                for b in range(4):
                    for k in range(4):
                        last = turn(SETS[r % 2][b][:, P * k:P * k + P], feats[:, 4 * r + b, P * k:P * k + P])
                    last.then_inc(rows_turned, 1)

            SK = BACK_TILES
            pe.wait_ge(planes_ready, 48)
            project(tile_at(T_MISC, 0), T_MISC - SK - 1)
            project(tile_at(T_IDX, 0), T_IDX - SK - 1)
            pe.wait_ge(prep_turn, 5)
            srcs = [cumT[:, :]] + [probs[0:SSD_HEADS, k, :] for k in range(4)]
            for k, src in enumerate(srcs):
                for i in range(QB):
                    c = 64 * k + 16 * i
                    last = turn(M[:, c:c + 16], src[:, P * i:P * i + P])
            last.then_inc(prep_turned, 1)
            pe.wait_ge(prep_ready, 1)
            mm(O[:, 0:64], last_row[:, :], ecumN[:, :, :].rearrange("p c h -> p (c h)")).then_inc(decay_spread, 1)

            def idx_scores(t, roped, summed):
                pe.wait_ge(idx_roped, roped)
                pe.wait_ge(idx_summed, summed)
                for half, dst in ((0, [B[1], B[2], B[3]]), (1, [B[0], O, M])):
                    lanes = slice(64 * half, 64 * half + 64)
                    for i in range(1, QB):
                        n = P * (i + 1)
                        last = mm(dst[i - 1][:, 0:n], qT[lanes, P * i:n], vT[lanes, 0:n])
                last.then_inc(idx_scored, 1)

            project(tile_at(T_IDX, 1), T_IDX + 1 - SK - 1)
            pe.wait_ge(kidx_ready, 1)
            idx_scores(0, 1, 1)
            with pe.Fori(1, 4) as tt:
                for half in range(2):
                    t = 2 * tt + half
                    project(tile_at(T_IDX, half, tt, 2), T_IDX + t - SK - 1)
                    idx_scores(t - 1, t, t)
            project(tile_at(T_KV, 0), T_KV - SK - 1)
            idx_scores(7, 8, 8)
            for t in range(1, 4):
                project(tile_at(T_KV, t), T_KV + t - SK - 1)
            pe.wait_ge(acc_taken, T_KV + 4 - SK)
            pe.wait_ge(idx_summed, 9)
            turn_v(0)
            pe.wait_ge(v_ready, HEADS + 1)
            turn_v(1)

            with pe.Fori(0, GROUPS) as g:
                def tile(k):
                    project(tile_at(T_SSD, k, g, 6), T_SSD + 6 * g + k - SK - 1)

                mv0, vv0 = MM_STEPS * g, VEC_STEPS * g
                BT, CT = probs[:, 0, :], probs[:, 1, :]
                for k in range(4):
                    tile(k)
                tile(4)
                pe.wait_ge(silu_done, 6 * g + 5)
                pe.wait_ge(v_ready, HEADS + 2)
                for c in range(QB):
                    chunk = slice(P * c, P * c + P)
                    last = mm(B[0][:, chunk], BT[:, chunk], CT[:, chunk])
                last.then_inc(ssd_mm, 1)
                for src, dst in ((0, B[3]), (2, O), (3, M)):
                    for c in range(QB):
                        chunk = slice(P * c, P * c + P)
                        last = turn(dst[:, chunk], probs[:, src, chunk])
                    last.then_inc(ssd_mm, 1)
                tile(5)
                pe.wait_ge(ssd_vec, vv0 + 3)
                for c in range(QB - 1):
                    dst = (B[3] if c < 2 else O)[:, 256 * (c % 2):256 * (c % 2) + 256]
                    last = mm(dst, vT[:, P * c:P * c + P], states[:, c, :])
                last.then_inc(ssd_mm, 1)

                def spread(r):
                    pe.wait_ge(ssd_vec, vv0 + (4, 6, 10, 13)[r])
                    mm([M, O][r % 2][:, :], ones[0:SSD_HEADS, :], gT[0:SSD_HEADS, :]).then_inc(ssd_mm, 1)

                def head_out(r):
                    pe.wait_ge(ssd_vec, vv0 + (10, 13, 15, 16)[r])
                    lanes = slice(64 * (r % 2), 64 * (r % 2) + 64)
                    dst = B[1 + r // 2]
                    L, E = [tmp[:, :], probsT[:, 2, :]][r % 2], [probsT[:, 3, :], qT[:, :]][r % 2]
                    for c in range(QB):
                        chunk = slice(P * c, P * c + P)
                        last = mm(dst[lanes, chunk], xdt[:, c, 64 * r:64 * r + 64], L[:, chunk], True, c == 0)
                        if c:
                            last = mm(dst[lanes, chunk], states[:, c, 64 * r:64 * r + 64], E[:, chunk],
                                      False, True)
                    last.then_inc(ssd_mm, 1)

                spread(0)
                spread(1)
                head_out(0)
                spread(2)
                head_out(1)
                spread(3)
                head_out(2)
                head_out(3)
                pe.wait_ge(ssd_vec, vv0 + 17)
                mm(M[:, :], ones[:, :], tmp[:, :], True, False)
                mm(M[:, :], ones[:, :], probsT[:, 2, :], False, True).then_inc(ssd_mm, 1)

            def attn_start2(g, h_ready):
                pe.wait_ge(q_roped, h_ready)
                head_scores(g)

            project(tile_at(T_HEAD2, 0), T_HEAD2 - SK - 1)
            project(tile_at(T_HEAD2, 1), T_HEAD2 - SK)
            pe.wait_ge(feat_done, 16 + 2 * GROUPS)
            pe.wait_ge(k_roped, 1)
            for g, lo_h, hi_h in ((0, 1, 5), (1, 5, 8)):
                with pe.Fori(lo_h, hi_h) as h:
                    a = HEADS + h - 1
                    attn_start2(g, h)
                    project(tile_at(T_HEAD2, 0, h, 2), T_HEAD2 + 2 * h - SK - 1)
                    head_turn(a)
                    project(tile_at(T_HEAD2, 1, h, 2), T_HEAD2 + 2 * h - SK)
                    head_pv(a, g)
            attn_start2(1, 8)
            head_turn(2 * HEADS - 1)
            head_pv(2 * HEADS - 1, 1)
            project_back(1, T_BACK2)

        @block.scalar
        def _(act):
            step = Steps(act, act_steps)

            def signal(ins, s, value):
                ins.then_inc(s, 1)
                act.wait_ge(s, value)

            def round_unit(m, s, reused=True):
                if reused:
                    act.wait_ge(unit_used, 4 * m + s - 3)
                act.wait_ge(raw_loaded[s], 16 * (m + 1))
                signal(nc.scalar.activation(w_hi[:, s, :], raw[:, s, :], ACT.Copy), hi_ready, 4 * m + s + 1)

            def turn_round(tile, end=False):
                m, p = tile
                if not end:
                    for u in range(2):
                        round_unit(m + 1, 2 * p + u)

            def take(tile, dst, count, src=slice(0, P)):
                m, p = tile
                act.wait_ge(unit_used, 4 * m + 2 * p + 2)
                signal(nc.scalar.activation(dst, ACC[p][src, :], ACT.Copy), acc_taken, count)

            def exp_gate(count):
                signal(nc.scalar.activation(gate[:, :], gT[:, :], ACT.Exp, scale=-1.0), gate_exp, count)

            def head_exps(a):
                for i in range(QB):
                    n = P * (i + 1)
                    act.wait_ge(logits_ready, 4 * a + i + 1)
                    signal(nc.scalar.activation(probs[:, i, 0:n], probs[:, i, 0:n], ACT.Exp, bias=nmax[:, i:i + 1],
                                                scale=-1.0, accum_out=rowsum[:, i:i + 1]),
                           probs_ready, 4 * a + i + 1)

            def cut_hi(k, value):
                signal(nc.scalar.activation(planes_hi[:, k, :], feats[:, k, :], ACT.Copy), plane_hi, value)

            act.dma_start(par[:, :], params).then_inc(par_loaded, 16)
            for s in range(4):
                round_unit(0, s, reused=False)
                act.wait_ge(x_loaded[s], 16)
                for k in range(4 * s, 4 * s + 4):
                    cut_hi(k, k + 1)
            act.wait_ge(par_loaded, 16)
            turn_round((0, 0))
            act.wait_ge(unit_used, 2)
            xs = tmp[0:HEADS, :]
            ls = gate[0:HEADS, :]
            signal(nc.scalar.activation(xs, ACC[0][0:HEADS, :], ACT.Identity,
                                        bias=par[0:HEADS, PC["b_f"]:PC["b_f"] + 1]), acc_taken, 1)
            act.wait_ge(fg_turn, 1)
            step(nc.scalar.activation(ls, ls, ACT.Exp))
            signal(nc.scalar.activation(ls, ls, ACT.Ln, bias=1.0), fg_turn, 2)
            for j, dst in enumerate((qT[:, :], kT[:, 0, :], vT[:, :], gT[:, :])):
                t = tile_at(T_HEAD1, j)
                turn_round(t)
                take(t, dst, T_HEAD1 + j + 1)
            act.wait_ge(cum_ready, 1)
            exp_gate(1)
            with step.loop(1, HEADS, 0) as h:
                head_exps(h - 1)
                for j, dst in enumerate((qT[:, :], kT[:, 0, :], vT[:, :], gT[:, :])):
                    t = tile_at(T_HEAD1, j, h, 4)
                    turn_round(t)
                    if j == 3:
                        act.wait_ge(feat_done, h)
                    take(t, dst, T_HEAD1 + 4 * h + j + 1)
                exp_gate(h + 1)
            head_exps(HEADS - 1)

            def conv_tiles(j):
                for k, dst in enumerate((qT[:, :], kT[:, 0, :], vT[:, :], gT[:, :])):
                    t = tile_at(T_CONV, k, j, 4)
                    turn_round(t)
                    if k == 0:
                        act.wait_ge(feat_done, HEADS + j)
                    take(t, dst, T_CONV + 4 * j + k + 1)
                exp_gate(HEADS + j + 1)

            for k, dst in enumerate((qT[:, :], kT[:, 0, :], vT[:, :], gT[:, :])):
                t = tile_at(T_CONV, k)
                turn_round(t)
                if k == 3:
                    act.wait_ge(feat_done, HEADS)
                take(t, dst, T_CONV + k + 1)
            exp_gate(HEADS + 1)
            act.wait_ge(feat_done, HEADS)
            act.dma_start(poolw, pool_w).then_inc(poolw_loaded, 16)
            with step.loop(1, 4, 0) as j:
                conv_tiles(j)
            for g in range(4):
                act_tiles = (padded[:, 16:16 + S], gT[:, :])
                for k in range(2):
                    t = tile_at(T_POOL, 2 * g + k)
                    turn_round(t)
                    if k == 0:
                        act.wait_ge(feat_done, HEADS + 4 + g)
                    take(t, act_tiles[k], T_POOL + 2 * g + k + 1)
                exp_gate(HEADS + 4 + g + 1)

            def back_and_norm(blk, first, rows_in, ln, dst):
                f0 = 16 * (blk + 1)
                act.wait_ge(feat_done, f0)
                act.dma_start(gamma, ln[0:1, :].to_broadcast([P, D])).then_inc(ln_loaded, 16)
                act.dma_start(beta, ln[1:2, :].to_broadcast([P, D])).then_inc(ln_loaded, 16)

                def load_resid(db):
                    act.dma_start(resid[db % 2][:, :, :],
                                  rows_in[:, S * db:S * db + S].rearrange("(m p) d -> p m d", p=P))\
                        .then_inc(resid_loaded[db % 2], 16)

                act.wait_ge(unit_used, 2 * first)
                for k in range(KT):
                    cut_hi(k, 16 + 32 * blk + k + 1)
                if blk:
                    act.wait_ge(rows_stored, 16 * QB)
                load_resid(0)
                load_resid(1)
                for db in range(4):
                    if db in (1, 2):
                        act.wait_ge(rows_taken, 16 * blk + 4 * db)
                        load_resid(db + 1)
                    for q in range(4):
                        t = tile_at(first, 4 * db + q)
                        turn_round(t, end=t[0] + 1 >= ROUNDS)
                for r in range(QB):
                    act.wait_ge(var_ready, 4 * blk + r + 1)
                    step(nc.scalar.activation(rstd[:, r, 0:1], mv[:, r, 1:2], ACT.Ln, bias=par_eps))
                    signal(nc.scalar.activation(rstd[:, r, 0:1], rstd[:, r, 0:1], ACT.Exp, scale=-0.5),
                           rstd_ready, 4 * blk + r + 1)
                for r in range(QB):
                    act.wait_ge(rows_normed, 4 * blk + r + 1)
                    act.dma_start(dst[P * r:P * r + P, :], feats[:, 4 * r:4 * r + 4, :].rearrange("p a b -> p (a b)"))\
                        .then_inc(rows_stored, 16)
                    if blk == 0:
                        for b in range(4):
                            act.wait_ge(rows_turned, 4 * r + b + 1)
                            signal(nc.scalar.activation(
                                planes_hi[:, 4 * b:4 * b + 4, P * r:P * r + P],
                                SETS[r % 2][b][:, :].rearrange("p (k n) -> p k n", k=4), ACT.Copy),
                                plane_hi, 32 + 4 * r + b + 1)

            par_eps = EPS
            back_and_norm(0, T_BACK1, x_rows, ln1, h_rows)

            SK = BACK_TILES
            act.wait_ge(planes_ready, 48)
            act.dma_start(rope_q[:, :, :], rope_qk).then_inc(rope_q_loaded, 16)
            act.dma_start(rope_i, rope_idx).then_inc(rope_i_loaded, 16)
            turn_round(tile_at(T_MISC, 0))
            take(tile_at(T_MISC, 0), gT[:, :], T_MISC - SK + 1)
            R = [probs[0:SSD_HEADS, k, :] for k in range(4)]
            act.wait_ge(prep_turn, 1)
            step(nc.scalar.activation(ea[:, :], par[0:SSD_HEADS, PC["a_log"]:PC["a_log"] + 1], ACT.Exp))
            step(nc.scalar.activation(R[1], R[1], ACT.Exp))
            signal(nc.scalar.activation(R[1], R[1], ACT.Ln, bias=1.0), prep_turn, 2)
            act.wait_ge(prep_turn, 3)
            step(nc.scalar.activation(R[1], R[1], ACT.Exp))
            signal(nc.scalar.activation(R[2], cumT[:, :], ACT.Exp), prep_turn, 4)
            t = tile_at(T_IDX, 0)
            turn_round(t)
            act.wait_ge(kidx_ready, 1)
            take(t, gT[:, :], T_IDX - SK + 1)
            t = tile_at(T_IDX, 1)
            turn_round(t)
            act.wait_ge(idx_roped, 1)
            take(t, gT[:, :], T_IDX - SK + 2)
            with step.loop(1, 4, 0) as tt:
                for half in range(2):
                    t = tile_at(T_IDX, half, tt, 2)
                    turn_round(t)
                    act.wait_ge(idx_roped, 2 * tt + half)
                    take(t, gT[:, :], T_IDX - SK + 2 * tt + half + 1)
            for k, dst in enumerate((kT[:, 0, :], kT[:, 1, :], vT[:, :], qT[:, :])):
                t = tile_at(T_KV, k)
                turn_round(t)
                if k == 2:
                    act.wait_ge(idx_scored, 8)
                take(t, dst, T_KV - SK + k + 1)

            with step.loop(0, GROUPS, 0) as g:
                for k in range(6):
                    t = tile_at(T_SSD, k, g, 6)
                    turn_round(t)
                    n = 6 * g + k
                    if k < 4:
                        act.wait_ge(conv_done, 4 * g + k + 1)
                        dst = padded[:, 16:16 + S]
                    else:
                        act.wait_ge(feat_done, 16 + 2 * g)
                        dst = probsT[:, k - 4, :]
                    take(t, dst, T_SSD - SK + n + 1)
                    if k < 4:
                        act.wait_ge(conv_done, 4 * g + k + 2)
                    act.wait_ge(silu_done, n + 1)
                    signal(nc.scalar.activation(gate[:, :], probs[:, k, :] if k < 4 else probsT[:, k - 4, :],
                                                ACT.Exp, scale=-1.0), silu_exp, n + 1)
                vv0, ev0 = VEC_STEPS * g, EXP_STEPS * g
                for r in range(4):
                    act.wait_ge(ssd_vec, vv0 + (7, 9, 12, 14)[r])
                    L, E = [tmp[:, :], probsT[:, 2, :]][r % 2], [probsT[:, 3, :], qT[:, :]][r % 2]
                    signal(nc.scalar.activation(L, L, ACT.Exp), ssd_exp, ev0 + 2 * r + 1)
                    signal(nc.scalar.activation(E, [M, O][r % 2][:, :], ACT.Exp), ssd_exp, ev0 + 2 * r + 2)
                act.wait_ge(ssd_mm, MM_STEPS * g + 14)
                signal(nc.scalar.activation(gT[:, :], M[:, :], ACT.Ln, bias=par_eps, scale=1.0 / 256), ssd_exp, ev0 + 9)
                signal(nc.scalar.activation(gT[:, :], gT[:, :], ACT.Exp, scale=-0.5), ssd_exp, ev0 + 10)

            t = tile_at(T_HEAD2, 0)
            turn_round(t)
            act.wait_ge(feat_done, 16 + 2 * GROUPS)
            take(t, tmp[:, :], T_HEAD2 - SK + 1)
            t = tile_at(T_HEAD2, 1)
            turn_round(t)
            take(t, gT[:, :], T_HEAD2 - SK + 2)
            exp_gate(17)
            with step.loop(1, HEADS, 0) as h:
                head_exps(HEADS + h - 1)
                t = tile_at(T_HEAD2, 0, h, 2)
                turn_round(t)
                act.wait_ge(q_roped, h)
                take(t, tmp[:, :], T_HEAD2 - SK + 2 * h + 1)
                t = tile_at(T_HEAD2, 1, h, 2)
                turn_round(t)
                act.wait_ge(feat_done, 16 + 2 * GROUPS + h)
                take(t, gT[:, :], T_HEAD2 - SK + 2 * h + 2)
                exp_gate(17 + h)
            head_exps(2 * HEADS - 1)
            back_and_norm(1, T_BACK2, h_rows, ln2, out)

        @block.vector
        def _(dve):
            V = nc.vector
            step = Steps(dve, dve_steps)

            def signal(ins, s, value):
                ins.then_inc(s, 1)
                dve.wait_ge(s, value)

            def stt(o, a, scalar, b, op0, op1):
                return V.scalar_tensor_tensor(out=o, in0=a, scalar=scalar, in1=b, op0=op0, op1=op1)

            def waited():
                dve.sem_inc(waits_passed, 1)

            def col(name, i=0):
                return par[:, at(PC[name] + i)]

            def sigmoid(g):
                step(V.tensor_scalar(g, g, 1.0, None, ADD))
                step(V.reciprocal(g, g))

            def cut_lo(k, value):
                dve.wait_ge(plane_hi, value)
                signal(V.tensor_sub(planes_lo[:, k, :], feats[:, k, :], planes_hi[:, k, :].bitcast(fp32)),
                       planes_ready, value)

            def pick_cum_row(a):
                signal(V.tensor_scalar(cum_row[0:HEADS, :], cumT[0:HEADS, :], ident[0:HEADS, at(a)], None, MULT),
                       cum_row_ready, a + 1)

            def logit_bias(a):
                dve.wait_ge(cum_spread, a + 1)
                for i in range(QB):
                    n = P * (i + 1)
                    step(stt(bias[:, i, 0:n], M[:, 0:n], cumN[:, i, at(a)], causal[:, S - n:S], SUB, ADD))

            def head_softmax(a):
                for i in range(QB):
                    n = P * (i + 1)
                    dve.wait_ge(scores_done, 4 * a + i + 1)
                    step(stt(probs[:, i, 0:n], B[i][:, 0:n], -SCALE, bias[:, i, 0:n], MULT, ADD))
                    signal(V.tensor_reduce(nmax[:, i:i + 1], probs[:, i, 0:n], AX, MIN), logits_ready, 4 * a + i + 1)

            def head_gate(count):
                dve.wait_ge(gate_exp, count)
                sigmoid(gate[:, :])
                step(V.tensor_mul(gate[:, :], gate[:, :], gT[:, :]))

            def head_scale(a):
                for i in range(QB):
                    n = P * (i + 1)
                    dve.wait_ge(probs_ready, 4 * a + i + 1)
                    step(V.reciprocal(rinv[:, i:i + 1], rowsum[:, i:i + 1]))
                    signal(V.tensor_scalar(probs[:, i, 0:n], probs[:, i, 0:n], rinv[:, i:i + 1], None, MULT),
                           probs_scaled, 4 * a + i + 1)

            def head_take_turned(a):
                dve.wait_ge(probs_turned, a + 1)
                for j in range(QB):
                    ins = V.tensor_copy(probsT[:, j, P * j:S], B[j][:, P * j:S])
                    if j < QB - 1:
                        step(ins)
                    else:
                        signal(ins, probsT_ready, a + 1)

            def head_finish(a, tile, count):
                dve.wait_ge(pv_done, a + 1)
                signal(V.tensor_mul(feats[:, at(tile), :].rearrange("p a n -> p (a n)"), O[:, :], gate[:, :]),
                       feat_done, count)

            def take_v(g, count):
                dve.wait_ge(v_turned, count)
                signal(V.tensor_copy(vN[:, g, :, :].rearrange("p j n -> p (j n)"), M[:, :]), v_ready, count)

            for k in range(KT):
                cut_lo(k, k + 1)
            xs, ls = tmp[0:HEADS, :], gate[0:HEADS, :]
            dve.wait_ge(acc_taken, 1)
            signal(stt(ls, xs, -1.0, xs, MULT, MIN), fg_turn, 1)
            dve.wait_ge(consts, 1)
            step(V.memset(probs[0:HEADS, 0, :], 1.0))
            dve.wait_ge(fg_turn, 2)
            step(stt(xs, xs, 0.0, ls, MIN, SUB))
            signal(V.tensor_tensor_scan(cumT[0:HEADS, :], probs[0:HEADS, 0, :], xs, 0.0, MULT, ADD), cum_ready, 1)
            dve.wait_ge(cum_turned, 1)
            step(V.tensor_copy(cumN[:, :, 0:HEADS], M[:, 0:32].rearrange("p (i h) -> p i h", i=QB)))
            pick_cum_row(0)
            take_v(0, 1)
            with step.loop(1, HEADS, 18) as h:
                a = h - 1
                logit_bias(a)
                head_softmax(a)
                head_gate(a + 1)
                head_scale(a)
                head_take_turned(a)
                head_finish(a, a, a + 1)
                pick_cum_row(h)
                take_v(0, h + 1)
            a = HEADS - 1
            logit_bias(a)
            head_softmax(a)
            head_gate(a + 1)
            head_scale(a)
            head_take_turned(a)
            head_finish(a, a, a + 1)

            def conv_mixer(j):
                dve.wait_ge(acc_taken, T_CONV + 4 * j + 4)
                step(V.tensor_mul(padded[:, 16:16 + S], kT[:, 0, :], vT[:, :]))
                step(V.tensor_scalar(tmp[:, :], padded[:, 14:14 + S], col("conv_w", 3 * j), None, MULT))
                for c in (1, 2):
                    step(stt(tmp[:, :], padded[:, 14 + c:14 + c + S], col("conv_w", 3 * j + c), tmp[:, :], MULT, ADD))
                step(V.tensor_mul(tmp[:, :], tmp[:, :], qT[:, :]))
                head_gate(HEADS + j + 1)
                signal(V.tensor_mul(feats[:, at(HEADS + j), :].rearrange("p a n -> p (a n)"), tmp[:, :], gate[:, :]),
                       feat_done, HEADS + j + 1)

            with step.loop(0, 4, 8) as j:
                conv_mixer(j)

            flat = probs[:, :, :].rearrange("p a b -> p (a b)")
            bufs = [flat[:, 0:16 + S], flat[:, 16 + S:2 * (16 + S)]]
            for b in bufs:
                step(V.memset(b[:, 0:16], 0.0))
            for g in range(4):
                w = 2 << g
                dve.wait_ge(acc_taken, T_POOL + 2 * g + 2)
                src = padded
                for lev in range(g + 1):
                    dst = bufs[lev % 2]
                    sh = 1 << lev
                    step(V.tensor_add(dst[:, 16:16 + S], src[:, 16:16 + S], src[:, 16 - sh:16 - sh + S]))
                    src = dst
                step(stt(tmp[:, :], src[:, 16:16 + S], 1.0 / w, padded[:, 16:16 + S], MULT, SUB))
                step(V.tensor_mul(tmp[:, 0:w - 1], src[:, 16:16 + w - 1], par[:, PC["inv_count"]:PC["inv_count"] + w - 1]))
                signal(V.tensor_sub(tmp[:, 0:w - 1], tmp[:, 0:w - 1], padded[:, 16:16 + w - 1]), pool_in, g + 1)
                head_gate(HEADS + 4 + g + 1)
                dve.wait_ge(pool_done, g + 1)
                signal(stt(feats[:, 12 + g, :], O[:, :], col("pool_scale", g), gate[:, :], MULT, MULT),
                       feat_done, 12 + g + 1)

            def back_and_norm(blk, first):
                for k in range(KT):
                    cut_lo(k, 16 + 32 * blk + k + 1)
                for db in range(4):
                    dve.wait_ge(resid_loaded[db % 2], 16 * (2 * blk + db // 2 + 1))
                    dve.wait_ge(unit_used, 2 * (first + 4 * db + 4))
                    for r in range(QB):
                        signal(stt(feats[:, 4 * r + db, :], resid[db % 2][:, r, :], ALPHA, SETS[db % 2][r][:, :],
                                   MULT, ADD), rows_taken, 16 * blk + 4 * db + r + 1)
                    for r in range(QB):
                        step(V.bn_stats(stats[:, r, db, :], feats[:, 4 * r + db, :]))
                for r in range(QB):
                    signal(V.bn_aggr(mv[:, r, :], stats[:, r, :, :]), var_ready, 4 * blk + r + 1)
                dve.wait_ge(ln_loaded, 32 * (blk + 1))

                def norm(r):
                    row = feats[:, 4 * r:4 * r + 4, :].rearrange("p a b -> p (a b)")
                    dve.wait_ge(rstd_ready, 4 * blk + r + 1)
                    step(V.tensor_scalar(rstd[:, r, 1:2], mv[:, r, 0:1], rstd[:, r, 0:1], -1.0, MULT, MULT))
                    step(V.tensor_scalar(row, row, rstd[:, r, 0:1], rstd[:, r, 1:2], MULT, ADD))
                    step(V.tensor_mul(row, row, gamma))
                    signal(V.tensor_add(row, row, beta), rows_normed, 4 * blk + r + 1)

                def cut_turned(r):
                    for b in range(4):
                        n = 32 + 4 * r + b + 1
                        dve.wait_ge(plane_hi, n)
                        signal(V.tensor_sub(planes_lo[:, 4 * b:4 * b + 4, P * r:P * r + P],
                                            SETS[r % 2][b][:, :].rearrange("p (k n) -> p k n", k=4),
                                            planes_hi[:, 4 * b:4 * b + 4, P * r:P * r + P].bitcast(fp32)),
                               planes_ready, n)

                norm(0)
                for r in range(1, QB):
                    norm(r)
                    if blk == 0:
                        cut_turned(r - 1)
                if blk == 0:
                    cut_turned(QB - 1)

            back_and_norm(0, T_BACK1)

            SK = BACK_TILES

            def rope(dst, src, lanes, table, mask, ins_signal, value, scratch):
                waited()
                step(V.stream_shuffle(scratch[0:lanes, :], src[0:lanes, :], mask))
                step(V.tensor_mul(scratch[0:lanes, :], scratch[0:lanes, :], table[0:lanes, 1, :]))
                step(V.tensor_mul(dst[0:lanes, :], src[0:lanes, :], table[0:lanes, 0, :]))
                ins = V.tensor_add(dst[0:lanes, :], dst[0:lanes, :], scratch[0:lanes, :])
                if ins_signal is None:
                    step(ins)
                else:
                    signal(ins, ins_signal, value)

            swap8 = [i + 8 if i < 8 else i - 8 if i < 16 else i for i in range(32)]
            swap16 = [(i + 16) % 32 for i in range(32)]
            R = [probs[0:SSD_HEADS, k, :] for k in range(4)]
            dve.wait_ge(rows_stored, 16 * QB)
            dve.wait_ge(acc_taken, T_MISC - SK + 1)
            step(V.tensor_copy(R[0], gT[64:80, :]))
            step(V.tensor_scalar(R[0], R[0], par[0:SSD_HEADS, PC["dt_bias"]:PC["dt_bias"] + 1], None, ADD))
            signal(stt(R[1], R[0], -1.0, R[0], MULT, MIN), prep_turn, 1)
            step(V.tensor_copy(R[3], gT[96:112, :]))
            step(V.tensor_scalar(R[3], R[3], W_IDX_SCALE, None, MULT))
            dve.wait_ge(rope_i_loaded, 16)
            rope(vT, gT, 64, rope_i, swap8, None, 0, tmp)
            signal(V.tensor_copy(vT[64:128, :], vT[0:64, :]), kidx_ready, 1)
            step(V.memset(R[2], 1.0))
            dve.wait_ge(prep_turn, 2)
            step(stt(R[0], R[0], 0.0, R[1], MAX, ADD))
            step(V.tensor_scalar(R[1], R[0], ea[:, 0:1], -1.0, MULT, MULT))
            for c in range(QB):
                chunk = slice(P * c, P * c + P)
                step(V.tensor_tensor_scan(cumT[:, chunk], R[2][:, chunk], R[1][:, chunk], 0.0, MULT, ADD))
            for c in range(QB):
                chunk, end = slice(P * c, P * c + P), P * c + P - 1
                ins = V.tensor_scalar(R[1][:, chunk], cumT[:, chunk], -1.0, cumT[:, end:end + 1], MULT, ADD)
                if c < QB - 1:
                    step(ins)
                else:
                    signal(ins, prep_turn, 3)
            dve.wait_ge(prep_turn, 4)
            signal(V.tensor_mul(R[1], R[1], R[0]), prep_turn, 5)
            dve.wait_ge(acc_taken, T_IDX - SK + 1)
            rope(qT, gT, P, rope_i, swap8, idx_roped, 1, tmp)
            dve.wait_ge(prep_turned, 1)
            for k, dst in enumerate((cumN, dtN, wN, ecumN, widxN)):
                ins = V.tensor_copy(dst[:, :, :], M[:, 64 * k:64 * k + 64].rearrange("p (c h) -> p c h", c=QB))
                if k < 4:
                    step(ins)
                else:
                    signal(ins, prep_ready, 1)
            dve.wait_ge(decay_spread, 1)
            step(V.tensor_copy(chunk_decay[:, :, :], O[:, 0:64].rearrange("p (c h) -> p c h", c=QB)))
            signal(V.memset(bias[:, :, :], 0.0), idx_summed, 1)

            def sum_scores(t, scored, summed):
                dve.wait_ge(idx_scored, scored)
                for half, src in ((0, [B[1], B[2], B[3]]), (1, [B[0], O, M])):
                    for i in range(1, QB):
                        n = P * (i + 1)
                        step(V.tensor_scalar(tmp[:, 0:n], src[i - 1][:, 0:n], 0.0, widxN[:, i, at(2 * t + half)], MAX, MULT))
                        ins = V.tensor_add(bias[:, i, 0:n], bias[:, i, 0:n], tmp[:, 0:n])
                        if half and i == QB - 1:
                            signal(ins, idx_summed, summed)
                        else:
                            step(ins)

            with step.loop(1, 8, 3 + 11) as t:
                sum_scores(t - 1, t, t + 1)
                dve.wait_ge(acc_taken, T_IDX - SK + t + 1)
                rope(qT, gT, P, rope_i, swap8, idx_roped, t + 1, tmp)
            sum_scores(7, 8, 9)

            for i in range(1, QB):
                step(V.memset(bias[0:64, i, P * i + 64:P * i + P], INADMISSIBLE))
            with step.loop(0, TOPK // 8, 6) as _r:
                for i in range(1, QB):
                    n = P * (i + 1)
                    waited()
                    step(V.max(top8[:, :], bias[:, i, 0:n]))
                    waited()
                    step(V.match_replace(bias[:, i, 0:n], top8[:, :], bias[:, i, 0:n], TAKEN))
            for i in range(1, QB):
                n = P * (i + 1)
                step(V.tensor_scalar(bias[:, i, 0:n], bias[:, i, 0:n], TAKEN, BIG, ALU.not_equal, MULT))
            step(V.memset(bias[0:64, 0, 64:P], BIG))
            dve.wait_ge(rope_q_loaded, 16)
            dve.wait_ge(acc_taken, T_KV - SK + 2)
            rope(kT[:, 0, :], kT[:, 0, :], P, rope_q, swap16, None, 0, tmp)
            rope(kT[:, 1, :], kT[:, 1, :], P, rope_q, swap16, k_roped, 1, tmp)
            take_v(0, HEADS + 1)
            take_v(1, HEADS + 2)
            signal(V.memset(nmax[:, :], 0.0), silu_done, 1)
            signal(V.memset(rowsum[:, :], 0.0), conv_done, 1)

            def silu_tile(g, k):
                n = 6 * g + k
                dve.wait_ge(acc_taken, T_SSD - SK + n + 1)
                if k < 4:
                    dst = probs[:, k, :]
                    ch = 4 * g + k
                    step(V.tensor_scalar(dst, padded[:, 16:16 + S], col("conv_w2", 4 * ch + 3), col("conv_b2", ch), MULT, ADD))
                    for c in (2, 1, 0):
                        ins = stt(dst, padded[:, 13 + c:13 + c + S], col("conv_w2", 4 * ch + c), dst, MULT, ADD)
                        if c:
                            step(ins)
                        else:
                            signal(ins, conv_done, 4 * g + k + 2)
                else:
                    dst = probsT[:, k - 4, :]
                dve.wait_ge(silu_exp, n + 1)
                sigmoid(gate[:, :])
                signal(V.tensor_mul(dst, dst, gate[:, :]), silu_done, n + 2)

            with step.loop(0, GROUPS, 55) as g:
                mm0, vv0, ev0 = MM_STEPS * g, VEC_STEPS * g, EXP_STEPS * g
                for k in range(5):
                    silu_tile(g, k)
                dve.wait_ge(ssd_mm, mm0 + 2)
                signal(V.tensor_copy(vT[:, :], B[3][:, :]), ssd_vec, vv0 + 1)
                for t, src in ((0, O), (1, M)):
                    dve.wait_ge(ssd_mm, mm0 + 3 + t)
                    for col_of, dst in ((dtN, xdt), (wN, states)):
                        for h in range(2):
                            d = dst[:, :, P * t + 64 * h:P * t + 64 * h + 64]
                            x = src[:, :].rearrange("p (c f) -> p c f", c=QB)[:, :, 64 * h:64 * h + 64]
                            ins = V.tensor_mul(d, x, col_of[:, :, at(4 * g + 2 * t + h)].to_broadcast([P, QB, 64]))
                            if col_of is wN and h:
                                signal(ins, ssd_vec, vv0 + 2 + t)
                            else:
                                step(ins)

                def pick_row(r, value):
                    signal(V.tensor_scalar(gT[0:SSD_HEADS, :], cumT[:, :], ident[0:SSD_HEADS, at(4 * g + r)], None, MULT),
                           ssd_vec, vv0 + value)

                def segments(r, value):
                    L = [tmp[:, :], probsT[:, 2, :]][r % 2]
                    for c in range(QB):
                        chunk = slice(P * c, P * c + P)
                        ins = stt(L[:, chunk], [M, O][r % 2][:, chunk], cumN[:, c, at(4 * g + r)], upper[:, :], SUB, ADD)
                        if c < QB - 1:
                            step(ins)
                        else:
                            signal(ins, ssd_vec, vv0 + value)

                def operands(r, value):
                    dve.wait_ge(ssd_exp, ev0 + 2 * r + 2)
                    L, E = [tmp[:, :], probsT[:, 2, :]][r % 2], [probsT[:, 3, :], qT[:, :]][r % 2]
                    step(V.tensor_mul(L, L, B[0][:, :]))
                    signal(V.tensor_mul(E, E, probs[:, 1, :]), ssd_vec, vv0 + value)

                pick_row(0, 4)
                dve.wait_ge(ssd_mm, mm0 + 5)
                step(V.tensor_copy(states[:, 1, :], B[3][:, 0:256]))
                for c in (1, 2):
                    new, old = states[:, c + 1, :], states[:, c, :]
                    dec = chunk_decay[:, c, at(4 * g, 4)].unsqueeze(2).to_broadcast([P, 4, 64])
                    step(V.tensor_mul(new.rearrange("p (h f) -> p h f", h=4), old.rearrange("p (h f) -> p h f", h=4), dec))
                    ins = V.tensor_add(new, new, (B[3][:, 256:512] if c == 1 else O[:, 0:256]))
                    if c == 1:
                        step(ins)
                    else:
                        signal(ins, ssd_vec, vv0 + 5)
                dve.wait_ge(ssd_mm, mm0 + 6)
                pick_row(1, 6)
                segments(0, 7)
                dve.wait_ge(ssd_mm, mm0 + 7)
                pick_row(2, 8)
                segments(1, 9)
                silu_tile(g, 5)
                operands(0, 10)
                dve.wait_ge(ssd_mm, mm0 + 9)
                pick_row(3, 11)
                segments(2, 12)
                operands(1, 13)
                dve.wait_ge(ssd_mm, mm0 + 11)
                segments(3, 14)
                operands(2, 15)
                operands(3, 16)
                dve.wait_ge(ssd_mm, mm0 + 13)
                for t, sq in ((0, tmp[:, :]), (1, probsT[:, 2, :])):
                    step(stt(sq, probs[:, 2 + t, :], col("d_skip", 2 * g + t), B[1 + t][:, :], MULT, ADD))
                    step(V.tensor_mul(probsT[:, t, :], probsT[:, t, :], sq))
                    ins = V.tensor_mul(sq, probsT[:, t, :], probsT[:, t, :])
                    if t:
                        signal(ins, ssd_vec, vv0 + 17)
                    else:
                        step(ins)
                dve.wait_ge(ssd_exp, ev0 + 10)
                for t in range(2):
                    signal(stt(feats[:, at(HEADS + 2 * g + t), :].rearrange("p a n -> p (a n)"), probsT[:, t, :],
                               col("norm_w", 2 * g + t), gT[:, :], MULT, MULT), feat_done, 17 + 2 * g + t)

            def rope_head(h):
                dve.wait_ge(acc_taken, T_HEAD2 - SK + 2 * h + 1)
                rope(qT, tmp, P, rope_q, swap16, q_roped, h + 1, padded[:, 16:16 + S])

            rope_head(0)
            with step.loop(1, HEADS, 17) as h:
                a = HEADS + h - 1
                head_softmax(a)
                head_gate(16 + h)
                head_scale(a)
                head_take_turned(a)
                rope_head(h)
                head_finish(a, h - 1, 24 + h)
            a = 2 * HEADS - 1
            head_softmax(a)
            head_gate(24)
            head_scale(a)
            head_take_turned(a)
            head_finish(a, HEADS - 1, 32)
            back_and_norm(1, T_BACK2)


def drawn_up(rows, cols):
    rot = cols // 4
    half = rot // 2
    f32 = np.float32
    inv = np.power(f32(500000.0), -np.arange(half, dtype=f32) * f32(2.0) / f32(rot), dtype=f32)
    ang = np.arange(S, dtype=f32)[:, None] * inv[None, :]
    cos, sin = np.cos(ang).T, np.sin(ang).T
    table = np.zeros((rows, cols, 2, S), f32)
    table[:, :, 0] = 1.0
    table[:, 0:half, 0] = cos
    table[:, half:rot, 0] = cos
    table[:, 0:half, 1] = -sin
    table[:, half:rot, 1] = sin
    return table.reshape(P, 2, S)


def tile_units(w, cols):
    t = np.zeros((D, P), np.float32)
    used = np.asarray(cols) >= 0
    t[:, :len(cols)][:, used] = w[:, np.asarray(cols)[used]]
    return t.reshape(2, UK, P, P).transpose(0, 2, 1, 3).reshape(2, P, UNIT)


def back_units(w):
    return w.reshape(KT // 2, 2, P, 4, S).transpose(3, 0, 2, 1, 4).reshape(32, P, UNIT)


def kernel(**inputs):
    import concourse.bacc as _bacc
    from concourse import mybir as _mybir
    from concourse.bass_utils import run_bass_kernel_spmd as _run

    a = {k: np.ascontiguousarray(v) for k, v in inputs.items()}
    w1, w2 = a["w_in"][0], a["w_in_2"][0]
    span = lambda start, n=P: list(range(start, start + n))
    tiles = [tile_units(w1, span(4096, 8))]
    for h in range(HEADS):
        tiles += [tile_units(w1, span(1024 * k + P * h)) for k in range(4)]
    for j in range(4):
        tiles += [tile_units(w1, span(4104 + 512 * k + P * j)) for k in range(4)]
    for g in range(4):
        tiles += [tile_units(w1, span(6152 + 512 * k + P * g)) for k in range(2)]
    tiles.append(back_units(a["w_out"][0]))
    q, k, v, z, qi, ki, wi, zs, xs, bm, cm, dt = 0, 1024, 1280, 1536, 2560, 3584, 3648, 3664, 4688, 5712, 6224, 6736
    tiles.append(tile_units(w2, span(ki, 64) + span(dt, 16) + [-1] * 16 + span(wi, 16)))
    tiles += [tile_units(w2, span(qi + P * t)) for t in range(8)]
    tiles += [tile_units(w2, span(c)) for c in (k, k + P, v, v + P)]
    xbc_tiles = []
    for g in range(GROUPS):
        conv_cols = [bm + P * g, cm + P * g, xs + 256 * g, xs + 256 * g + P]
        xbc_tiles += [c - xs for c in conv_cols]
        tiles += [tile_units(w2, span(c)) for c in conv_cols + [zs + 256 * g, zs + 256 * g + P]]
    for h in range(HEADS):
        tiles += [tile_units(w2, span(q + P * h)), tile_units(w2, span(z + P * h))]
    tiles.append(back_units(a["w_out_2"][0]))

    par = np.zeros((P, NPAR), np.float32)

    def put(name, x):
        par[:x.shape[0], PC[name]:PC[name] + x.shape[1]] = x

    put("b_f", a["b_f"][0][:, None])
    put("conv_w", a["conv_w"][0].reshape(3, 4, P).transpose(2, 1, 0).reshape(P, 12))
    put("pool_scale", a["pool_scale"][0].reshape(4, P).T)
    put("conv_w2", np.stack([a["conv_w_2"][0][:, c:c + P] for c in xbc_tiles]).transpose(2, 0, 1).reshape(P, 64))
    put("conv_b2", np.stack([a["conv_b_2"][0][c:c + P] for c in xbc_tiles]).T)
    put("dt_bias", a["dt_bias_2"][0][:, None])
    put("a_log", a["a_log_2"][0][:, None])
    put("d_skip", np.repeat(a["d_skip_2"][0], 64).reshape(8, P).T)
    put("norm_w", a["ssd_norm_w_2"][0].reshape(8, P).T)
    put("inv_count", np.broadcast_to(np.float32(1) / np.arange(1, 17, dtype=np.float32), (P, 16)))

    x = a["x"][0]
    arrays = {
        "x_t": np.ascontiguousarray(x.T.reshape(KT, P, S).transpose(1, 0, 2)),
        "x_rows": x,
        "stream": np.concatenate(tiles),
        "params": par,
        "pool_w": np.ascontiguousarray(a["pool_w"][0].transpose(1, 0, 2)),
        "ln1": np.concatenate([a["ln_g"], a["ln_b"]]),
        "ln2": np.concatenate([a["ln_g_2"], a["ln_b_2"]]),
        "rope_idx": drawn_up(2, 64),
        "rope_qk": drawn_up(1, P),
    }
    nc = _bacc.Bacc("TRN2", target_bir_lowering=False, num_devices=1)
    args = [nc.dram_tensor(f"in_{n}", v.shape, _mybir.dt.from_np(v.dtype), kind="ExternalInput").ap()
            for n, v in arrays.items()]
    out = nc.dram_tensor("out", (S, D), _mybir.dt.float32, kind="ExternalOutput").ap()
    block_kernel(nc, *args, out)
    r = _run(nc, [{f"in_{n}": v for n, v in arrays.items()}], core_ids=[0])
    return r.results[0]["out"].reshape(1, S, D)
```

```python
from contextlib import ExitStack, contextmanager

import concourse.bass as bass
from concourse import mybir
import numpy as np

P = 128
S = 512
D = 2048
QB = S // P
KT = D // P
UNIT = 1024
UK = UNIT // P
HEADS = 8
IDX_HEADS = 16
SSD_HEADS = 16
GROUPS = 4
TOPK = min(256, S // 4)
SCALE = float(P) ** -0.5
W_IDX_SCALE = 16 ** -0.5 * 64 ** -0.5
ALPHA = 2.0 ** 0.25
EPS = 1e-5
BIG = 1e30
INADMISSIBLE = -1e38
TAKEN = -3e38

T_HEAD1 = 1
T_CONV = T_HEAD1 + 4 * HEADS
T_POOL = T_CONV + 4 * 4
T_BACK1 = T_POOL + 2 * 4
T_MISC = T_BACK1 + 16
T_SSD = T_MISC + 1
T_IDX = T_SSD + 6 * GROUPS
T_KV = T_IDX + 8
T_HEAD2 = T_KV + 4
T_BACK2 = T_HEAD2 + 2 * HEADS
T_END = T_BACK2 + 16
ROUNDS = T_END // 2
BACK_TILES = 16

PC = {}
NPAR = 0
for _name, _n in (("b_f", 1), ("conv_w", 12), ("pool_scale", 4), ("conv_w2", 64), ("conv_b2", 16),
                  ("dt_bias", 1), ("a_log", 1), ("d_skip", 8), ("norm_w", 8), ("inv_count", 16)):
    PC[_name] = NPAR
    NPAR += _n


class Steps:

    def __init__(self, eng, sem):
        self.eng, self.sem, self.n, self.off = eng, sem, 0, 0

    def __call__(self, ins):
        ins.then_inc(self.sem, 1)
        self.n += 1
        self.eng.wait_ge(self.sem, self.off + self.n)

    @contextmanager
    def loop(self, start, end, per):
        n0 = self.n
        with self.eng.Fori(start, end) as i:
            self.off = (i - start) * per
            yield i
            assert self.n - n0 == per, (self.n - n0, per)
        self.off = 0
        self.n = n0 + per * (end - start)


def at(i, n=1):
    return bass.ds(i, n)


def tile_at(first, n, i=0, per=0):
    return (first + n) // 2 + i * (per // 2), (first + n) % 2


def block_kernel(nc, x_t, x_rows, stream, params, pool_w, ln1, ln2, rope_idx, rope_qk, out):
    fp32, fp32r = mybir.dt.float32, mybir.dt.float32r
    ACT, ALU, AX = mybir.ActivationFunctionType, mybir.AluOpType, mybir.AxisListType.X
    MULT, ADD, SUB, MIN, MAX = ALU.mult, ALU.add, ALU.subtract, ALU.min, ALU.max
    h_rows = nc.dram_tensor("h_rows", [S, D], fp32, kind="Internal").ap()

    with ExitStack() as ctx:
        def sb(name, shape, dt=fp32):
            return ctx.enter_context(nc.sbuf_tensor(name, shape, dt))

        def sem(name):
            return ctx.enter_context(nc.semaphore(name))

        planes_hi = sb("planes_hi", [P, KT, S], fp32r)
        planes_lo = sb("planes_lo", [P, KT, S], fp32r)
        feats = sb("feats", [P, KT, S])
        raw = sb("raw", [P, 4, UNIT])
        w_hi = sb("w_hi", [P, 4, UNIT], fp32r)
        w_lo = sb("w_lo", [P, 4, UNIT], fp32r)
        kT = sb("kT", [P, 2, S])
        vN = sb("vN", [P, 2, QB, P])
        qT = sb("qT", [P, S])
        vT = sb("vT", [P, S])
        gT = sb("gT", [P, S])
        gate = sb("gate", [P, S])
        tmp = sb("tmp", [P, S])
        padded = sb("padded", [P, 16 + S])
        bias = sb("bias", [P, QB, S])
        probs = sb("probs", [P, QB, S])
        probsT = sb("probsT", [P, QB, S])
        wide = sb("wide", [P, D])
        rope_q = sb("rope_q", [P, 2, S])
        ident = sb("ident", [P, P])
        upper = sb("upper", [P, P])
        last_row = sb("last_row", [P, P])
        ones = sb("ones", [P, P])
        par = sb("par", [P, NPAR])
        cumT = sb("cumT", [SSD_HEADS, S])
        cumN = sb("cumN", [P, QB, 16])
        dtN = sb("dtN", [P, QB, 16])
        wN = sb("wN", [P, QB, 16])
        ecumN = sb("ecumN", [P, QB, 16])
        widxN = sb("widxN", [P, QB, 16])
        chunk_decay = sb("chunk_decay", [P, QB, 16])
        nmax = sb("nmax", [P, QB])
        rowsum = sb("rowsum", [P, QB])
        rinv = sb("rinv", [P, QB])
        stats = sb("stats", [P, QB, 4, 6])
        mv = sb("mv", [P, QB, 2])
        rstd = sb("rstd", [P, QB, 2])
        top8 = sb("top8", [P, 8])
        ea = sb("ea", [SSD_HEADS, 1])

        causal = rope_q[:, 1, :]
        cum_row = rope_q[0:SSD_HEADS, 0, :]
        poolw = probsT[:, 0, :].rearrange("p (g d) -> p g d", g=4)
        gamma = probsT[:, :, :].rearrange("p a b -> p (a b)")
        beta = wide[:, :]
        xdt = wide[:, 0:1024].rearrange("p (c f) -> p c f", c=QB)
        states = wide[:, 1024:2048].rearrange("p (c f) -> p c f", c=QB)
        resid = [bias, probs]
        rope_i = feats[:, 6:8, :]
        k_idx = vN[:, 1, :, :].rearrange("p j n -> p (j n)")
        XBC = [probs, feats]
        Z = [[probsT[:, 0, :], probsT[:, 1, :]], [feats[:, 4, :], feats[:, 5, :]]]
        LB = [tmp[:, :], probsT[:, 2, :]]
        EB = [probsT[:, 3, :], qT[:, :]]
        QI = [probs[:, 0, :], probs[:, 1, :], probs[:, 2, :], probs[:, 3, :], probsT[:, 0, :], probsT[:, 1, :],
              feats[:, 0, :], feats[:, 1, :]]
        RELU = [[tmp, qT, vT], [gT, probsT[:, 2, :], probsT[:, 3, :]]]

        banks = [ctx.enter_context(nc.psum_tensor(f"bank{i}", [P, S], fp32)) for i in range(8)]
        ACC, B, O, M = banks[0:2], banks[2:6], banks[6], banks[7]
        SETS = [B, [ACC[0], ACC[1], O, M]]
        SCORES = [[B[1], B[2], B[3]], [B[0], O, M]]

        raw_loaded = [sem(f"raw_loaded{s}") for s in range(4)]
        hi_ready, lo_ready, unit_used = sem("hi_ready"), sem("lo_ready"), sem("unit_used")
        acc_taken = sem("acc_taken")
        x_loaded = [sem(f"x_loaded{c}") for c in range(4)]
        par_loaded, poolw_loaded = sem("par_loaded"), sem("poolw_loaded")
        rope_i_loaded, rope_q_loaded = sem("rope_i_loaded"), sem("rope_q_loaded")
        consts, waits_passed = sem("consts"), sem("waits_passed")
        plane_hi, planes_ready = sem("plane_hi"), sem("planes_ready")
        act_steps, dve_steps, pool_steps = sem("act_steps"), sem("dve_steps"), sem("pool_steps")
        fg_turn = sem("fg_turn")
        cum_ready, cum_turned = sem("cum_ready"), sem("cum_turned")
        cum_row_ready, cum_spread = sem("cum_row_ready"), sem("cum_spread")
        scores_done, logits_ready = sem("scores_done"), sem("logits_ready")
        probs_ready, probs_scaled = sem("probs_ready"), sem("probs_scaled")
        probs_turned, probsT_ready, pv_done = sem("probs_turned"), sem("probsT_ready"), sem("pv_done")
        gate_exp, feat_done = sem("gate_exp"), sem("feat_done")
        v_turned, v_ready = sem("v_turned"), sem("v_ready")
        pool_in, pool_done = sem("pool_in"), sem("pool_done")
        resid_loaded = [sem("resid_loaded0"), sem("resid_loaded1")]
        ln_loaded, rows_taken = sem("ln_loaded"), sem("rows_taken")
        var_ready, rstd_ready, rows_normed = sem("var_ready"), sem("rstd_ready"), sem("rows_normed")
        rows_turned, rows_stored = sem("rows_turned"), sem("rows_stored")
        prep_turn, prep_turned = sem("prep_turn"), sem("prep_turned")
        prep_ready, decay_spread = sem("prep_ready"), sem("decay_spread")
        idx_roped, idx_scored, idx_summed = sem("idx_roped"), sem("idx_scored"), sem("idx_summed")
        relu_done = sem("relu_done")
        k_roped, q_roped = sem("k_roped"), sem("q_roped")
        conv_done, silu_exp, silu_done = sem("conv_done"), sem("silu_exp"), sem("silu_done")
        ssd_mm, ssd_vec, ssd_exp = sem("ssd_mm"), sem("ssd_vec"), sem("ssd_exp")
        MM_STEPS, VEC_STEPS, EXP_STEPS = 14, 17, 10

        block = ctx.enter_context(nc.Block())

        @block.sync
        def _(sp):
            def load(m, s):
                sp.dma_start(raw[:, s, :], stream[at(4 * m + s), :, :].rearrange("u p n -> p (u n)"))\
                    .then_inc(raw_loaded[s], 16)

            for s in range(4):
                load(0, s)
                sp.dma_start(feats[:, 4 * s:4 * s + 4, :], x_t[:, 4 * s:4 * s + 4, :]).then_inc(x_loaded[s], 16)
            with sp.Fori(1, ROUNDS) as m:
                for s in range(4):
                    sp.wait_ge(lo_ready, 4 * m - 3 + s)
                    load(m, s)
            sp.wait_ge(rows_stored, 2 * 16 * QB)

        @block.gpsimd
        def _(pool):
            step = Steps(pool, pool_steps)

            def select(ap, op, fill, base, pattern, mult):
                step(nc.gpsimd.affine_select(out=ap, in_=ap, compare_op=op, fill=fill, base=base,
                                             pattern=pattern, channel_multiplier=mult))

            step(nc.gpsimd.memset(ident[:, :], 0.0))
            select(ident[:, :], ALU.not_equal, 1.0, 0, [[-1, P]], 1)
            step(nc.gpsimd.memset(causal, 0.0))
            select(causal[:, S - P:S], ALU.is_ge, BIG, 0, [[-1, P]], 1)
            step(nc.gpsimd.memset(upper[:, :], 0.0))
            select(upper[:, :], ALU.is_ge, -BIG, 0, [[1, P]], -1)
            step(nc.gpsimd.memset(last_row[:, :], 0.0))
            select(last_row[:, :], ALU.not_equal, 1.0, -(P - 1), [[0, P]], 1)
            step(nc.gpsimd.memset(padded[:, 0:16], 0.0))
            nc.gpsimd.memset(ones[:, :], 1.0).then_inc(consts, 1)
            with pool.Fori(0, ROUNDS) as m:
                for s in range(4):
                    pool.wait_ge(hi_ready, 4 * m + s + 1)
                    nc.gpsimd.tensor_sub(w_lo[:, s, :], raw[:, s, :], w_hi[:, s, :].bitcast(fp32))\
                        .then_inc(lo_ready, 1)

        @block.tensor
        def _(pe):
            def mm(o, a, b, start=True, stop=True):
                return nc.tensor.matmul(o, a, b, start=start, stop=stop)

            def turn(o, a):
                k = a.shape[0]
                return nc.tensor.transpose(o, a, ident[0:k, 0:k])

            def project(tile, acc_before):
                m, p = tile
                if acc_before is not None:
                    pe.wait_ge(acc_taken, acc_before)
                for u in range(2):
                    s = 2 * p + u
                    pe.wait_ge(lo_ready, 4 * m + s + 1)
                    for k in range(UK):
                        e = u * UK + k
                        if acc_before is None and p == 0:
                            pe.wait_ge(planes_ready, e + 1)
                        hi, lo = w_hi[:, s, P * k:P * k + P], w_lo[:, s, P * k:P * k + P]
                        mm(ACC[p][:, :], hi, planes_hi[:, e, :], e == 0, False)
                        mm(ACC[p][:, :], hi, planes_lo[:, e, :], False, False)
                        last = mm(ACC[p][:, :], lo, planes_hi[:, e, :], False, e == KT - 1)
                    last.then_inc(unit_used, 1)

            def head_scores(g):
                for i in range(QB):
                    n = P * (i + 1)
                    mm(B[i][:, 0:n], qT[:, P * i:n], kT[:, g, 0:n]).then_inc(scores_done, 1)

            def head_turn(a):
                for i in range(QB):
                    pe.wait_ge(probs_scaled, 4 * a + i + 1)
                    for j in range(i + 1):
                        last = turn(B[j][:, P * i:P * i + P], probs[:, i, P * j:P * j + P])
                last.then_inc(probs_turned, 1)

            def head_pv(a, g):
                pe.wait_ge(probsT_ready, a + 1)
                for j in range(QB):
                    last = mm(O[:, P * j:S], vN[:, g, j, :], probsT[:, j, P * j:S], j == 0, j == QB - 1)
                last.then_inc(pv_done, 1)

            def turn_v(dst, src):
                for j in range(QB):
                    last = turn(dst[:, P * j:P * j + P], src[:, P * j:P * j + P])
                last.then_inc(v_turned, 1)

            def attn_start1(a):
                pe.wait_ge(cum_row_ready, a + 1)
                pe.wait_ge(v_ready, a + 1)
                mm(M[:, :], ones[0:HEADS, :], cum_row[0:HEADS, :]).then_inc(cum_spread, 1)
                pe.wait_ge(acc_taken, T_HEAD1 + 4 * a + 2)
                head_scores(0)

            pe.wait_ge(consts, 1)
            project((0, 0), None)
            for j in range(4):
                project(tile_at(T_HEAD1, j), None if j == 0 else j)
            pe.wait_ge(cum_ready, 1)
            for i in range(QB):
                last = turn(M[:, 8 * i:8 * i + 8], cumT[0:HEADS, P * i:P * i + P])
            last.then_inc(cum_turned, 1)
            pe.wait_ge(acc_taken, T_HEAD1 + 3)
            pe.wait_ge(cum_row_ready, 1)
            turn_v(M, vT)

            with pe.Fori(1, HEADS) as h:
                a = h - 1
                first = T_HEAD1 + 4 * h
                attn_start1(a)
                project(tile_at(T_HEAD1, 0, h, 4), first - 1)
                head_turn(a)
                project(tile_at(T_HEAD1, 1, h, 4), first)
                head_pv(a, 0)
                project(tile_at(T_HEAD1, 2, h, 4), first + 1)
                project(tile_at(T_HEAD1, 3, h, 4), first + 2)
                pe.wait_ge(acc_taken, first + 3)
                turn_v(M, vT)
            a = HEADS - 1
            attn_start1(a)
            project(tile_at(T_CONV, 0), T_CONV - 1)
            head_turn(a)
            project(tile_at(T_CONV, 1), T_CONV)
            head_pv(a, 0)
            project(tile_at(T_CONV, 2), T_CONV + 1)
            project(tile_at(T_CONV, 3), T_CONV + 2)
            with pe.Fori(1, 4) as j:
                for t in range(4):
                    project(tile_at(T_CONV, t, j, 4), T_CONV + 4 * j + t - 1)
            pe.wait_ge(poolw_loaded, 16)
            for g in range(4):
                project(tile_at(T_POOL, 2 * g), T_POOL + 2 * g - 1)
                if g:
                    pe.wait_ge(pool_in, g)
                    mm(O[:, :], poolw[:, g - 1, :], tmp[:, :]).then_inc(pool_done, 1)
                project(tile_at(T_POOL, 2 * g + 1), T_POOL + 2 * g)
            pe.wait_ge(pool_in, 4)
            mm(O[:, :], poolw[:, 3, :], tmp[:, :]).then_inc(pool_done, 1)

            def project_back(blk, first):
                for db in range(4):
                    dst = SETS[db % 2]
                    if db >= 2:
                        pe.wait_ge(rows_taken, 16 * blk + 4 * (db - 1))
                    for q in range(4):
                        m, p = tile_at(first, 4 * db + q)
                        for u in range(2):
                            s = 2 * p + u
                            pe.wait_ge(lo_ready, 4 * m + s + 1)
                            for k in range(2):
                                e = 4 * q + 2 * u + k
                                if db == 0:
                                    pe.wait_ge(planes_ready, (16 if blk == 0 else 48) + e + 1)
                                hi, lo = w_hi[:, s, S * k:S * k + S], w_lo[:, s, S * k:S * k + S]
                                for r in range(QB):
                                    rows = slice(P * r, P * r + P)
                                    mm(dst[r][:, :], planes_hi[:, e, rows], hi, e == 0, False)
                                    mm(dst[r][:, :], planes_hi[:, e, rows], lo, False, False)
                                    last = mm(dst[r][:, :], planes_lo[:, e, rows], hi, False, e == KT - 1)
                            last.then_inc(unit_used, 1)

            project_back(0, T_BACK1)
            for r in range(QB):
                pe.wait_ge(rows_normed, r + 1)
                if r == 0:
                    pe.wait_ge(rows_taken, 16)
                if r >= 2:
                    pe.wait_ge(planes_ready, 32 + 4 * (r - 1))
                for b in range(4):
                    for k in range(4):
                        last = turn(SETS[r % 2][b][:, P * k:P * k + P], feats[:, 4 * r + b, P * k:P * k + P])
                    last.then_inc(rows_turned, 1)

            SK = BACK_TILES
            pe.wait_ge(planes_ready, 48)
            project(tile_at(T_MISC, 0), T_MISC - SK - 1)

            def prepare():
                pe.wait_ge(prep_turn, 5)
                srcs = [cumT[:, :]] + [probs[0:SSD_HEADS, k, :] for k in range(4)]
                for k, src in enumerate(srcs):
                    for i in range(QB):
                        c = 64 * k + 16 * i
                        last = turn(M[:, c:c + 16], src[:, P * i:P * i + P])
                last.then_inc(prep_turned, 1)
                pe.wait_ge(prep_ready, 1)
                mm(O[:, 0:64], last_row[:, :], ecumN[:, :, :].rearrange("p c h -> p (c h)")).then_inc(decay_spread, 1)

            def idx_scores(t):
                pe.wait_ge(idx_roped, t + 1)
                for i in range(1, QB):
                    n = P * (i + 1)
                    for half in range(2):
                        lanes = slice(64 * half, 64 * half + 64)
                        if t:
                            pe.wait_ge(relu_done, 6 * (t - 1) + 2 * i - 1 + half)
                        mm(SCORES[half][i - 1][:, 0:n], QI[t][lanes, P * i:n], k_idx[lanes, 0:n]).then_inc(idx_scored, 1)

            def ssd_tile(n):
                project(tile_at(T_SSD, n), T_SSD + n - SK - 1)

            def ssd_turn(g):
                xbc = XBC[g % 2]
                pe.wait_ge(silu_done, 6 * g + 4)
                for c in range(QB):
                    chunk = slice(P * c, P * c + P)
                    last = mm(B[0][:, chunk], xbc[:, 0, chunk], xbc[:, 1, chunk])
                last.then_inc(ssd_mm, 1)
                for src, dst in ((0, B[3]), (2, O), (3, M)):
                    if src == 3 and g:
                        pe.wait_ge(ssd_exp, EXP_STEPS * (g - 1) + 9)
                    for c in range(QB):
                        chunk = slice(P * c, P * c + P)
                        last = turn(dst[:, chunk], xbc[:, src, chunk])
                    last.then_inc(ssd_mm, 1)

            def ssd_states(g):
                pe.wait_ge(ssd_vec, VEC_STEPS * g + 3)
                for c in range(QB - 1):
                    dst = (B[3] if c < 2 else O)[:, 256 * (c % 2):256 * (c % 2) + 256]
                    last = mm(dst, vT[:, P * c:P * c + P], states[:, c, :])
                last.then_inc(ssd_mm, 1)

            def ssd_spread(g, r):
                pe.wait_ge(ssd_vec, VEC_STEPS * g + (4, 6, 10, 13)[r])
                mm([M, O][r % 2][:, :], ones[0:SSD_HEADS, :], gT[0:SSD_HEADS, :]).then_inc(ssd_mm, 1)

            def ssd_head(g, r):
                pe.wait_ge(ssd_vec, VEC_STEPS * g + (10, 13, 15, 16)[r])
                lanes = slice(64 * (r % 2), 64 * (r % 2) + 64)
                dst, L, E = B[1 + r // 2], LB[r % 2], EB[r % 2]
                for c in range(QB):
                    chunk = slice(P * c, P * c + P)
                    last = mm(dst[lanes, chunk], xdt[:, c, 64 * r:64 * r + 64], L[:, chunk], True, c == 0)
                    if c:
                        last = mm(dst[lanes, chunk], states[:, c, 64 * r:64 * r + 64], E[:, chunk], False, True)
                last.then_inc(ssd_mm, 1)

            def ssd_squares(g):
                pe.wait_ge(ssd_vec, VEC_STEPS * g + 17)
                mm(M[:, :], ones[:, :], LB[0], True, False)
                mm(M[:, :], ones[:, :], LB[1], False, True).then_inc(ssd_mm, 1)

            for it in range(GROUPS + 1):
                g = it - 1
                ssd_tile(6 * it)
                if g >= 1:
                    ssd_squares(g - 1)
                if g >= 0:
                    ssd_turn(g)
                ssd_tile(6 * it + 1)
                if g < 0:
                    prepare()
                else:
                    ssd_states(g)
                    ssd_spread(g, 0)
                ssd_tile(6 * it + 2)
                if g >= 0:
                    ssd_spread(g, 1)
                ssd_tile(6 * it + 3)
                if g >= 0:
                    ssd_head(g, 0)
                    ssd_spread(g, 2)
                ssd_tile(6 * it + 4)
                if g >= 0:
                    ssd_head(g, 1)
                    ssd_spread(g, 3)
                ssd_tile(6 * it + 5)
                if g >= 0:
                    ssd_head(g, 2)
                    ssd_head(g, 3)
            project(tile_at(T_IDX, 6), T_IDX + 6 - SK - 1)
            ssd_squares(GROUPS - 1)
            pe.wait_ge(ssd_exp, EXP_STEPS * (GROUPS - 1) + 9)
            for t in range(3):
                idx_scores(t)
            project(tile_at(T_IDX, 7), T_IDX + 7 - SK - 1)
            for t in range(3, 6):
                idx_scores(t)
            project(tile_at(T_KV, 0), T_KV - SK - 1)
            for t in range(6, 8):
                idx_scores(t)
            for t in range(1, 4):
                project(tile_at(T_KV, t), T_KV + t - SK - 1)
            project(tile_at(T_HEAD2, 0), T_HEAD2 - SK - 1)
            pe.wait_ge(relu_done, 48)
            pe.wait_ge(acc_taken, T_KV + 4 - SK)
            turn_v(O, feats[:, 2, :])
            turn_v(M, feats[:, 3, :])
            project(tile_at(T_HEAD2, 1), T_HEAD2 - SK)
            pe.wait_ge(k_roped, 1)
            pe.wait_ge(v_ready, HEADS + 2)

            def attn_start2(g, h_ready):
                pe.wait_ge(q_roped, h_ready)
                head_scores(g)

            for g, lo_h, hi_h in ((0, 1, 5), (1, 5, 8)):
                with pe.Fori(lo_h, hi_h) as h:
                    a = HEADS + h - 1
                    attn_start2(g, h)
                    project(tile_at(T_HEAD2, 0, h, 2), T_HEAD2 + 2 * h - SK - 1)
                    head_turn(a)
                    project(tile_at(T_HEAD2, 1, h, 2), T_HEAD2 + 2 * h - SK)
                    head_pv(a, g)
            attn_start2(1, 8)
            head_turn(2 * HEADS - 1)
            head_pv(2 * HEADS - 1, 1)
            project_back(1, T_BACK2)

        @block.scalar
        def _(act):
            step = Steps(act, act_steps)

            def signal(ins, s, value):
                ins.then_inc(s, 1)
                act.wait_ge(s, value)

            def round_unit(m, s, reused=True):
                if reused:
                    act.wait_ge(unit_used, 4 * m + s - 3)
                act.wait_ge(raw_loaded[s], 16 * (m + 1))
                signal(nc.scalar.activation(w_hi[:, s, :], raw[:, s, :], ACT.Copy), hi_ready, 4 * m + s + 1)

            def turn_round(tile, end=False):
                m, p = tile
                if not end:
                    for u in range(2):
                        round_unit(m + 1, 2 * p + u)

            def take(tile, dst, count, src=slice(0, P)):
                m, p = tile
                act.wait_ge(unit_used, 4 * m + 2 * p + 2)
                signal(nc.scalar.activation(dst, ACC[p][src, :], ACT.Copy), acc_taken, count)

            def exp_gate(count):
                signal(nc.scalar.activation(gate[:, :], gT[:, :], ACT.Exp, scale=-1.0), gate_exp, count)

            def head_exps(a):
                for i in range(QB):
                    n = P * (i + 1)
                    act.wait_ge(logits_ready, 4 * a + i + 1)
                    signal(nc.scalar.activation(probs[:, i, 0:n], probs[:, i, 0:n], ACT.Exp, bias=nmax[:, i:i + 1],
                                                scale=-1.0, accum_out=rowsum[:, i:i + 1]),
                           probs_ready, 4 * a + i + 1)

            def cut_hi(k, value):
                signal(nc.scalar.activation(planes_hi[:, k, :], feats[:, k, :], ACT.Copy), plane_hi, value)

            act.dma_start(par[:, :], params).then_inc(par_loaded, 16)
            for s in range(4):
                round_unit(0, s, reused=False)
                act.wait_ge(x_loaded[s], 16)
                for k in range(4 * s, 4 * s + 4):
                    cut_hi(k, k + 1)
            act.wait_ge(par_loaded, 16)
            turn_round((0, 0))
            act.wait_ge(unit_used, 2)
            xs = tmp[0:HEADS, :]
            ls = gate[0:HEADS, :]
            signal(nc.scalar.activation(xs, ACC[0][0:HEADS, :], ACT.Identity,
                                        bias=par[0:HEADS, PC["b_f"]:PC["b_f"] + 1]), acc_taken, 1)
            act.wait_ge(fg_turn, 1)
            step(nc.scalar.activation(ls, ls, ACT.Exp))
            signal(nc.scalar.activation(ls, ls, ACT.Ln, bias=1.0), fg_turn, 2)
            for j, dst in enumerate((qT[:, :], kT[:, 0, :], vT[:, :], gT[:, :])):
                t = tile_at(T_HEAD1, j)
                turn_round(t)
                take(t, dst, T_HEAD1 + j + 1)
            act.wait_ge(cum_ready, 1)
            exp_gate(1)
            with step.loop(1, HEADS, 0) as h:
                head_exps(h - 1)
                for j, dst in enumerate((qT[:, :], kT[:, 0, :], vT[:, :], gT[:, :])):
                    t = tile_at(T_HEAD1, j, h, 4)
                    turn_round(t)
                    if j == 3:
                        act.wait_ge(feat_done, h)
                    take(t, dst, T_HEAD1 + 4 * h + j + 1)
                exp_gate(h + 1)
            head_exps(HEADS - 1)

            def conv_tiles(j):
                for k, dst in enumerate((qT[:, :], kT[:, 0, :], vT[:, :], gT[:, :])):
                    t = tile_at(T_CONV, k, j, 4)
                    turn_round(t)
                    if k == 0:
                        act.wait_ge(feat_done, HEADS + j)
                    take(t, dst, T_CONV + 4 * j + k + 1)
                exp_gate(HEADS + j + 1)

            for k, dst in enumerate((qT[:, :], kT[:, 0, :], vT[:, :], gT[:, :])):
                t = tile_at(T_CONV, k)
                turn_round(t)
                if k == 3:
                    act.wait_ge(feat_done, HEADS)
                take(t, dst, T_CONV + k + 1)
            exp_gate(HEADS + 1)
            act.wait_ge(feat_done, HEADS)
            act.dma_start(poolw, pool_w).then_inc(poolw_loaded, 16)
            with step.loop(1, 4, 0) as j:
                conv_tiles(j)
            for g in range(4):
                act_tiles = (padded[:, 16:16 + S], gT[:, :])
                for k in range(2):
                    t = tile_at(T_POOL, 2 * g + k)
                    turn_round(t)
                    if k == 0:
                        act.wait_ge(feat_done, HEADS + 4 + g)
                    take(t, act_tiles[k], T_POOL + 2 * g + k + 1)
                exp_gate(HEADS + 4 + g + 1)

            def back_and_norm(blk, first, rows_in, ln, dst):
                f0 = 16 * (blk + 1)
                act.wait_ge(feat_done, f0)
                act.dma_start(gamma, ln[0:1, :].to_broadcast([P, D])).then_inc(ln_loaded, 16)
                act.dma_start(beta, ln[1:2, :].to_broadcast([P, D])).then_inc(ln_loaded, 16)

                def load_resid(db):
                    act.dma_start(resid[db % 2][:, :, :],
                                  rows_in[:, S * db:S * db + S].rearrange("(m p) d -> p m d", p=P))\
                        .then_inc(resid_loaded[db % 2], 16)

                act.wait_ge(unit_used, 2 * first)
                for k in range(KT):
                    cut_hi(k, 16 + 32 * blk + k + 1)
                if blk:
                    act.wait_ge(rows_stored, 16 * QB)
                load_resid(0)
                load_resid(1)
                for db in range(4):
                    if db in (1, 2):
                        act.wait_ge(rows_taken, 16 * blk + 4 * db)
                        load_resid(db + 1)
                    for q in range(4):
                        t = tile_at(first, 4 * db + q)
                        turn_round(t, end=t[0] + 1 >= ROUNDS)
                for r in range(QB):
                    act.wait_ge(var_ready, 4 * blk + r + 1)
                    step(nc.scalar.activation(rstd[:, r, 0:1], mv[:, r, 1:2], ACT.Ln, bias=par_eps))
                    signal(nc.scalar.activation(rstd[:, r, 0:1], rstd[:, r, 0:1], ACT.Exp, scale=-0.5),
                           rstd_ready, 4 * blk + r + 1)
                for r in range(QB):
                    act.wait_ge(rows_normed, 4 * blk + r + 1)
                    act.dma_start(dst[P * r:P * r + P, :], feats[:, 4 * r:4 * r + 4, :].rearrange("p a b -> p (a b)"))\
                        .then_inc(rows_stored, 16)
                    if blk == 0:
                        for b in range(4):
                            act.wait_ge(rows_turned, 4 * r + b + 1)
                            signal(nc.scalar.activation(
                                planes_hi[:, 4 * b:4 * b + 4, P * r:P * r + P],
                                SETS[r % 2][b][:, :].rearrange("p (k n) -> p k n", k=4), ACT.Copy),
                                plane_hi, 32 + 4 * r + b + 1)

            par_eps = EPS
            back_and_norm(0, T_BACK1, x_rows, ln1, h_rows)

            SK = BACK_TILES
            act.wait_ge(planes_ready, 48)
            act.dma_start(rope_q[:, :, :], rope_qk).then_inc(rope_q_loaded, 16)
            turn_round(tile_at(T_MISC, 0))
            take(tile_at(T_MISC, 0), gT[:, :], T_MISC - SK + 1)
            R = [probs[0:SSD_HEADS, k, :] for k in range(4)]
            act.wait_ge(prep_turn, 1)
            step(nc.scalar.activation(ea[:, :], par[0:SSD_HEADS, PC["a_log"]:PC["a_log"] + 1], ACT.Exp))
            step(nc.scalar.activation(R[1], R[1], ACT.Exp))
            signal(nc.scalar.activation(R[1], R[1], ACT.Ln, bias=1.0), prep_turn, 2)
            act.wait_ge(prep_turn, 3)
            step(nc.scalar.activation(R[1], R[1], ACT.Exp))
            signal(nc.scalar.activation(R[2], cumT[:, :], ACT.Exp), prep_turn, 4)

            def ssd_tile(it, k):
                n = 6 * it + k
                t = tile_at(T_SSD, n)
                turn_round(t)
                if k == 0 and it >= 2:
                    ssd_root(it - 2)
                if it == GROUPS:
                    if k == 0:
                        act.wait_ge(feat_done, 16 + 2 * (it - 1))
                    take(t, QI[k], T_SSD - SK + n + 1)
                    return
                if k < 4:
                    if 4 * it + k:
                        act.wait_ge(conv_done, 4 * it + k)
                    take(t, padded[:, 16:16 + S], T_SSD - SK + n + 1)
                    act.wait_ge(conv_done, 4 * it + k + 1)
                    src = XBC[it % 2][:, k, :]
                else:
                    if it >= 2:
                        act.wait_ge(feat_done, 16 + 2 * (it - 1))
                    src = Z[it % 2][k - 4]
                    if it == 1:
                        act.wait_ge(rows_stored, 16 * QB)
                    take(t, src, T_SSD - SK + n + 1)
                if n:
                    act.wait_ge(silu_done, n)
                signal(nc.scalar.activation(gate[:, :], src, ACT.Exp, scale=-1.0), silu_exp, n + 1)

            def ssd_exps(g, r):
                act.wait_ge(ssd_vec, VEC_STEPS * g + (7, 9, 12, 14)[r])
                n = EXP_STEPS * g + 2 * r + 1
                signal(nc.scalar.activation(LB[r % 2], LB[r % 2], ACT.Exp), ssd_exp, n)
                signal(nc.scalar.activation(EB[r % 2], [M, O][r % 2][:, :], ACT.Exp), ssd_exp, n + 1)

            def ssd_root(g):
                act.wait_ge(ssd_mm, MM_STEPS * g + 14)
                n = EXP_STEPS * g + 9
                signal(nc.scalar.activation(gT[:, :], M[:, :], ACT.Ln, bias=par_eps, scale=1.0 / 256), ssd_exp, n)
                signal(nc.scalar.activation(gT[:, :], gT[:, :], ACT.Exp, scale=-0.5), ssd_exp, n + 1)

            def relu_scores(t):
                for i in range(1, QB):
                    for half in range(2):
                        n = 6 * t + 2 * i - 1 + half
                        act.wait_ge(idx_scored, n)
                        if t:
                            act.wait_ge(idx_summed, n - 6)
                        w = P * (i + 1)
                        signal(nc.scalar.activation(RELU[half][i - 1][:, 0:w], SCORES[half][i - 1][:, 0:w], ACT.Relu),
                               relu_done, n)

            for it in range(GROUPS + 1):
                for k in range(6):
                    ssd_tile(it, k)
                    if it == 1 and k == 0:
                        act.wait_ge(rows_stored, 16 * QB)
                        act.dma_start(rope_i, rope_idx).then_inc(rope_i_loaded, 16)
                    if it and 1 <= k <= 4:
                        ssd_exps(it - 1, k - 1)
            t = tile_at(T_IDX, 6)
            turn_round(t)
            ssd_root(GROUPS - 1)
            act.wait_ge(feat_done, 16 + 2 * GROUPS)
            take(t, QI[6], T_IDX - SK + 7)
            for t in range(3):
                relu_scores(t)
            t = tile_at(T_IDX, 7)
            turn_round(t)
            take(t, QI[7], T_IDX - SK + 8)
            for t in range(3, 6):
                relu_scores(t)
            for k, dst in enumerate((kT[:, 0, :], kT[:, 1, :], feats[:, 2, :], feats[:, 3, :])):
                t = tile_at(T_KV, k)
                turn_round(t)
                take(t, dst, T_KV - SK + k + 1)
                if k == 0:
                    relu_scores(6)
                    relu_scores(7)
            t = tile_at(T_HEAD2, 0)
            turn_round(t)
            act.wait_ge(idx_summed, 48)
            take(t, tmp[:, :], T_HEAD2 - SK + 1)
            for g, src in ((0, O), (1, M)):
                act.wait_ge(v_turned, HEADS + 1 + g)
                signal(nc.scalar.activation(vN[:, g, :, :].rearrange("p j n -> p (j n)"), src[:, :], ACT.Copy),
                       v_ready, HEADS + 1 + g)
            t = tile_at(T_HEAD2, 1)
            turn_round(t)
            take(t, gT[:, :], T_HEAD2 - SK + 2)
            exp_gate(17)
            with step.loop(1, HEADS, 0) as h:
                head_exps(HEADS + h - 1)
                t = tile_at(T_HEAD2, 0, h, 2)
                turn_round(t)
                act.wait_ge(q_roped, h)
                take(t, tmp[:, :], T_HEAD2 - SK + 2 * h + 1)
                t = tile_at(T_HEAD2, 1, h, 2)
                turn_round(t)
                act.wait_ge(feat_done, 16 + 2 * GROUPS + h)
                take(t, gT[:, :], T_HEAD2 - SK + 2 * h + 2)
                exp_gate(17 + h)
            head_exps(2 * HEADS - 1)
            back_and_norm(1, T_BACK2, h_rows, ln2, out)

        @block.vector
        def _(dve):
            V = nc.vector
            step = Steps(dve, dve_steps)

            def signal(ins, s, value):
                ins.then_inc(s, 1)
                dve.wait_ge(s, value)

            def stt(o, a, scalar, b, op0, op1):
                return V.scalar_tensor_tensor(out=o, in0=a, scalar=scalar, in1=b, op0=op0, op1=op1)

            def waited():
                dve.sem_inc(waits_passed, 1)

            def col(name, i=0):
                return par[:, at(PC[name] + i)]

            def sigmoid(g):
                step(V.tensor_scalar(g, g, 1.0, None, ADD))
                step(V.reciprocal(g, g))

            def cut_lo(k, value):
                dve.wait_ge(plane_hi, value)
                signal(V.tensor_sub(planes_lo[:, k, :], feats[:, k, :], planes_hi[:, k, :].bitcast(fp32)),
                       planes_ready, value)

            def pick_cum_row(a):
                signal(V.tensor_scalar(cum_row[0:HEADS, :], cumT[0:HEADS, :], ident[0:HEADS, at(a)], None, MULT),
                       cum_row_ready, a + 1)

            def logit_bias(a):
                dve.wait_ge(cum_spread, a + 1)
                for i in range(QB):
                    n = P * (i + 1)
                    step(stt(bias[:, i, 0:n], M[:, 0:n], cumN[:, i, at(a)], causal[:, S - n:S], SUB, ADD))

            def head_softmax(a):
                for i in range(QB):
                    n = P * (i + 1)
                    dve.wait_ge(scores_done, 4 * a + i + 1)
                    step(stt(probs[:, i, 0:n], B[i][:, 0:n], -SCALE, bias[:, i, 0:n], MULT, ADD))
                    signal(V.tensor_reduce(nmax[:, i:i + 1], probs[:, i, 0:n], AX, MIN), logits_ready, 4 * a + i + 1)

            def head_gate(count):
                dve.wait_ge(gate_exp, count)
                sigmoid(gate[:, :])
                step(V.tensor_mul(gate[:, :], gate[:, :], gT[:, :]))

            def head_scale(a):
                for i in range(QB):
                    n = P * (i + 1)
                    dve.wait_ge(probs_ready, 4 * a + i + 1)
                    step(V.reciprocal(rinv[:, i:i + 1], rowsum[:, i:i + 1]))
                    signal(V.tensor_scalar(probs[:, i, 0:n], probs[:, i, 0:n], rinv[:, i:i + 1], None, MULT),
                           probs_scaled, 4 * a + i + 1)

            def head_take_turned(a):
                dve.wait_ge(probs_turned, a + 1)
                for j in range(QB):
                    ins = V.tensor_copy(probsT[:, j, P * j:S], B[j][:, P * j:S])
                    if j < QB - 1:
                        step(ins)
                    else:
                        signal(ins, probsT_ready, a + 1)

            def head_finish(a, tile, count):
                dve.wait_ge(pv_done, a + 1)
                signal(V.tensor_mul(feats[:, at(tile), :].rearrange("p a n -> p (a n)"), O[:, :], gate[:, :]),
                       feat_done, count)

            def take_v(g, count):
                dve.wait_ge(v_turned, count)
                signal(V.tensor_copy(vN[:, g, :, :].rearrange("p j n -> p (j n)"), M[:, :]), v_ready, count)

            for k in range(KT):
                cut_lo(k, k + 1)
            xs, ls = tmp[0:HEADS, :], gate[0:HEADS, :]
            dve.wait_ge(acc_taken, 1)
            signal(stt(ls, xs, -1.0, xs, MULT, MIN), fg_turn, 1)
            dve.wait_ge(consts, 1)
            step(V.memset(probs[0:HEADS, 0, :], 1.0))
            dve.wait_ge(fg_turn, 2)
            step(stt(xs, xs, 0.0, ls, MIN, SUB))
            signal(V.tensor_tensor_scan(cumT[0:HEADS, :], probs[0:HEADS, 0, :], xs, 0.0, MULT, ADD), cum_ready, 1)
            dve.wait_ge(cum_turned, 1)
            step(V.tensor_copy(cumN[:, :, 0:HEADS], M[:, 0:32].rearrange("p (i h) -> p i h", i=QB)))
            pick_cum_row(0)
            take_v(0, 1)
            with step.loop(1, HEADS, 18) as h:
                a = h - 1
                logit_bias(a)
                head_softmax(a)
                head_gate(a + 1)
                head_scale(a)
                head_take_turned(a)
                head_finish(a, a, a + 1)
                pick_cum_row(h)
                take_v(0, h + 1)
            a = HEADS - 1
            logit_bias(a)
            head_softmax(a)
            head_gate(a + 1)
            head_scale(a)
            head_take_turned(a)
            head_finish(a, a, a + 1)

            def conv_mixer(j):
                dve.wait_ge(acc_taken, T_CONV + 4 * j + 4)
                step(V.tensor_mul(padded[:, 16:16 + S], kT[:, 0, :], vT[:, :]))
                step(V.tensor_scalar(tmp[:, :], padded[:, 14:14 + S], col("conv_w", 3 * j), None, MULT))
                for c in (1, 2):
                    step(stt(tmp[:, :], padded[:, 14 + c:14 + c + S], col("conv_w", 3 * j + c), tmp[:, :], MULT, ADD))
                step(V.tensor_mul(tmp[:, :], tmp[:, :], qT[:, :]))
                head_gate(HEADS + j + 1)
                signal(V.tensor_mul(feats[:, at(HEADS + j), :].rearrange("p a n -> p (a n)"), tmp[:, :], gate[:, :]),
                       feat_done, HEADS + j + 1)

            with step.loop(0, 4, 8) as j:
                conv_mixer(j)

            flat = probs[:, :, :].rearrange("p a b -> p (a b)")
            bufs = [flat[:, 0:16 + S], flat[:, 16 + S:2 * (16 + S)]]
            for b in bufs:
                step(V.memset(b[:, 0:16], 0.0))
            for g in range(4):
                w = 2 << g
                dve.wait_ge(acc_taken, T_POOL + 2 * g + 2)
                src = padded
                for lev in range(g + 1):
                    dst = bufs[lev % 2]
                    sh = 1 << lev
                    step(V.tensor_add(dst[:, 16:16 + S], src[:, 16:16 + S], src[:, 16 - sh:16 - sh + S]))
                    src = dst
                step(stt(tmp[:, :], src[:, 16:16 + S], 1.0 / w, padded[:, 16:16 + S], MULT, SUB))
                step(V.tensor_mul(tmp[:, 0:w - 1], src[:, 16:16 + w - 1], par[:, PC["inv_count"]:PC["inv_count"] + w - 1]))
                signal(V.tensor_sub(tmp[:, 0:w - 1], tmp[:, 0:w - 1], padded[:, 16:16 + w - 1]), pool_in, g + 1)
                head_gate(HEADS + 4 + g + 1)
                dve.wait_ge(pool_done, g + 1)
                signal(stt(feats[:, 12 + g, :], O[:, :], col("pool_scale", g), gate[:, :], MULT, MULT),
                       feat_done, 12 + g + 1)

            def back_and_norm(blk, first):
                for k in range(KT):
                    cut_lo(k, 16 + 32 * blk + k + 1)
                for db in range(4):
                    dve.wait_ge(resid_loaded[db % 2], 16 * (2 * blk + db // 2 + 1))
                    dve.wait_ge(unit_used, 2 * (first + 4 * db + 4))
                    for r in range(QB):
                        signal(stt(feats[:, 4 * r + db, :], resid[db % 2][:, r, :], ALPHA, SETS[db % 2][r][:, :],
                                   MULT, ADD), rows_taken, 16 * blk + 4 * db + r + 1)
                    for r in range(QB):
                        step(V.bn_stats(stats[:, r, db, :], feats[:, 4 * r + db, :]))
                for r in range(QB):
                    signal(V.bn_aggr(mv[:, r, :], stats[:, r, :, :]), var_ready, 4 * blk + r + 1)
                dve.wait_ge(ln_loaded, 32 * (blk + 1))

                def norm(r):
                    row = feats[:, 4 * r:4 * r + 4, :].rearrange("p a b -> p (a b)")
                    dve.wait_ge(rstd_ready, 4 * blk + r + 1)
                    step(V.tensor_scalar(rstd[:, r, 1:2], mv[:, r, 0:1], rstd[:, r, 0:1], -1.0, MULT, MULT))
                    step(V.tensor_scalar(row, row, rstd[:, r, 0:1], rstd[:, r, 1:2], MULT, ADD))
                    step(V.tensor_mul(row, row, gamma))
                    signal(V.tensor_add(row, row, beta), rows_normed, 4 * blk + r + 1)

                def cut_turned(r):
                    for b in range(4):
                        n = 32 + 4 * r + b + 1
                        dve.wait_ge(plane_hi, n)
                        signal(V.tensor_sub(planes_lo[:, 4 * b:4 * b + 4, P * r:P * r + P],
                                            SETS[r % 2][b][:, :].rearrange("p (k n) -> p k n", k=4),
                                            planes_hi[:, 4 * b:4 * b + 4, P * r:P * r + P].bitcast(fp32)),
                               planes_ready, n)

                norm(0)
                for r in range(1, QB):
                    norm(r)
                    if blk == 0:
                        cut_turned(r - 1)
                if blk == 0:
                    cut_turned(QB - 1)

            back_and_norm(0, T_BACK1)

            SK = BACK_TILES

            def rope(dst, src, lanes, table, mask, ins_signal, value, scratch):
                waited()
                step(V.stream_shuffle(scratch[0:lanes, :], src[0:lanes, :], mask))
                step(V.tensor_mul(scratch[0:lanes, :], scratch[0:lanes, :], table[0:lanes, 1, :]))
                step(V.tensor_mul(dst[0:lanes, :], src[0:lanes, :], table[0:lanes, 0, :]))
                ins = V.tensor_add(dst[0:lanes, :], dst[0:lanes, :], scratch[0:lanes, :])
                if ins_signal is None:
                    step(ins)
                else:
                    signal(ins, ins_signal, value)

            swap8 = [i + 8 if i < 8 else i - 8 if i < 16 else i for i in range(32)]
            swap16 = [(i + 16) % 32 for i in range(32)]
            R = [probs[0:SSD_HEADS, k, :] for k in range(4)]
            dve.wait_ge(acc_taken, T_MISC - SK + 1)
            step(V.tensor_copy(R[0], gT[64:80, :]))
            step(V.tensor_scalar(R[0], R[0], par[0:SSD_HEADS, PC["dt_bias"]:PC["dt_bias"] + 1], None, ADD))
            signal(stt(R[1], R[0], -1.0, R[0], MULT, MIN), prep_turn, 1)
            step(V.tensor_copy(R[3], gT[96:112, :]))
            step(V.tensor_scalar(R[3], R[3], W_IDX_SCALE, None, MULT))
            step(V.tensor_copy(k_idx[0:64, :], gT[0:64, :]))
            step(V.memset(R[2], 1.0))
            dve.wait_ge(prep_turn, 2)
            step(stt(R[0], R[0], 0.0, R[1], MAX, ADD))
            step(V.tensor_scalar(R[1], R[0], ea[:, 0:1], -1.0, MULT, MULT))
            for c in range(QB):
                chunk = slice(P * c, P * c + P)
                step(V.tensor_tensor_scan(cumT[:, chunk], R[2][:, chunk], R[1][:, chunk], 0.0, MULT, ADD))
            for c in range(QB):
                chunk, end = slice(P * c, P * c + P), P * c + P - 1
                ins = V.tensor_scalar(R[1][:, chunk], cumT[:, chunk], -1.0, cumT[:, end:end + 1], MULT, ADD)
                if c < QB - 1:
                    step(ins)
                else:
                    signal(ins, prep_turn, 3)
            dve.wait_ge(prep_turn, 4)
            signal(V.tensor_mul(R[1], R[1], R[0]), prep_turn, 5)
            dve.wait_ge(prep_turned, 1)
            for k, dst in enumerate((cumN, dtN, wN, ecumN, widxN)):
                ins = V.tensor_copy(dst[:, :, :], M[:, 64 * k:64 * k + 64].rearrange("p (c h) -> p c h", c=QB))
                if k < 4:
                    step(ins)
                else:
                    signal(ins, prep_ready, 1)
            dve.wait_ge(decay_spread, 1)
            step(V.tensor_copy(chunk_decay[:, :, :], O[:, 0:64].rearrange("p (c h) -> p c h", c=QB)))

            def silu_tile(n):
                it, k = divmod(n, 6)
                dve.wait_ge(acc_taken, T_SSD - SK + n + 1)
                if it == GROUPS:
                    rope(QI[k], QI[k], P, rope_i, swap8, idx_roped, k + 1, padded[:, 16:16 + S])
                    return
                if k < 4:
                    dst = XBC[it % 2][:, k, :]
                    ch = 4 * it + k
                    step(V.tensor_scalar(dst, padded[:, 16:16 + S], col("conv_w2", 4 * ch + 3), col("conv_b2", ch), MULT, ADD))
                    for c in (2, 1, 0):
                        ins = stt(dst, padded[:, 13 + c:13 + c + S], col("conv_w2", 4 * ch + c), dst, MULT, ADD)
                        if c:
                            step(ins)
                        else:
                            signal(ins, conv_done, 4 * it + k + 1)
                else:
                    dst = Z[it % 2][k - 4]
                dve.wait_ge(silu_exp, n + 1)
                sigmoid(gate[:, :])
                signal(V.tensor_mul(dst, dst, gate[:, :]), silu_done, n + 1)

            def ssd_rows(g):
                mm0, vv0 = MM_STEPS * g, VEC_STEPS * g
                dve.wait_ge(ssd_mm, mm0 + 2)
                signal(V.tensor_copy(vT[:, :], B[3][:, :]), ssd_vec, vv0 + 1)
                for t, src in ((0, O), (1, M)):
                    dve.wait_ge(ssd_mm, mm0 + 3 + t)
                    for col_of, dst in ((dtN, xdt), (wN, states)):
                        for h in range(2):
                            d = dst[:, :, P * t + 64 * h:P * t + 64 * h + 64]
                            x = src[:, :].rearrange("p (c f) -> p c f", c=QB)[:, :, 64 * h:64 * h + 64]
                            ins = V.tensor_mul(d, x, col_of[:, :, at(4 * g + 2 * t + h)].to_broadcast([P, QB, 64]))
                            if col_of is wN and h:
                                signal(ins, ssd_vec, vv0 + 2 + t)
                            else:
                                step(ins)

            def pick_row(g, r, value):
                signal(V.tensor_scalar(gT[0:SSD_HEADS, :], cumT[:, :], ident[0:SSD_HEADS, at(4 * g + r)], None, MULT),
                       ssd_vec, VEC_STEPS * g + value)

            def segments(g, r, value):
                for c in range(QB):
                    chunk = slice(P * c, P * c + P)
                    ins = stt(LB[r % 2][:, chunk], [M, O][r % 2][:, chunk], cumN[:, c, at(4 * g + r)], upper[:, :], SUB, ADD)
                    if c < QB - 1:
                        step(ins)
                    else:
                        signal(ins, ssd_vec, VEC_STEPS * g + value)

            def operands(g, r, value):
                dve.wait_ge(ssd_exp, EXP_STEPS * g + 2 * r + 2)
                L, E = LB[r % 2], EB[r % 2]
                step(V.tensor_mul(L, L, B[0][:, :]))
                signal(V.tensor_mul(E, E, XBC[g % 2][:, 1, :]), ssd_vec, VEC_STEPS * g + value)

            def ssd_carry(g):
                dve.wait_ge(ssd_mm, MM_STEPS * g + 5)
                step(V.tensor_copy(states[:, 1, :], B[3][:, 0:256]))
                for c in (1, 2):
                    new, old = states[:, c + 1, :], states[:, c, :]
                    dec = chunk_decay[:, c, at(4 * g, 4)].unsqueeze(2).to_broadcast([P, 4, 64])
                    step(V.tensor_mul(new.rearrange("p (h f) -> p h f", h=4), old.rearrange("p (h f) -> p h f", h=4), dec))
                    ins = V.tensor_add(new, new, (B[3][:, 256:512] if c == 1 else O[:, 0:256]))
                    if c == 1:
                        step(ins)
                    else:
                        signal(ins, ssd_vec, VEC_STEPS * g + 5)

            def ssd_gated(g):
                dve.wait_ge(ssd_mm, MM_STEPS * g + 13)
                for t in range(2):
                    sq, z = LB[t], Z[g % 2][t]
                    step(stt(sq, XBC[g % 2][:, 2 + t, :], col("d_skip", 2 * g + t), B[1 + t][:, :], MULT, ADD))
                    step(V.tensor_mul(z, z, sq))
                    ins = V.tensor_mul(sq, z, z)
                    if t:
                        signal(ins, ssd_vec, VEC_STEPS * g + 17)
                    else:
                        step(ins)

            def ssd_normed(g):
                dve.wait_ge(ssd_exp, EXP_STEPS * g + 10)
                for t in range(2):
                    signal(stt(feats[:, HEADS + 2 * g + t, :], Z[g % 2][t], col("norm_w", 2 * g + t), gT[:, :],
                               MULT, MULT), feat_done, 17 + 2 * g + t)

            for it in range(GROUPS + 1):
                g = it - 1
                if it >= 2:
                    ssd_gated(it - 2)
                if it >= 1:
                    silu_tile(6 * it - 1)
                if it >= 2:
                    ssd_normed(it - 2)
                if it >= 1:
                    ssd_rows(g)
                    pick_row(g, 0, 4)
                if it == 1:
                    dve.wait_ge(rows_stored, 16 * QB)
                silu_tile(6 * it)
                if it >= 1:
                    ssd_carry(g)
                    dve.wait_ge(ssd_mm, MM_STEPS * g + 6)
                    pick_row(g, 1, 6)
                    segments(g, 0, 7)
                silu_tile(6 * it + 1)
                if it >= 1:
                    dve.wait_ge(ssd_mm, MM_STEPS * g + 7)
                    pick_row(g, 2, 8)
                    segments(g, 1, 9)
                    operands(g, 0, 10)
                if it == 1:
                    dve.wait_ge(rope_i_loaded, 16)
                    rope(k_idx, k_idx, 64, rope_i, swap8, None, 0, bias[:, 0, :])
                    step(V.tensor_copy(k_idx[64:128, :], k_idx[0:64, :]))
                silu_tile(6 * it + 2)
                if it >= 1:
                    dve.wait_ge(ssd_mm, MM_STEPS * g + 9)
                    pick_row(g, 3, 11)
                    segments(g, 2, 12)
                    operands(g, 1, 13)
                silu_tile(6 * it + 3)
                if it >= 1:
                    dve.wait_ge(ssd_mm, MM_STEPS * g + 11)
                    segments(g, 3, 14)
                    operands(g, 2, 15)
                    operands(g, 3, 16)
                silu_tile(6 * it + 4)
            ssd_gated(GROUPS - 1)
            silu_tile(6 * GROUPS + 5)
            ssd_normed(GROUPS - 1)

            def sum_scores(t):
                for i in range(1, QB):
                    for half in range(2):
                        n = 6 * t + 2 * i - 1 + half
                        w = P * (i + 1)
                        dve.wait_ge(relu_done, n)
                        relu, wi = RELU[half][i - 1][:, 0:w], widxN[:, i, 2 * t + half:2 * t + half + 1]
                        if t == 0 and half == 0:
                            ins = V.tensor_scalar(bias[:, i, 0:w], relu, wi, None, MULT)
                        else:
                            ins = stt(bias[:, i, 0:w], relu, wi, bias[:, i, 0:w], MULT, ADD)
                        signal(ins, idx_summed, n)

            def rope_q_idx(t):
                dve.wait_ge(acc_taken, T_IDX - SK + t + 1)
                rope(QI[t], QI[t], P, rope_i, swap8, idx_roped, t + 1, padded[:, 16:16 + S])

            rope_q_idx(6)
            for t in range(3):
                sum_scores(t)
            rope_q_idx(7)
            for t in range(3, 8):
                sum_scores(t)

            for i in range(1, QB):
                step(V.memset(bias[0:64, i, P * i + 64:P * i + P], INADMISSIBLE))
            with step.loop(0, TOPK // 8, 6) as _r:
                for i in range(1, QB):
                    n = P * (i + 1)
                    waited()
                    step(V.max(top8[:, :], bias[:, i, 0:n]))
                    waited()
                    step(V.match_replace(bias[:, i, 0:n], top8[:, :], bias[:, i, 0:n], TAKEN))
            for i in range(1, QB):
                n = P * (i + 1)
                step(V.tensor_scalar(bias[:, i, 0:n], bias[:, i, 0:n], TAKEN, BIG, ALU.not_equal, MULT))
            step(V.memset(bias[:, 0, 0:P], 0.0))
            step(V.memset(bias[0:64, 0, 64:P], BIG))
            dve.wait_ge(rope_q_loaded, 16)
            dve.wait_ge(acc_taken, T_KV - SK + 2)
            rope(kT[:, 0, :], kT[:, 0, :], P, rope_q, swap16, None, 0, padded[:, 16:16 + S])
            rope(kT[:, 1, :], kT[:, 1, :], P, rope_q, swap16, k_roped, 1, padded[:, 16:16 + S])
            def rope_head(h):
                dve.wait_ge(acc_taken, T_HEAD2 - SK + 2 * h + 1)
                rope(qT, tmp, P, rope_q, swap16, q_roped, h + 1, padded[:, 16:16 + S])

            rope_head(0)
            with step.loop(1, HEADS, 17) as h:
                a = HEADS + h - 1
                head_softmax(a)
                head_gate(16 + h)
                head_scale(a)
                head_take_turned(a)
                rope_head(h)
                head_finish(a, h - 1, 24 + h)
            a = 2 * HEADS - 1
            head_softmax(a)
            head_gate(24)
            head_scale(a)
            head_take_turned(a)
            head_finish(a, HEADS - 1, 32)
            back_and_norm(1, T_BACK2)


def drawn_up(rows, cols):
    rot = cols // 4
    half = rot // 2
    f32 = np.float32
    inv = np.power(f32(500000.0), -np.arange(half, dtype=f32) * f32(2.0) / f32(rot), dtype=f32)
    ang = np.arange(S, dtype=f32)[:, None] * inv[None, :]
    cos, sin = np.cos(ang).T, np.sin(ang).T
    table = np.zeros((rows, cols, 2, S), f32)
    table[:, :, 0] = 1.0
    table[:, 0:half, 0] = cos
    table[:, half:rot, 0] = cos
    table[:, 0:half, 1] = -sin
    table[:, half:rot, 1] = sin
    return table.reshape(P, 2, S)


def tile_units(w, cols):
    t = np.zeros((D, P), np.float32)
    used = np.asarray(cols) >= 0
    t[:, :len(cols)][:, used] = w[:, np.asarray(cols)[used]]
    return t.reshape(2, UK, P, P).transpose(0, 2, 1, 3).reshape(2, P, UNIT)


def back_units(w):
    return w.reshape(KT // 2, 2, P, 4, S).transpose(3, 0, 2, 1, 4).reshape(32, P, UNIT)


def kernel(**inputs):
    import concourse.bacc as _bacc
    from concourse import mybir as _mybir
    from concourse.bass_utils import run_bass_kernel_spmd as _run

    a = {k: np.ascontiguousarray(v) for k, v in inputs.items()}
    w1, w2 = a["w_in"][0], a["w_in_2"][0]
    span = lambda start, n=P: list(range(start, start + n))
    tiles = [tile_units(w1, span(4096, 8))]
    for h in range(HEADS):
        tiles += [tile_units(w1, span(1024 * k + P * h)) for k in range(4)]
    for j in range(4):
        tiles += [tile_units(w1, span(4104 + 512 * k + P * j)) for k in range(4)]
    for g in range(4):
        tiles += [tile_units(w1, span(6152 + 512 * k + P * g)) for k in range(2)]
    tiles.append(back_units(a["w_out"][0]))
    q, k, v, z, qi, ki, wi, zs, xs, bm, cm, dt = 0, 1024, 1280, 1536, 2560, 3584, 3648, 3664, 4688, 5712, 6224, 6736
    tiles.append(tile_units(w2, span(ki, 64) + span(dt, 16) + [-1] * 16 + span(wi, 16)))
    xbc_tiles = []
    for g in range(GROUPS):
        conv_cols = [bm + P * g, cm + P * g, xs + 256 * g, xs + 256 * g + P]
        xbc_tiles += [c - xs for c in conv_cols]
        tiles += [tile_units(w2, span(c)) for c in conv_cols + [zs + 256 * g, zs + 256 * g + P]]
    tiles += [tile_units(w2, span(qi + P * t)) for t in range(8)]
    tiles += [tile_units(w2, span(c)) for c in (k, k + P, v, v + P)]
    for h in range(HEADS):
        tiles += [tile_units(w2, span(q + P * h)), tile_units(w2, span(z + P * h))]
    tiles.append(back_units(a["w_out_2"][0]))

    par = np.zeros((P, NPAR), np.float32)

    def put(name, x):
        par[:x.shape[0], PC[name]:PC[name] + x.shape[1]] = x

    put("b_f", a["b_f"][0][:, None])
    put("conv_w", a["conv_w"][0].reshape(3, 4, P).transpose(2, 1, 0).reshape(P, 12))
    put("pool_scale", a["pool_scale"][0].reshape(4, P).T)
    put("conv_w2", np.stack([a["conv_w_2"][0][:, c:c + P] for c in xbc_tiles]).transpose(2, 0, 1).reshape(P, 64))
    put("conv_b2", np.stack([a["conv_b_2"][0][c:c + P] for c in xbc_tiles]).T)
    put("dt_bias", a["dt_bias_2"][0][:, None])
    put("a_log", a["a_log_2"][0][:, None])
    put("d_skip", np.repeat(a["d_skip_2"][0], 64).reshape(8, P).T)
    put("norm_w", a["ssd_norm_w_2"][0].reshape(8, P).T)
    put("inv_count", np.broadcast_to(np.float32(1) / np.arange(1, 17, dtype=np.float32), (P, 16)))

    x = a["x"][0]
    arrays = {
        "x_t": np.ascontiguousarray(x.T.reshape(KT, P, S).transpose(1, 0, 2)),
        "x_rows": x,
        "stream": np.concatenate(tiles),
        "params": par,
        "pool_w": np.ascontiguousarray(a["pool_w"][0].transpose(1, 0, 2)),
        "ln1": np.concatenate([a["ln_g"], a["ln_b"]]),
        "ln2": np.concatenate([a["ln_g_2"], a["ln_b_2"]]),
        "rope_idx": drawn_up(2, 64),
        "rope_qk": drawn_up(1, P),
    }
    nc = _bacc.Bacc("TRN2", target_bir_lowering=False, num_devices=1)
    args = [nc.dram_tensor(f"in_{n}", v.shape, _mybir.dt.from_np(v.dtype), kind="ExternalInput").ap()
            for n, v in arrays.items()]
    out = nc.dram_tensor("out", (S, D), _mybir.dt.float32, kind="ExternalOutput").ap()
    block_kernel(nc, *args, out)
    r = _run(nc, [{f"in_{n}": v for n, v in arrays.items()}], core_ids=[0])
    return r.results[0]["out"].reshape(1, S, D)
```

```python
from contextlib import ExitStack, contextmanager

import concourse.bass as bass
from concourse import mybir
import numpy as np

P = 128
S = 512
D = 2048
QB = S // P
KT = D // P
UNIT = 1024
UK = UNIT // P
HEADS = 8
SSD_HEADS = 16
GROUPS = 4
TOPK = min(256, S // 4)
SCALE = float(P) ** -0.5
W_IDX_SCALE = 16 ** -0.5 * 64 ** -0.5
ALPHA = 2.0 ** 0.25
EPS = 1e-5
BIG = 1e30
INADMISSIBLE = -1e38
TAKEN = -3e38

T_HEAD1 = 1
T_CONV = T_HEAD1 + 4 * HEADS
T_POOL = T_CONV + 4 * 4
T_BACK1 = T_POOL + 2 * 4
T_MISC = T_BACK1 + 16
T_SSD = T_MISC + 1
T_IDX = T_SSD + 6 * GROUPS
T_KV = T_IDX + 8
T_HEAD2 = T_KV + 4
T_BACK2 = T_HEAD2 + 2 * HEADS
T_END = T_BACK2 + 16
ROUNDS = T_END // 2
NORM_CUTS = [(0, 1024, 1536, D)] * (QB - 1) + [(0, 640, 1344, D)]
STORES = 16 * 3
BACK_TILES = 16

PC = {}
NPAR = 0
for _name, _n in (("b_f", 1), ("conv_w", 12), ("pool_scale", 4), ("conv_w2", 64), ("conv_b2", 16),
                  ("dt_bias", 1), ("a_log", 1), ("d_skip", 8), ("norm_w", 8), ("inv_count", 16)):
    PC[_name] = NPAR
    NPAR += _n


class Steps:

    def __init__(self, eng, sem):
        self.eng, self.sem, self.n, self.off = eng, sem, 0, 0

    def __call__(self, ins):
        ins.then_inc(self.sem, 1)
        self.n += 1
        self.eng.wait_ge(self.sem, self.off + self.n)

    @contextmanager
    def loop(self, start, end, per):
        n0 = self.n
        with self.eng.Fori(start, end) as i:
            self.off = (i - start) * per
            yield i
            assert self.n - n0 == per, (self.n - n0, per)
        self.off = 0
        self.n = n0 + per * (end - start)


def at(i, n=1):
    return bass.ds(i, n)


def tile_at(first, n, i=0, per=0):
    return (first + n) // 2 + i * (per // 2), (first + n) % 2


BACK_ORDER = [list(range(12)) + [15, 14, 13, 12], list(range(8, 16)) + list(range(8))]

def block_kernel(nc, x_t, x_rows, stream, params, pool_w, ln1, ln2, rope_idx, rope_qk, out):
    fp32, fp32r = mybir.dt.float32, mybir.dt.float32r
    ACT, ALU, AX = mybir.ActivationFunctionType, mybir.AluOpType, mybir.AxisListType.X
    MULT, ADD, SUB, MIN, MAX = ALU.mult, ALU.add, ALU.subtract, ALU.min, ALU.max
    h_rows = nc.dram_tensor("h_rows", [S, D], fp32, kind="Internal").ap()

    with ExitStack() as ctx:
        def sb(name, shape, dt=fp32):
            return ctx.enter_context(nc.sbuf_tensor(name, shape, dt))

        def sem(name):
            return ctx.enter_context(nc.semaphore(name))

        planes_hi = sb("planes_hi", [P, KT, S], fp32r)
        planes_lo = sb("planes_lo", [P, KT, S], fp32r)
        feats = sb("feats", [P, KT, S])
        raw = sb("raw", [P, 4, UNIT])
        w_hi = sb("w_hi", [P, 4, UNIT], fp32r)
        w_lo = sb("w_lo", [P, 4, UNIT], fp32r)
        kT = sb("kT", [P, 2, S])
        vN = sb("vN", [P, 2, QB, P])
        qT = sb("qT", [P, S])
        vT = sb("vT", [P, S])
        gT = sb("gT", [P, S])
        gate = sb("gate", [P, S])
        tmp = sb("tmp", [P, S])
        padded = sb("padded", [P, 16 + S])
        bias = sb("bias", [P, QB, S])
        probs = sb("probs", [P, QB, S])
        probsT = sb("probsT", [P, QB, S])
        wide = sb("wide", [P, D])
        rope_q = sb("rope_q", [P, 2, S])
        ident = sb("ident", [P, P])
        upper = sb("upper", [P, P])
        last_row = sb("last_row", [P, P])
        ones = sb("ones", [P, P])
        par = sb("par", [P, NPAR])
        cumT = sb("cumT", [SSD_HEADS, S])
        cumN = sb("cumN", [P, QB, 16])
        dtN = sb("dtN", [P, QB, 16])
        wN = sb("wN", [P, QB, 16])
        ecumN = sb("ecumN", [P, QB, 16])
        widxN = sb("widxN", [P, QB, 16])
        chunk_decay = sb("chunk_decay", [P, QB, 16])
        nmax = sb("nmax", [P, QB])
        rowsum = sb("rowsum", [P, QB])
        rinv = sb("rinv", [P, QB])
        stats = sb("stats", [P, QB, 4, 6])
        mv = sb("mv", [P, QB, 2])
        rstd = sb("rstd", [P, QB, 2])
        top8 = sb("top8", [P, QB, 8])
        ea = sb("ea", [SSD_HEADS, 1])
        sqrt_table = sb("sqrt_table", [P, 1])

        causal = rope_q[:, 1, :]
        cum_row = rope_q[0:SSD_HEADS, 0, :]
        poolw = probsT[:, 0, :].rearrange("p (g d) -> p g d", g=4)
        gamma = probsT[:, :, :].rearrange("p a b -> p (a b)")
        beta = wide[:, :]
        xdt = wide[:, 0:1024].rearrange("p (c f) -> p c f", c=QB)
        states = wide[:, 1024:2048].rearrange("p (c f) -> p c f", c=QB)
        resid = [bias, probs]

        def norm_part(r, i):
            return feats[:, 4 * r:4 * r + 4, :].rearrange("p a b -> p (a b)")[:, NORM_CUTS[r][i]:NORM_CUTS[r][i + 1]]

        rope_i = feats[:, 6:8, :]
        k_idx = vN[:, 1, :, :].rearrange("p j n -> p (j n)")
        XBC = [probs, feats]
        Z = [[probsT[:, 0, :], probsT[:, 1, :]], [feats[:, 4, :], feats[:, 5, :]]]
        LB = [tmp[:, :], probsT[:, 2, :]]
        EB = [probsT[:, 3, :], qT[:, :]]
        QI = [probs[:, 0, :], probs[:, 1, :], probs[:, 2, :], probs[:, 3, :], probsT[:, 0, :], probsT[:, 1, :],
              feats[:, 0, :], feats[:, 1, :]]
        RELU = [[tmp, qT, vT], [gT, probsT[:, 2, :], probsT[:, 3, :]]]

        banks = [ctx.enter_context(nc.psum_tensor(f"bank{i}", [P, S], fp32)) for i in range(8)]
        ACC, B, O, M = banks[0:2], banks[2:6], banks[6], banks[7]
        SETS = [B, [ACC[1], ACC[0], O, M]]
        BACK_SETS = [SETS, SETS[::-1]]
        SCORES = [[B[1], B[2], B[3]], [B[0], O, M]]

        raw_loaded = [sem(f"raw_loaded{s}") for s in range(4)]
        hi_ready, lo_ready, unit_used = sem("hi_ready"), sem("lo_ready"), sem("unit_used")
        acc_taken = sem("acc_taken")
        x_loaded = [sem(f"x_loaded{c}") for c in range(4)]
        par_loaded, poolw_loaded = sem("par_loaded"), sem("poolw_loaded")
        rope_i_loaded, rope_q_loaded = sem("rope_i_loaded"), sem("rope_q_loaded")
        consts, waits_passed = sem("consts"), sem("waits_passed")
        plane_hi, planes_ready = sem("plane_hi"), sem("planes_ready")
        act_steps, dve_steps, pool_steps = sem("act_steps"), sem("dve_steps"), sem("pool_steps")
        fg_turn = sem("fg_turn")
        cum_ready, cum_turned = sem("cum_ready"), sem("cum_turned")
        cum_row_ready, cum_spread = sem("cum_row_ready"), sem("cum_spread")
        scores_done, logits_ready = sem("scores_done"), sem("logits_ready")
        probs_ready, probs_scaled = sem("probs_ready"), sem("probs_scaled")
        probs_turned, probsT_ready, pv_done = sem("probs_turned"), sem("probsT_ready"), sem("pv_done")
        gate_exp, feat_done = sem("gate_exp"), sem("feat_done")
        v_turned, v_ready = sem("v_turned"), sem("v_ready")
        pool_in, pool_done = sem("pool_in"), sem("pool_done")
        resid_loaded = [sem("resid_loaded0"), sem("resid_loaded1")]
        ln_loaded, rows_taken = sem("ln_loaded"), sem("rows_taken")
        var_ready, root_ready, rstd_ready = sem("var_ready"), sem("root_ready"), sem("rstd_ready")
        rows_scaled, rows_normed = sem("rows_scaled"), sem("rows_normed")
        rest_normed, rows_summed = sem("rest_normed"), sem("rows_summed")
        rows_turned, rows_stored = sem("rows_turned"), sem("rows_stored")
        prep_turn, prep_turned = sem("prep_turn"), sem("prep_turned")
        prep_ready, decay_spread = sem("prep_ready"), sem("decay_spread")
        idx_roped, idx_scored, idx_summed = sem("idx_roped"), sem("idx_scored"), sem("idx_summed")
        relu_done = sem("relu_done")
        keys_found, keys_taken = sem("keys_found"), sem("keys_taken")
        k_roped, q_roped = sem("k_roped"), sem("q_roped")
        conv_done, silu_exp, silu_done = sem("conv_done"), sem("silu_exp"), sem("silu_done")
        ssd_mm, ssd_vec, ssd_exp = sem("ssd_mm"), sem("ssd_vec"), sem("ssd_exp")
        MM_STEPS, VEC_STEPS, EXP_STEPS = 14, 17, 10

        block = ctx.enter_context(nc.Block())

        @block.sync
        def _(sp):
            def load(m, s):
                sp.dma_start(raw[:, s, :], stream[at(4 * m + s), :, :].rearrange("u p n -> p (u n)"))\
                    .then_inc(raw_loaded[s], 16)

            for s in range(4):
                load(0, s)
                sp.dma_start(feats[:, 4 * s:4 * s + 4, :], x_t[:, 4 * s:4 * s + 4, :]).then_inc(x_loaded[s], 16)
            with sp.Fori(1, ROUNDS) as m:
                for s in range(4):
                    sp.wait_ge(lo_ready, 4 * m - 3 + s)
                    load(m, s)
            sp.wait_ge(rows_stored, 2 * STORES * QB)

        @block.gpsimd
        def _(pool):
            step = Steps(pool, pool_steps)

            def select(ap, op, fill, base, pattern, mult):
                step(nc.gpsimd.affine_select(out=ap, in_=ap, compare_op=op, fill=fill, base=base,
                                             pattern=pattern, channel_multiplier=mult))

            step(nc.gpsimd.memset(ident[:, :], 0.0))
            select(ident[:, :], ALU.not_equal, 1.0, 0, [[-1, P]], 1)
            step(nc.gpsimd.memset(causal, 0.0))
            select(causal[:, S - P:S], ALU.is_ge, BIG, 0, [[-1, P]], 1)
            step(nc.gpsimd.memset(upper[:, :], 0.0))
            select(upper[:, :], ALU.is_ge, -BIG, 0, [[1, P]], -1)
            step(nc.gpsimd.memset(last_row[:, :], 0.0))
            select(last_row[:, :], ALU.not_equal, 1.0, -(P - 1), [[0, P]], 1)
            step(nc.gpsimd.memset(padded[:, 0:16], 0.0))
            nc.gpsimd.memset(ones[:, :], 1.0).then_inc(consts, 1)

            def low_part(m, s):
                pool.wait_ge(hi_ready, 4 * m + s + 1)
                nc.gpsimd.tensor_sub(w_lo[:, s, :], raw[:, s, :], w_hi[:, s, :].bitcast(fp32)).then_inc(lo_ready, 1)

            def low_parts(start, end):
                with pool.Fori(start, end) as m:
                    for s in range(4):
                        low_part(m, s)

            def norm_rows(blk):
                pool.wait_ge(ln_loaded, 32 * (blk + 1))
                for r in range(QB):
                    n, part = 4 * blk + r + 1, norm_part(r, 0)
                    pool.wait_ge(rows_scaled, n)
                    step(nc.gpsimd.tensor_mul(part, part, gamma[:, 0:NORM_CUTS[r][1]]))
                    nc.gpsimd.tensor_add(part, part, beta[:, 0:NORM_CUTS[r][1]]).then_inc(rows_normed, 1)

            m = T_MISC // 2
            low_parts(0, m)
            low_part(m, 0)
            low_part(m, 1)
            norm_rows(0)
            low_part(m, 2)
            low_part(m, 3)
            low_parts(m + 1, ROUNDS)
            norm_rows(1)

        @block.tensor
        def _(pe):
            def mm(o, a, b, start=True, stop=True):
                return nc.tensor.matmul(o, a, b, start=start, stop=stop)

            def turn(o, a):
                k = a.shape[0]
                return nc.tensor.transpose(o, a, ident[0:k, 0:k])

            def project(tile, acc_before, planes_cut=None):
                m, p = tile
                if acc_before is not None:
                    pe.wait_ge(acc_taken, acc_before)
                for u in range(2):
                    s = 2 * p + u
                    pe.wait_ge(lo_ready, 4 * m + s + 1)
                    for k in range(UK):
                        e = u * UK + k
                        if planes_cut is not None:
                            pe.wait_ge(planes_ready, planes_cut(e))
                        hi, lo = w_hi[:, s, P * k:P * k + P], w_lo[:, s, P * k:P * k + P]
                        mm(ACC[p][:, :], hi, planes_hi[:, e, :], e == 0, False)
                        mm(ACC[p][:, :], hi, planes_lo[:, e, :], False, False)
                        last = mm(ACC[p][:, :], lo, planes_hi[:, e, :], False, e == KT - 1)
                    last.then_inc(unit_used, 1)

            def head_scores(g):
                for i in range(QB):
                    n = P * (i + 1)
                    mm(B[i][:, 0:n], qT[:, P * i:n], kT[:, g, 0:n]).then_inc(scores_done, 1)

            def head_turn(a):
                for i in range(QB):
                    pe.wait_ge(probs_scaled, 4 * a + i + 1)
                    for j in range(i + 1):
                        last = turn(B[j][:, P * i:P * i + P], probs[:, i, P * j:P * j + P])
                last.then_inc(probs_turned, 1)

            def head_pv(a, g, dst=O):
                pe.wait_ge(probsT_ready, a + 1)
                for j in range(QB):
                    last = mm(dst[:, P * j:S], vN[:, g, j, :], probsT[:, j, P * j:S], j == 0, j == QB - 1)
                last.then_inc(pv_done, 1)

            def turn_v(dst, src):
                for j in range(QB):
                    last = turn(dst[:, P * j:P * j + P], src[:, P * j:P * j + P])
                last.then_inc(v_turned, 1)

            def attn_start1(a):
                pe.wait_ge(cum_row_ready, a + 1)
                pe.wait_ge(v_ready, a + 1)
                mm(M[:, :], ones[0:HEADS, :], cum_row[0:HEADS, :]).then_inc(cum_spread, 1)
                pe.wait_ge(acc_taken, T_HEAD1 + 4 * a + 2)
                head_scores(0)

            pe.wait_ge(consts, 1)
            project((0, 0), None, lambda e: e + 1)
            for j in range(4):
                project(tile_at(T_HEAD1, j), None if j == 0 else j)
            pe.wait_ge(cum_ready, 1)
            for i in range(QB):
                last = turn(M[:, 8 * i:8 * i + 8], cumT[0:HEADS, P * i:P * i + P])
            last.then_inc(cum_turned, 1)
            pe.wait_ge(acc_taken, T_HEAD1 + 3)
            pe.wait_ge(cum_row_ready, 1)
            turn_v(M, vT)

            with pe.Fori(1, HEADS) as h:
                a = h - 1
                first = T_HEAD1 + 4 * h
                attn_start1(a)
                project(tile_at(T_HEAD1, 0, h, 4), first - 1)
                head_turn(a)
                project(tile_at(T_HEAD1, 1, h, 4), first)
                head_pv(a, 0)
                project(tile_at(T_HEAD1, 2, h, 4), first + 1)
                project(tile_at(T_HEAD1, 3, h, 4), first + 2)
                pe.wait_ge(acc_taken, first + 3)
                turn_v(M, vT)
            a = HEADS - 1
            attn_start1(a)
            project(tile_at(T_CONV, 0), T_CONV - 1)
            head_turn(a)
            project(tile_at(T_CONV, 1), T_CONV)
            head_pv(a, 0)
            project(tile_at(T_CONV, 2), T_CONV + 1)
            project(tile_at(T_CONV, 3), T_CONV + 2)
            with pe.Fori(1, 4) as j:
                for t in range(4):
                    project(tile_at(T_CONV, t, j, 4), T_CONV + 4 * j + t - 1)
            pe.wait_ge(poolw_loaded, 16)
            def pool_window(g):
                pe.wait_ge(pool_in, 4 - g)
                mm(O[:, :], poolw[:, g, :], tmp[:, :]).then_inc(pool_done, 1)

            for n, g in enumerate((3, 2, 1, 0)):
                project(tile_at(T_POOL, 2 * n), T_POOL + 2 * n - 1)
                if n:
                    pool_window(g + 1)
                project(tile_at(T_POOL, 2 * n + 1), T_POOL + 2 * n)

            def back_products(blk, db, n, s, k, r):
                e, rows, o = BACK_ORDER[blk][n], slice(P * r, P * r + P), BACK_SETS[blk][db % 2][r][:, :]
                hi, lo = w_hi[:, s, S * k:S * k + S], w_lo[:, s, S * k:S * k + S]
                mm(o, planes_hi[:, e, rows], hi, n == 0, False)
                mm(o, planes_hi[:, e, rows], lo, False, False)
                return mm(o, planes_lo[:, e, rows], hi, False, n == KT - 1)

            def project_back(blk, first, after_unit, after_row_block):
                for db in range(4):
                    if db >= 2:
                        pe.wait_ge(rows_taken, 16 * blk + 4 * (db - 1))
                    for q in range(4 if db < 3 else 2):
                        m, p = tile_at(first, 4 * db + q)
                        for u in range(2):
                            s = 2 * p + u
                            pe.wait_ge(lo_ready, 4 * m + s + 1)
                            for k in range(2):
                                n = 4 * q + 2 * u + k
                                if db == 0:
                                    pe.wait_ge(planes_ready, (16 if blk == 0 else 48) + n + 1)
                                for r in range(QB):
                                    last = back_products(blk, db, n, s, k, r)
                            last.then_inc(unit_used, 1)
                            if db == 0 and 2 * q + u in after_unit:
                                after_unit[2 * q + u]()
                for r in range(QB):
                    for v in range(4):
                        m, p = tile_at(first, 14 + v // 2)
                        s = 2 * p + v % 2
                        if r == 0:
                            pe.wait_ge(lo_ready, 4 * m + s + 1)
                        for k in range(2):
                            last = back_products(blk, 3, 8 + 2 * v + k, s, k, r)
                        if r == QB - 1:
                            last.then_inc(unit_used, 1)
                        elif v == 3:
                            last.then_inc(rows_summed, 1)
                        if (r, v) in after_row_block:
                            after_row_block[r, v]()

            def turn_rows(r):
                pe.wait_ge(rows_normed, r + 1)
                pe.wait_ge(rest_normed, 2 * r + 2)
                if r == 0:
                    pe.wait_ge(rows_taken, 12)
                if r == 1:
                    pe.wait_ge(rows_taken, 16)
                if r >= 2:
                    pe.wait_ge(planes_ready, 32 + 4 * (r - 1))
                for b in range(4):
                    for k in range(4):
                        last = turn(SETS[r % 2][b][:, P * k:P * k + P], feats[:, 4 * r + b, P * k:P * k + P])
                    last.then_inc(rows_turned, 1)

            project_back(0, T_BACK1, {0: lambda: pool_window(0)}, {(3, 0): lambda: turn_rows(0)})
            for r in range(1, QB):
                turn_rows(r)

            SK = BACK_TILES
            project(tile_at(T_MISC, 0), T_MISC - SK - 1, lambda e: 32 + 4 * (QB - 1) + e // 4 + 1)

            def prepare():
                pe.wait_ge(prep_turn, 5)
                srcs = [cumT[:, :]] + [probs[0:SSD_HEADS, k, :] for k in range(4)]
                for k, src in enumerate(srcs):
                    for i in range(QB):
                        c = 64 * k + 16 * i
                        last = turn(M[:, c:c + 16], src[:, P * i:P * i + P])
                last.then_inc(prep_turned, 1)
                pe.wait_ge(prep_ready, 1)
                mm(O[:, 0:64], last_row[:, :], ecumN[:, :, :].rearrange("p c h -> p (c h)")).then_inc(decay_spread, 1)

            def idx_scores(t):
                pe.wait_ge(idx_roped, t + 1)
                for i in range(1, QB):
                    n = P * (i + 1)
                    if t:
                        pe.wait_ge(relu_done, 6 * (t - 1) + 2 * i)
                    for half in range(2):
                        lanes = slice(64 * half, 64 * half + 64)
                        if t == 0 and SCORES[half][i - 1] is M:
                            pe.wait_ge(ssd_exp, EXP_STEPS * (GROUPS - 1) + 9)
                        mm(SCORES[half][i - 1][:, 0:n], QI[t][lanes, P * i:n], k_idx[lanes, 0:n]).then_inc(idx_scored, 1)

            def ssd_tile(n):
                project(tile_at(T_SSD, n), T_SSD + n - SK - 1)

            def ssd_turn(g):
                xbc = XBC[g % 2]
                pe.wait_ge(silu_done, 6 * g + 4)
                for c in range(QB):
                    chunk = slice(P * c, P * c + P)
                    last = mm(B[0][:, chunk], xbc[:, 0, chunk], xbc[:, 1, chunk])
                last.then_inc(ssd_mm, 1)
                for src, dst in ((0, B[3]), (2, O), (3, M)):
                    if src == 3 and g:
                        pe.wait_ge(ssd_exp, EXP_STEPS * (g - 1) + 9)
                    for c in range(QB):
                        chunk = slice(P * c, P * c + P)
                        last = turn(dst[:, chunk], xbc[:, src, chunk])
                    last.then_inc(ssd_mm, 1)

            def ssd_states(g):
                pe.wait_ge(ssd_vec, VEC_STEPS * g + 3)
                for c in range(QB - 1):
                    dst = (B[3] if c < 2 else O)[:, 256 * (c % 2):256 * (c % 2) + 256]
                    last = mm(dst, vT[:, P * c:P * c + P], states[:, c, :])
                last.then_inc(ssd_mm, 1)

            def ssd_spread(g, r):
                pe.wait_ge(ssd_vec, VEC_STEPS * g + (4, 6, 10, 13)[r])
                mm([M, O][r % 2][:, :], ones[0:SSD_HEADS, :], gT[0:SSD_HEADS, :]).then_inc(ssd_mm, 1)

            def ssd_head(g, r):
                pe.wait_ge(ssd_vec, VEC_STEPS * g + (10, 13, 15, 16)[r])
                lanes = slice(64 * (r % 2), 64 * (r % 2) + 64)
                dst, L, E = B[1 + r // 2], LB[r % 2], EB[r % 2]
                for c in range(QB):
                    chunk = slice(P * c, P * c + P)
                    last = mm(dst[lanes, chunk], xdt[:, c, 64 * r:64 * r + 64], L[:, chunk], True, c == 0)
                    if c:
                        last = mm(dst[lanes, chunk], states[:, c, 64 * r:64 * r + 64], E[:, chunk], False, True)
                last.then_inc(ssd_mm, 1)

            def ssd_squares(g):
                pe.wait_ge(ssd_vec, VEC_STEPS * g + 17)
                mm(M[:, :], ones[:, :], LB[0], True, False)
                mm(M[:, :], ones[:, :], LB[1], False, True).then_inc(ssd_mm, 1)

            for it in range(GROUPS + 1):
                g = it - 1
                ssd_tile(6 * it)
                if g >= 1:
                    ssd_squares(g - 1)
                if g >= 0:
                    ssd_turn(g)
                ssd_tile(6 * it + 1)
                if g < 0:
                    prepare()
                else:
                    ssd_states(g)
                    ssd_spread(g, 0)
                ssd_tile(6 * it + 2)
                if g >= 0:
                    ssd_spread(g, 1)
                ssd_tile(6 * it + 3)
                if g >= 0:
                    ssd_head(g, 0)
                    ssd_spread(g, 2)
                ssd_tile(6 * it + 4)
                if g >= 0:
                    ssd_head(g, 1)
                    ssd_spread(g, 3)
                ssd_tile(6 * it + 5)
                if g >= 0:
                    ssd_head(g, 2)
                    ssd_head(g, 3)
            project(tile_at(T_IDX, 6), T_IDX + 6 - SK - 1)
            ssd_squares(GROUPS - 1)
            project(tile_at(T_IDX, 7), T_IDX + 7 - SK - 1)
            for t in range(8):
                idx_scores(t)
            project(tile_at(T_KV, 0), T_KV - SK - 1)
            for t in range(1, 4):
                project(tile_at(T_KV, t), T_KV + t - SK - 1)
            project(tile_at(T_HEAD2, 0), T_HEAD2 - SK - 1)
            pe.wait_ge(relu_done, 48)
            pe.wait_ge(acc_taken, T_KV + 4 - SK)
            turn_v(O, feats[:, 2, :])
            turn_v(M, feats[:, 3, :])
            project(tile_at(T_HEAD2, 1), T_HEAD2 - SK)
            pe.wait_ge(k_roped, 1)
            pe.wait_ge(v_ready, HEADS + 2)

            def attn_start2(g, h_ready):
                pe.wait_ge(q_roped, h_ready)
                head_scores(g)

            for g, lo_h, hi_h in ((0, 1, 5), (1, 5, 8)):
                with pe.Fori(lo_h, hi_h) as h:
                    a = HEADS + h - 1
                    attn_start2(g, h)
                    project(tile_at(T_HEAD2, 0, h, 2), T_HEAD2 + 2 * h - SK - 1)
                    head_turn(a)
                    project(tile_at(T_HEAD2, 1, h, 2), T_HEAD2 + 2 * h - SK)
                    head_pv(a, g)
            a = 2 * HEADS - 1
            attn_start2(1, 8)
            pe.wait_ge(acc_taken, T_BACK2 - SK)
            pe.wait_ge(feat_done, a + 16)
            project_back(1, T_BACK2, {1: lambda: head_turn(a), 3: lambda: head_pv(a, 1, B[0])}, {})

        @block.scalar
        def _(act):
            step = Steps(act, act_steps)

            def signal(ins, s, value):
                ins.then_inc(s, 1)
                act.wait_ge(s, value)

            def round_unit(m, s, reused=True):
                if reused:
                    act.wait_ge(unit_used, 4 * m + s - 3)
                act.wait_ge(raw_loaded[s], 16 * (m + 1))
                signal(nc.scalar.activation(w_hi[:, s, :], raw[:, s, :], ACT.Copy), hi_ready, 4 * m + s + 1)

            def turn_round(tile, end=False):
                m, p = tile
                if not end:
                    for u in range(2):
                        round_unit(m + 1, 2 * p + u)

            def take(tile, dst, count):
                m, p = tile
                act.wait_ge(unit_used, 4 * m + 2 * p + 2)
                signal(nc.scalar.activation(dst, ACC[p][:, :], ACT.Copy), acc_taken, count)

            def exp_gate(count):
                signal(nc.scalar.activation(gate[:, :], gT[:, :], ACT.Exp, scale=-1.0), gate_exp, count)

            def head_exps(a):
                for i in range(QB):
                    n = P * (i + 1)
                    act.wait_ge(logits_ready, 4 * a + i + 1)
                    signal(nc.scalar.activation(probs[:, i, 0:n], probs[:, i, 0:n], ACT.Exp, bias=nmax[:, i:i + 1],
                                                scale=-1.0, accum_out=rowsum[:, i:i + 1]),
                           probs_ready, 4 * a + i + 1)

            def cut_hi(k, value):
                signal(nc.scalar.activation(planes_hi[:, k, :], feats[:, k, :], ACT.Copy), plane_hi, value)

            act.dma_start(par[:, :], params).then_inc(par_loaded, 16)
            for s in range(4):
                round_unit(0, s, reused=False)
                act.wait_ge(x_loaded[s], 16)
                for k in range(4 * s, 4 * s + 4):
                    cut_hi(k, k + 1)
            act.wait_ge(par_loaded, 16)
            turn_round((0, 0))
            act.wait_ge(unit_used, 2)
            xs = tmp[0:HEADS, :]
            ls = gate[0:HEADS, :]
            signal(nc.scalar.activation(xs, ACC[0][0:HEADS, :], ACT.Identity,
                                        bias=par[0:HEADS, PC["b_f"]:PC["b_f"] + 1]), acc_taken, 1)
            act.wait_ge(fg_turn, 1)
            step(nc.scalar.activation(ls, ls, ACT.Exp))
            signal(nc.scalar.activation(ls, ls, ACT.Ln, bias=1.0), fg_turn, 2)
            for j, dst in enumerate((qT[:, :], kT[:, 0, :], vT[:, :], gT[:, :])):
                t = tile_at(T_HEAD1, j)
                turn_round(t)
                take(t, dst, T_HEAD1 + j + 1)
            act.wait_ge(cum_ready, 1)
            exp_gate(1)
            with step.loop(1, HEADS, 0) as h:
                head_exps(h - 1)
                for j, dst in enumerate((qT[:, :], kT[:, 0, :], vT[:, :], gT[:, :])):
                    t = tile_at(T_HEAD1, j, h, 4)
                    turn_round(t)
                    if j == 3:
                        act.wait_ge(feat_done, h)
                    take(t, dst, T_HEAD1 + 4 * h + j + 1)
                exp_gate(h + 1)
            head_exps(HEADS - 1)

            def conv_tiles(j):
                for k, dst in enumerate((qT[:, :], kT[:, 0, :], vT[:, :], gT[:, :])):
                    t = tile_at(T_CONV, k, j, 4)
                    turn_round(t)
                    if k == 0:
                        act.wait_ge(feat_done, HEADS + j)
                    take(t, dst, T_CONV + 4 * j + k + 1)
                exp_gate(HEADS + j + 1)

            for k, dst in enumerate((qT[:, :], kT[:, 0, :], vT[:, :], gT[:, :])):
                t = tile_at(T_CONV, k)
                turn_round(t)
                if k == 3:
                    act.wait_ge(feat_done, HEADS)
                take(t, dst, T_CONV + k + 1)
            exp_gate(HEADS + 1)
            act.wait_ge(feat_done, HEADS)
            act.dma_start(poolw, pool_w).then_inc(poolw_loaded, 16)
            with step.loop(1, 4, 0) as j:
                conv_tiles(j)
            for n in range(4):
                for k, dst in enumerate((gT[:, :], padded[:, 16:16 + S])):
                    t = tile_at(T_POOL, 2 * n + k)
                    if 2 * n + k < 7:
                        turn_round(t)
                    if k == 0:
                        act.wait_ge(feat_done, HEADS + 4 + n)
                    take(t, dst, T_POOL + 2 * n + k + 1)
                    if k == 0:
                        exp_gate(HEADS + 4 + n + 1)

            def back_and_norm(blk, first, rows_in, ln, dst, after_cut):
                act.wait_ge(unit_used, 2 * first)
                act.wait_ge(feat_done, 16 * blk + 15)
                for n in range(KT):
                    if n == KT - 1:
                        turn_round(tile_at(first, 0))
                        turn_round(tile_at(first, 1))
                        act.wait_ge(feat_done, 16 * (blk + 1))
                    cut_hi(BACK_ORDER[blk][n], 16 + 32 * blk + n + 1)
                    if n in after_cut:
                        after_cut[n]()

                def load_resid(db):
                    act.dma_start(resid[db % 2][:, :, :],
                                  rows_in[:, S * db:S * db + S].rearrange("(m p) d -> p m d", p=P))\
                        .then_inc(resid_loaded[db % 2], 16)

                if blk:
                    act.wait_ge(rows_stored, STORES * QB)
                load_resid(0)
                load_resid(1)
                act.dma_start(gamma, ln[0:1, :].to_broadcast([P, D])).then_inc(ln_loaded, 16)
                act.dma_start(beta, ln[1:2, :].to_broadcast([P, D])).then_inc(ln_loaded, 16)
                for db in range(4):
                    if db in (1, 2):
                        act.wait_ge(rows_taken, 16 * blk + 4 * db)
                        load_resid(db + 1)
                    for q in ((2, 3), range(4), range(4), (0, 1))[db]:
                        t = tile_at(first, 4 * db + q)
                        turn_round(t, end=t[0] + 1 >= ROUNDS)
                step(nc.scalar.activation(sqrt_table[:, :], ones[:, 0:1], ACT.Sqrt))

                def root(r):
                    n = 4 * blk + r + 1
                    act.wait_ge(var_ready, n)
                    signal(nc.scalar.activation(rstd[:, r, 0:1], mv[:, r, 1:2], ACT.Sqrt, bias=EPS), root_ready, n)

                def scale_rows(r):
                    n, part = 4 * blk + r + 1, norm_part(r, 0)
                    act.wait_ge(rstd_ready, n)
                    signal(nc.scalar.activation(part, part, ACT.Identity, bias=rstd[:, r, 1:2], scale=rstd[:, r, 0:1]),
                           rows_scaled, n)

                def store_rows(r):
                    n = 4 * blk + r + 1
                    for i, ready, value in ((1, rest_normed, 2 * n - 1), (0, rows_normed, n), (2, rest_normed, 2 * n)):
                        act.wait_ge(ready, value)
                        act.dma_start(dst[P * r:P * r + P, NORM_CUTS[r][i]:NORM_CUTS[r][i + 1]], norm_part(r, i))\
                            .then_inc(rows_stored, 16)

                def cut_turned(r):
                    for b in range(4):
                        act.wait_ge(rows_turned, 4 * r + b + 1)
                        signal(nc.scalar.activation(
                            planes_hi[:, 4 * b:4 * b + 4, P * r:P * r + P],
                            SETS[r % 2][b][:, :].rearrange("p (k n) -> p k n", k=4), ACT.Copy),
                            plane_hi, 32 + 4 * r + b + 1)

                for r in range(QB):
                    root(r)
                    scale_rows(r)
                    if blk == 0 and r == 2:
                        cut_turned(0)
                    if blk and r:
                        store_rows(r - 1)
                if blk == 0:
                    turn_round(tile_at(first, 14))
                    for r in range(1, QB):
                        cut_turned(r)
                    turn_round(tile_at(first, 15))
                    for r in range(QB - 1):
                        store_rows(r)
                store_rows(QB - 1)

            back_and_norm(0, T_BACK1, x_rows, ln1, h_rows, {1: lambda: turn_round(tile_at(T_POOL, 7))})

            SK = BACK_TILES
            act.wait_ge(planes_ready, 48)
            act.dma_start(rope_q[:, :, :], rope_qk).then_inc(rope_q_loaded, 16)
            turn_round(tile_at(T_MISC, 0))
            take(tile_at(T_MISC, 0), gT[:, :], T_MISC - SK + 1)
            R = [probs[0:SSD_HEADS, k, :] for k in range(4)]
            act.wait_ge(prep_turn, 1)
            step(nc.scalar.activation(ea[:, :], par[0:SSD_HEADS, PC["a_log"]:PC["a_log"] + 1], ACT.Exp))
            step(nc.scalar.activation(R[1], R[1], ACT.Exp))
            signal(nc.scalar.activation(R[1], R[1], ACT.Ln, bias=1.0), prep_turn, 2)
            act.wait_ge(prep_turn, 3)
            step(nc.scalar.activation(R[1], R[1], ACT.Exp))
            signal(nc.scalar.activation(R[2], cumT[:, :], ACT.Exp), prep_turn, 4)

            def ssd_tile(it, k):
                n = 6 * it + k
                t = tile_at(T_SSD, n)
                turn_round(t)
                if k == 0 and it >= 2:
                    ssd_root(it - 2)
                if it == GROUPS:
                    if k == 0:
                        act.wait_ge(feat_done, 16 + 2 * (it - 1))
                    take(t, QI[k], T_SSD - SK + n + 1)
                    return
                if k < 4:
                    if 4 * it + k:
                        act.wait_ge(conv_done, 4 * it + k)
                    take(t, padded[:, 16:16 + S], T_SSD - SK + n + 1)
                    act.wait_ge(conv_done, 4 * it + k + 1)
                    src = XBC[it % 2][:, k, :]
                else:
                    if it >= 2:
                        act.wait_ge(feat_done, 16 + 2 * (it - 1))
                    src = Z[it % 2][k - 4]
                    if it == 1:
                        act.wait_ge(rows_stored, STORES * QB)
                    take(t, src, T_SSD - SK + n + 1)
                if n:
                    act.wait_ge(silu_done, n)
                signal(nc.scalar.activation(gate[:, :], src, ACT.Exp, scale=-1.0), silu_exp, n + 1)

            def ssd_exps(g, r):
                act.wait_ge(ssd_vec, VEC_STEPS * g + (7, 9, 12, 14)[r])
                n = EXP_STEPS * g + 2 * r + 1
                signal(nc.scalar.activation(LB[r % 2], LB[r % 2], ACT.Exp), ssd_exp, n)
                signal(nc.scalar.activation(EB[r % 2], [M, O][r % 2][:, :], ACT.Exp), ssd_exp, n + 1)

            def ssd_root(g):
                act.wait_ge(ssd_mm, MM_STEPS * g + 14)
                n = EXP_STEPS * g + 9
                signal(nc.scalar.activation(gT[:, :], M[:, :], ACT.Ln, bias=EPS, scale=1.0 / 256), ssd_exp, n)
                signal(nc.scalar.activation(gT[:, :], gT[:, :], ACT.Exp, scale=-0.5), ssd_exp, n + 1)

            def relu_scores(t):
                for i in range(1, QB):
                    for half in range(2):
                        n = 6 * t + 2 * i - 1 + half
                        act.wait_ge(idx_scored, n)
                        if t:
                            act.wait_ge(idx_summed, n - 6)
                        w = P * (i + 1)
                        signal(nc.scalar.activation(RELU[half][i - 1][:, 0:w], SCORES[half][i - 1][:, 0:w], ACT.Relu),
                               relu_done, n)

            for it in range(GROUPS + 1):
                for k in range(6):
                    ssd_tile(it, k)
                    if it == 1 and k == 0:
                        act.wait_ge(rows_stored, STORES * QB)
                        act.dma_start(rope_i, rope_idx).then_inc(rope_i_loaded, 16)
                    if it and 1 <= k <= 4:
                        ssd_exps(it - 1, k - 1)
            t = tile_at(T_IDX, 6)
            turn_round(t)
            ssd_root(GROUPS - 1)
            act.wait_ge(feat_done, 16 + 2 * GROUPS)
            take(t, QI[6], T_IDX - SK + 7)
            t = tile_at(T_IDX, 7)
            turn_round(t)
            take(t, QI[7], T_IDX - SK + 8)
            for t in range(8):
                relu_scores(t)
            for k, dst in enumerate((kT[:, 0, :], kT[:, 1, :], feats[:, 2, :], feats[:, 3, :])):
                t = tile_at(T_KV, k)
                turn_round(t)
                take(t, dst, T_KV - SK + k + 1)
            t = tile_at(T_HEAD2, 0)
            turn_round(t)
            act.wait_ge(idx_summed, 48)
            take(t, tmp[:, :], T_HEAD2 - SK + 1)
            for g, src in ((0, O), (1, M)):
                act.wait_ge(v_turned, HEADS + 1 + g)
                signal(nc.scalar.activation(vN[:, g, :, :].rearrange("p j n -> p (j n)"), src[:, :], ACT.Copy),
                       v_ready, HEADS + 1 + g)
            t = tile_at(T_HEAD2, 1)
            turn_round(t)
            take(t, gT[:, :], T_HEAD2 - SK + 2)
            exp_gate(17)
            with step.loop(1, HEADS, 0) as h:
                head_exps(HEADS + h - 1)
                t = tile_at(T_HEAD2, 0, h, 2)
                turn_round(t)
                act.wait_ge(q_roped, h)
                take(t, tmp[:, :], T_HEAD2 - SK + 2 * h + 1)
                t = tile_at(T_HEAD2, 1, h, 2)
                turn_round(t)
                act.wait_ge(feat_done, 16 + 2 * GROUPS + h)
                take(t, gT[:, :], T_HEAD2 - SK + 2 * h + 2)
                exp_gate(17 + h)
            back_and_norm(1, T_BACK2, h_rows, ln2, out, {3: lambda: head_exps(2 * HEADS - 1)})

        @block.vector
        def _(dve):
            V = nc.vector
            step = Steps(dve, dve_steps)

            def signal(ins, s, value):
                ins.then_inc(s, 1)
                dve.wait_ge(s, value)

            def stt(o, a, scalar, b, op0, op1):
                return V.scalar_tensor_tensor(out=o, in0=a, scalar=scalar, in1=b, op0=op0, op1=op1)

            def waited():
                dve.sem_inc(waits_passed, 1)

            def col(name, i=0):
                return par[:, at(PC[name] + i)]

            def sigmoid(g):
                step(V.tensor_scalar(g, g, 1.0, None, ADD))
                step(V.reciprocal(g, g))

            def cut_lo(k, value):
                dve.wait_ge(plane_hi, value)
                signal(V.tensor_sub(planes_lo[:, k, :], feats[:, k, :], planes_hi[:, k, :].bitcast(fp32)),
                       planes_ready, value)

            def cut_back(blk, start, end):
                for n in range(start, end):
                    cut_lo(BACK_ORDER[blk][n], 16 + 32 * blk + n + 1)

            def pick_cum_row(a):
                signal(V.tensor_scalar(cum_row[0:HEADS, :], cumT[0:HEADS, :], ident[0:HEADS, at(a)], None, MULT),
                       cum_row_ready, a + 1)

            def logit_bias(a):
                dve.wait_ge(cum_spread, a + 1)
                for i in range(QB):
                    n = P * (i + 1)
                    step(stt(bias[:, i, 0:n], M[:, 0:n], cumN[:, i, at(a)], causal[:, S - n:S], SUB, ADD))

            def head_softmax(a):
                for i in range(QB):
                    n = P * (i + 1)
                    dve.wait_ge(scores_done, 4 * a + i + 1)
                    step(stt(probs[:, i, 0:n], B[i][:, 0:n], -SCALE, bias[:, i, 0:n], MULT, ADD))
                    signal(V.tensor_reduce(nmax[:, i:i + 1], probs[:, i, 0:n], AX, MIN), logits_ready, 4 * a + i + 1)

            def head_gate(count):
                dve.wait_ge(gate_exp, count)
                sigmoid(gate[:, :])
                step(V.tensor_mul(gate[:, :], gate[:, :], gT[:, :]))

            def head_scale(a):
                for i in range(QB):
                    n = P * (i + 1)
                    dve.wait_ge(probs_ready, 4 * a + i + 1)
                    step(V.reciprocal(rinv[:, i:i + 1], rowsum[:, i:i + 1]))
                    signal(V.tensor_scalar(probs[:, i, 0:n], probs[:, i, 0:n], rinv[:, i:i + 1], None, MULT),
                           probs_scaled, 4 * a + i + 1)

            def head_take_turned(a):
                dve.wait_ge(probs_turned, a + 1)
                for j in range(QB):
                    ins = V.tensor_copy(probsT[:, j, P * j:S], B[j][:, P * j:S])
                    if j < QB - 1:
                        step(ins)
                    else:
                        signal(ins, probsT_ready, a + 1)

            def head_finish(a, tile, count, src=O):
                dve.wait_ge(pv_done, a + 1)
                signal(V.tensor_mul(feats[:, at(tile), :].rearrange("p a n -> p (a n)"), src[:, :], gate[:, :]),
                       feat_done, count)

            def take_v(g, count):
                dve.wait_ge(v_turned, count)
                signal(V.tensor_copy(vN[:, g, :, :].rearrange("p j n -> p (j n)"), M[:, :]), v_ready, count)

            for k in range(KT):
                cut_lo(k, k + 1)
            xs, ls = tmp[0:HEADS, :], gate[0:HEADS, :]
            dve.wait_ge(acc_taken, 1)
            signal(stt(ls, xs, -1.0, xs, MULT, MIN), fg_turn, 1)
            dve.wait_ge(consts, 1)
            step(V.memset(probs[0:HEADS, 0, :], 1.0))
            dve.wait_ge(fg_turn, 2)
            step(stt(xs, xs, 0.0, ls, MIN, SUB))
            signal(V.tensor_tensor_scan(cumT[0:HEADS, :], probs[0:HEADS, 0, :], xs, 0.0, MULT, ADD), cum_ready, 1)
            dve.wait_ge(cum_turned, 1)
            step(V.tensor_copy(cumN[:, :, 0:HEADS], M[:, 0:32].rearrange("p (i h) -> p i h", i=QB)))
            pick_cum_row(0)
            take_v(0, 1)
            with step.loop(1, HEADS, 18) as h:
                a = h - 1
                logit_bias(a)
                head_softmax(a)
                head_gate(a + 1)
                head_scale(a)
                head_take_turned(a)
                head_finish(a, a, a + 1)
                pick_cum_row(h)
                take_v(0, h + 1)
            a = HEADS - 1
            logit_bias(a)
            head_softmax(a)
            head_gate(a + 1)
            head_scale(a)
            head_take_turned(a)
            head_finish(a, a, a + 1)

            def conv_mixer(j):
                dve.wait_ge(acc_taken, T_CONV + 4 * j + 4)
                step(V.tensor_mul(padded[:, 16:16 + S], kT[:, 0, :], vT[:, :]))
                step(V.tensor_scalar(tmp[:, :], padded[:, 14:14 + S], col("conv_w", 3 * j), None, MULT))
                for c in (1, 2):
                    step(stt(tmp[:, :], padded[:, 14 + c:14 + c + S], col("conv_w", 3 * j + c), tmp[:, :], MULT, ADD))
                step(V.tensor_mul(tmp[:, :], tmp[:, :], qT[:, :]))
                head_gate(HEADS + j + 1)
                signal(V.tensor_mul(feats[:, at(HEADS + j), :].rearrange("p a n -> p (a n)"), tmp[:, :], gate[:, :]),
                       feat_done, HEADS + j + 1)

            with step.loop(0, 4, 8) as j:
                conv_mixer(j)

            flat = probs[:, :, :].rearrange("p a b -> p (a b)")
            bufs = [flat[:, 0:16 + S], flat[:, 16 + S:2 * (16 + S)]]
            for b in bufs:
                step(V.memset(b[:, 0:16], 0.0))
            for n, g in enumerate((3, 2, 1, 0)):
                w = 2 << g
                head_gate(HEADS + 4 + n + 1)
                if g == 0:
                    cut_back(0, 0, 2)
                dve.wait_ge(acc_taken, T_POOL + 2 * n + 2)
                src = padded
                for lev in range(g + 1):
                    dst = bufs[lev % 2]
                    sh = 1 << lev
                    step(V.tensor_add(dst[:, 16:16 + S], src[:, 16:16 + S], src[:, 16 - sh:16 - sh + S]))
                    src = dst
                step(stt(tmp[:, :], src[:, 16:16 + S], 1.0 / w, padded[:, 16:16 + S], MULT, SUB))
                step(V.tensor_mul(tmp[:, 0:w - 1], src[:, 16:16 + w - 1], par[:, PC["inv_count"]:PC["inv_count"] + w - 1]))
                signal(V.tensor_sub(tmp[:, 0:w - 1], tmp[:, 0:w - 1], padded[:, 16:16 + w - 1]), pool_in, n + 1)
                if g == 0:
                    cut_back(0, 2, 4)
                dve.wait_ge(pool_done, n + 1)
                signal(stt(feats[:, 12 + g, :], O[:, :], col("pool_scale", g), gate[:, :], MULT, MULT),
                       feat_done, 12 + n + 1)
            cut_back(0, 4, KT)

            def back_and_norm(blk, first):
                def take_rows(db, r):
                    signal(stt(feats[:, 4 * r + db, :], resid[db % 2][:, r, :], ALPHA, BACK_SETS[blk][db % 2][r][:, :],
                               MULT, ADD), rows_taken, 16 * blk + 4 * db + r + 1)
                    step(V.bn_stats(stats[:, r, db, :], feats[:, 4 * r + db, :]))

                def scales(r):
                    n = 4 * blk + r + 1
                    dve.wait_ge(root_ready, n)
                    step(V.reciprocal(rstd[:, r, 0:1], rstd[:, r, 0:1]))
                    signal(V.tensor_scalar(rstd[:, r, 1:2], mv[:, r, 0:1], rstd[:, r, 0:1], -1.0, MULT, MULT),
                           rstd_ready, n)

                def norm_rows(r):
                    c = NORM_CUTS[r][1]
                    rest = feats[:, 4 * r:4 * r + 4, :].rearrange("p a b -> p (a b)")[:, c:D]
                    step(stt(rest, rest, mv[:, r, 0:1], gamma[:, c:D], SUB, MULT))
                    for i in (1, 2):
                        part = norm_part(r, i)
                        signal(stt(part, part, rstd[:, r, 0:1], beta[:, NORM_CUTS[r][i]:NORM_CUTS[r][i + 1]], MULT, ADD),
                               rest_normed, 2 * (4 * blk + r) + i)

                def cut_turned(r):
                    for b in range(4):
                        n = 32 + 4 * r + b + 1
                        dve.wait_ge(plane_hi, n)
                        signal(V.tensor_sub(planes_lo[:, 4 * b:4 * b + 4, P * r:P * r + P],
                                            SETS[r % 2][b][:, :].rearrange("p (k n) -> p k n", k=4),
                                            planes_hi[:, 4 * b:4 * b + 4, P * r:P * r + P].bitcast(fp32)),
                               planes_ready, n)

                for db in range(3):
                    dve.wait_ge(resid_loaded[db % 2], 16 * (2 * blk + db // 2 + 1))
                    dve.wait_ge(unit_used, 2 * (first + 4 * db + 4))
                    for r in range(QB):
                        take_rows(db, r)
                dve.wait_ge(resid_loaded[1], 16 * (2 * blk + 2))
                dve.wait_ge(ln_loaded, 32 * (blk + 1))
                for r in range(QB):
                    if r < QB - 1:
                        dve.wait_ge(rows_summed, (QB - 1) * blk + r + 1)
                    else:
                        dve.wait_ge(unit_used, 2 * (first + 16))
                    take_rows(3, r)
                    signal(V.bn_aggr(mv[:, r, :], stats[:, r, :, :]), var_ready, 4 * blk + r + 1)
                    scales(r)
                    if blk == 0 and r == QB - 1:
                        cut_turned(0)
                    norm_rows(r)
                if blk == 0:
                    for r in range(1, QB):
                        cut_turned(r)

            back_and_norm(0, T_BACK1)

            SK = BACK_TILES

            def rope(dst, src, lanes, table, mask, ins_signal, value, scratch):
                waited()
                step(V.stream_shuffle(scratch[0:lanes, :], src[0:lanes, :], mask))
                step(V.tensor_mul(scratch[0:lanes, :], scratch[0:lanes, :], table[0:lanes, 1, :]))
                step(V.tensor_mul(dst[0:lanes, :], src[0:lanes, :], table[0:lanes, 0, :]))
                ins = V.tensor_add(dst[0:lanes, :], dst[0:lanes, :], scratch[0:lanes, :])
                if ins_signal is None:
                    step(ins)
                else:
                    signal(ins, ins_signal, value)

            swap8 = [i + 8 if i < 8 else i - 8 if i < 16 else i for i in range(32)]
            swap16 = [(i + 16) % 32 for i in range(32)]
            R = [probs[0:SSD_HEADS, k, :] for k in range(4)]
            dve.wait_ge(acc_taken, T_MISC - SK + 1)
            step(V.tensor_copy(R[0], gT[64:80, :]))
            step(V.tensor_scalar(R[0], R[0], par[0:SSD_HEADS, PC["dt_bias"]:PC["dt_bias"] + 1], None, ADD))
            signal(stt(R[1], R[0], -1.0, R[0], MULT, MIN), prep_turn, 1)
            step(V.tensor_copy(R[3], gT[96:112, :]))
            step(V.tensor_scalar(R[3], R[3], W_IDX_SCALE, None, MULT))
            step(V.tensor_copy(k_idx[0:64, :], gT[0:64, :]))
            step(V.memset(R[2], 1.0))
            dve.wait_ge(prep_turn, 2)
            step(stt(R[0], R[0], 0.0, R[1], MAX, ADD))
            step(V.tensor_scalar(R[1], R[0], ea[:, 0:1], -1.0, MULT, MULT))
            for c in range(QB):
                chunk = slice(P * c, P * c + P)
                step(V.tensor_tensor_scan(cumT[:, chunk], R[2][:, chunk], R[1][:, chunk], 0.0, MULT, ADD))
            for c in range(QB):
                chunk, end = slice(P * c, P * c + P), P * c + P - 1
                ins = V.tensor_scalar(R[1][:, chunk], cumT[:, chunk], -1.0, cumT[:, end:end + 1], MULT, ADD)
                if c < QB - 1:
                    step(ins)
                else:
                    signal(ins, prep_turn, 3)
            dve.wait_ge(prep_turn, 4)
            signal(V.tensor_mul(R[1], R[1], R[0]), prep_turn, 5)
            dve.wait_ge(prep_turned, 1)
            for k, dst in enumerate((cumN, dtN, wN, ecumN, widxN)):
                ins = V.tensor_copy(dst[:, :, :], M[:, 64 * k:64 * k + 64].rearrange("p (c h) -> p c h", c=QB))
                if k < 4:
                    step(ins)
                else:
                    signal(ins, prep_ready, 1)
            dve.wait_ge(decay_spread, 1)
            step(V.tensor_copy(chunk_decay[:, :, :], O[:, 0:64].rearrange("p (c h) -> p c h", c=QB)))

            def silu_tile(n):
                it, k = divmod(n, 6)
                dve.wait_ge(acc_taken, T_SSD - SK + n + 1)
                if it == GROUPS:
                    rope(QI[k], QI[k], P, rope_i, swap8, idx_roped, k + 1, padded[:, 16:16 + S])
                    return
                if k < 4:
                    dst = XBC[it % 2][:, k, :]
                    ch = 4 * it + k
                    step(V.tensor_scalar(dst, padded[:, 16:16 + S], col("conv_w2", 4 * ch + 3), col("conv_b2", ch), MULT, ADD))
                    for c in (2, 1, 0):
                        ins = stt(dst, padded[:, 13 + c:13 + c + S], col("conv_w2", 4 * ch + c), dst, MULT, ADD)
                        if c:
                            step(ins)
                        else:
                            signal(ins, conv_done, 4 * it + k + 1)
                else:
                    dst = Z[it % 2][k - 4]
                dve.wait_ge(silu_exp, n + 1)
                sigmoid(gate[:, :])
                signal(V.tensor_mul(dst, dst, gate[:, :]), silu_done, n + 1)

            def ssd_rows(g):
                mm0, vv0 = MM_STEPS * g, VEC_STEPS * g
                dve.wait_ge(ssd_mm, mm0 + 2)
                signal(V.tensor_copy(vT[:, :], B[3][:, :]), ssd_vec, vv0 + 1)
                for t, src in ((0, O), (1, M)):
                    dve.wait_ge(ssd_mm, mm0 + 3 + t)
                    for col_of, dst in ((dtN, xdt), (wN, states)):
                        for h in range(2):
                            d = dst[:, :, P * t + 64 * h:P * t + 64 * h + 64]
                            x = src[:, :].rearrange("p (c f) -> p c f", c=QB)[:, :, 64 * h:64 * h + 64]
                            ins = V.tensor_mul(d, x, col_of[:, :, at(4 * g + 2 * t + h)].to_broadcast([P, QB, 64]))
                            if col_of is wN and h:
                                signal(ins, ssd_vec, vv0 + 2 + t)
                            else:
                                step(ins)

            def pick_row(g, r, value):
                signal(V.tensor_scalar(gT[0:SSD_HEADS, :], cumT[:, :], ident[0:SSD_HEADS, at(4 * g + r)], None, MULT),
                       ssd_vec, VEC_STEPS * g + value)

            def segments(g, r, value):
                for c in range(QB):
                    chunk = slice(P * c, P * c + P)
                    ins = stt(LB[r % 2][:, chunk], [M, O][r % 2][:, chunk], cumN[:, c, at(4 * g + r)], upper[:, :], SUB, ADD)
                    if c < QB - 1:
                        step(ins)
                    else:
                        signal(ins, ssd_vec, VEC_STEPS * g + value)

            def operands(g, r, value):
                dve.wait_ge(ssd_exp, EXP_STEPS * g + 2 * r + 2)
                L, E = LB[r % 2], EB[r % 2]
                step(V.tensor_mul(L, L, B[0][:, :]))
                signal(V.tensor_mul(E, E, XBC[g % 2][:, 1, :]), ssd_vec, VEC_STEPS * g + value)

            def ssd_carry(g):
                dve.wait_ge(ssd_mm, MM_STEPS * g + 5)
                step(V.tensor_copy(states[:, 1, :], B[3][:, 0:256]))
                for c in (1, 2):
                    new, old = states[:, c + 1, :], states[:, c, :]
                    dec = chunk_decay[:, c, at(4 * g, 4)].unsqueeze(2).to_broadcast([P, 4, 64])
                    step(V.tensor_mul(new.rearrange("p (h f) -> p h f", h=4), old.rearrange("p (h f) -> p h f", h=4), dec))
                    ins = V.tensor_add(new, new, (B[3][:, 256:512] if c == 1 else O[:, 0:256]))
                    if c == 1:
                        step(ins)
                    else:
                        signal(ins, ssd_vec, VEC_STEPS * g + 5)

            def ssd_gated(g):
                dve.wait_ge(ssd_mm, MM_STEPS * g + 13)
                for t in range(2):
                    sq, z = LB[t], Z[g % 2][t]
                    step(stt(sq, XBC[g % 2][:, 2 + t, :], col("d_skip", 2 * g + t), B[1 + t][:, :], MULT, ADD))
                    step(V.tensor_mul(z, z, sq))
                    ins = V.tensor_mul(sq, z, z)
                    if t:
                        signal(ins, ssd_vec, VEC_STEPS * g + 17)
                    else:
                        step(ins)

            def ssd_normed(g):
                dve.wait_ge(ssd_exp, EXP_STEPS * g + 10)
                for t in range(2):
                    signal(stt(feats[:, HEADS + 2 * g + t, :], Z[g % 2][t], col("norm_w", 2 * g + t), gT[:, :],
                               MULT, MULT), feat_done, 17 + 2 * g + t)

            for it in range(GROUPS + 1):
                g = it - 1
                if it >= 2:
                    ssd_gated(it - 2)
                if it >= 1:
                    silu_tile(6 * it - 1)
                if it >= 2:
                    ssd_normed(it - 2)
                if it >= 1:
                    ssd_rows(g)
                    pick_row(g, 0, 4)
                if it == 1:
                    dve.wait_ge(rows_stored, STORES * QB)
                silu_tile(6 * it)
                if it >= 1:
                    ssd_carry(g)
                    dve.wait_ge(ssd_mm, MM_STEPS * g + 6)
                    pick_row(g, 1, 6)
                    segments(g, 0, 7)
                silu_tile(6 * it + 1)
                if it >= 1:
                    dve.wait_ge(ssd_mm, MM_STEPS * g + 7)
                    pick_row(g, 2, 8)
                    segments(g, 1, 9)
                    operands(g, 0, 10)
                if it == 1:
                    dve.wait_ge(rope_i_loaded, 16)
                    rope(k_idx, k_idx, 64, rope_i, swap8, None, 0, bias[:, 0, :])
                    step(V.tensor_copy(k_idx[64:128, :], k_idx[0:64, :]))
                silu_tile(6 * it + 2)
                if it >= 1:
                    dve.wait_ge(ssd_mm, MM_STEPS * g + 9)
                    pick_row(g, 3, 11)
                    segments(g, 2, 12)
                    operands(g, 1, 13)
                silu_tile(6 * it + 3)
                if it >= 1:
                    dve.wait_ge(ssd_mm, MM_STEPS * g + 11)
                    segments(g, 3, 14)
                    operands(g, 2, 15)
                    operands(g, 3, 16)
                silu_tile(6 * it + 4)
            ssd_gated(GROUPS - 1)
            silu_tile(6 * GROUPS + 5)
            ssd_normed(GROUPS - 1)

            def sum_scores(t):
                for i in range(1, QB):
                    for half in range(2):
                        n = 6 * t + 2 * i - 1 + half
                        w = P * (i + 1)
                        dve.wait_ge(relu_done, n)
                        relu, wi = RELU[half][i - 1][:, 0:w], widxN[:, i, 2 * t + half:2 * t + half + 1]
                        if t == 0 and half == 0:
                            ins = V.tensor_scalar(bias[:, i, 0:w], relu, wi, None, MULT)
                        else:
                            ins = stt(bias[:, i, 0:w], relu, wi, bias[:, i, 0:w], MULT, ADD)
                        signal(ins, idx_summed, n)

            def rope_q_idx(t):
                dve.wait_ge(acc_taken, T_IDX - SK + t + 1)
                rope(QI[t], QI[t], P, rope_i, swap8, idx_roped, t + 1, padded[:, 16:16 + S])

            rope_q_idx(6)
            rope_q_idx(7)
            for t in range(8):
                sum_scores(t)

            for i in range(1, QB):
                step(V.memset(bias[0:64, i, P * i + 64:P * i + P], INADMISSIBLE))
            for r in range(TOPK // 8):
                for i in range(1, QB):
                    n = P * (i + 1)
                    if r:
                        dve.wait_ge(keys_taken, 3 * (r - 1) + i)
                    V.max(top8[:, i, :], bias[:, i, 0:n]).then_inc(keys_found, 1)
                for i in range(1, QB):
                    n = P * (i + 1)
                    dve.wait_ge(keys_found, 3 * r + i)
                    V.match_replace(bias[:, i, 0:n], top8[:, i, :], bias[:, i, 0:n], TAKEN).then_inc(keys_taken, 1)
            dve.wait_ge(keys_taken, 3 * (TOPK // 8))
            for i in range(1, QB):
                n = P * (i + 1)
                step(V.tensor_scalar(bias[:, i, 0:n], bias[:, i, 0:n], TAKEN, BIG, ALU.not_equal, MULT))
            step(V.memset(bias[:, 0, 0:P], 0.0))
            step(V.memset(bias[0:64, 0, 64:P], BIG))
            dve.wait_ge(rope_q_loaded, 16)
            dve.wait_ge(acc_taken, T_KV - SK + 2)
            rope(kT[:, 0, :], kT[:, 0, :], P, rope_q, swap16, None, 0, padded[:, 16:16 + S])
            rope(kT[:, 1, :], kT[:, 1, :], P, rope_q, swap16, k_roped, 1, padded[:, 16:16 + S])
            def rope_head(h):
                dve.wait_ge(acc_taken, T_HEAD2 - SK + 2 * h + 1)
                rope(qT, tmp, P, rope_q, swap16, q_roped, h + 1, padded[:, 16:16 + S])

            rope_head(0)
            with step.loop(1, HEADS, 17) as h:
                a = HEADS + h - 1
                head_softmax(a)
                head_gate(16 + h)
                head_scale(a)
                head_take_turned(a)
                rope_head(h)
                head_finish(a, h - 1, 24 + h)
            a = 2 * HEADS - 1
            cut_back(1, 0, 2)
            head_softmax(a)
            cut_back(1, 2, 4)
            head_gate(24)
            cut_back(1, 4, 5)
            head_scale(a)
            cut_back(1, 5, 7)
            head_take_turned(a)
            cut_back(1, 7, 9)
            head_finish(a, HEADS - 1, 32, B[0])
            cut_back(1, 9, KT)
            back_and_norm(1, T_BACK2)


def rope_table(rows, cols):
    rot = cols // 4
    half = rot // 2
    f32 = np.float32
    inv = np.power(f32(500000.0), -np.arange(half, dtype=f32) * f32(2.0) / f32(rot), dtype=f32)
    ang = np.arange(S, dtype=f32)[:, None] * inv[None, :]
    cos, sin = np.cos(ang).T, np.sin(ang).T
    table = np.zeros((rows, cols, 2, S), f32)
    table[:, :, 0] = 1.0
    table[:, 0:half, 0] = cos
    table[:, half:rot, 0] = cos
    table[:, 0:half, 1] = -sin
    table[:, half:rot, 1] = sin
    return table.reshape(P, 2, S)


def tile_units(w, cols):
    t = np.zeros((D, P), np.float32)
    used = np.asarray(cols) >= 0
    t[:, :len(cols)][:, used] = w[:, np.asarray(cols)[used]]
    return t.reshape(2, UK, P, P).transpose(0, 2, 1, 3).reshape(2, P, UNIT)


def back_units(w, order):
    w = w.reshape(KT, P, 4, S)[np.asarray(order)]
    return w.reshape(KT // 2, 2, P, 4, S).transpose(3, 0, 2, 1, 4).reshape(32, P, UNIT)


def kernel(**inputs):
    import concourse.bacc as _bacc
    from concourse import mybir as _mybir
    from concourse.bass_utils import run_bass_kernel_spmd as _run

    a = {k: np.ascontiguousarray(v) for k, v in inputs.items()}
    w1, w2 = a["w_in"][0], a["w_in_2"][0]
    span = lambda start, n=P: list(range(start, start + n))
    tiles = [tile_units(w1, span(4096, 8))]
    for h in range(HEADS):
        tiles += [tile_units(w1, span(1024 * k + P * h)) for k in range(4)]
    for j in range(4):
        tiles += [tile_units(w1, span(4104 + 512 * k + P * j)) for k in range(4)]
    for g in (3, 2, 1, 0):
        tiles += [tile_units(w1, span(6152 + 512 * k + P * g)) for k in (1, 0)]
    tiles.append(back_units(a["w_out"][0], BACK_ORDER[0]))
    q, k, v, z, qi, ki, wi, zs, xs, bm, cm, dt = 0, 1024, 1280, 1536, 2560, 3584, 3648, 3664, 4688, 5712, 6224, 6736
    tiles.append(tile_units(w2, span(ki, 64) + span(dt, 16) + [-1] * 16 + span(wi, 16)))
    xbc_tiles = []
    for g in range(GROUPS):
        conv_cols = [bm + P * g, cm + P * g, xs + 256 * g, xs + 256 * g + P]
        xbc_tiles += [c - xs for c in conv_cols]
        tiles += [tile_units(w2, span(c)) for c in conv_cols + [zs + 256 * g, zs + 256 * g + P]]
    tiles += [tile_units(w2, span(qi + P * t)) for t in range(8)]
    tiles += [tile_units(w2, span(c)) for c in (k, k + P, v, v + P)]
    for h in range(HEADS):
        tiles += [tile_units(w2, span(q + P * h)), tile_units(w2, span(z + P * h))]
    tiles.append(back_units(a["w_out_2"][0], BACK_ORDER[1]))

    par = np.zeros((P, NPAR), np.float32)

    def put(name, x):
        par[:x.shape[0], PC[name]:PC[name] + x.shape[1]] = x

    put("b_f", a["b_f"][0][:, None])
    put("conv_w", a["conv_w"][0].reshape(3, 4, P).transpose(2, 1, 0).reshape(P, 12))
    put("pool_scale", a["pool_scale"][0].reshape(4, P).T)
    put("conv_w2", np.stack([a["conv_w_2"][0][:, c:c + P] for c in xbc_tiles]).transpose(2, 0, 1).reshape(P, 64))
    put("conv_b2", np.stack([a["conv_b_2"][0][c:c + P] for c in xbc_tiles]).T)
    put("dt_bias", a["dt_bias_2"][0][:, None])
    put("a_log", a["a_log_2"][0][:, None])
    put("d_skip", np.repeat(a["d_skip_2"][0], 64).reshape(8, P).T)
    put("norm_w", a["ssd_norm_w_2"][0].reshape(8, P).T)
    put("inv_count", np.broadcast_to(np.float32(1) / np.arange(1, 17, dtype=np.float32), (P, 16)))

    x = a["x"][0]
    arrays = {
        "x_t": np.ascontiguousarray(x.T.reshape(KT, P, S).transpose(1, 0, 2)),
        "x_rows": x,
        "stream": np.concatenate(tiles),
        "params": par,
        "pool_w": np.ascontiguousarray(a["pool_w"][0].transpose(1, 0, 2)),
        "ln1": np.concatenate([a["ln_g"], a["ln_b"]]),
        "ln2": np.concatenate([a["ln_g_2"], a["ln_b_2"]]),
        "rope_idx": rope_table(2, 64),
        "rope_qk": rope_table(1, P),
    }
    nc = _bacc.Bacc("TRN2", target_bir_lowering=False, num_devices=1)
    args = [nc.dram_tensor(f"in_{n}", v.shape, _mybir.dt.from_np(v.dtype), kind="ExternalInput").ap()
            for n, v in arrays.items()]
    out = nc.dram_tensor("out", (S, D), _mybir.dt.float32, kind="ExternalOutput").ap()
    block_kernel(nc, *args, out)
    r = _run(nc, [{f"in_{n}": v for n, v in arrays.items()}], core_ids=[0])
    return r.results[0]["out"].reshape(1, S, D)
```
